# Optimizing a Trainium2 kernel written in Bass

```python
import math
import jax, jax.numpy as jnp
from jax import lax
import numpy as np

D_MODEL = 1024
BATCH = 1
SEQ = 256
DEPTH = 2

HEAD_DIM = 64
ROPE_THETA = 500000.0
ROPE_DIM = HEAD_DIM // 4
NORM_EPS = 1e-6
Q_BLOCK = 128
NEG = -1e30
D_FF = 4 * D_MODEL

A_HEADS = 4
A_NOPE = HEAD_DIM - ROPE_DIM
A_VDIM = HEAD_DIM
A_KV_RANK = 128
IDX_HEADS = 4
IDX_DIM = 32
IDX_ROPE = IDX_DIM // 4
DSA_TOPK = 256

B_WIDTH = 256
S5_GROUP = 16
S5_GROUPS = B_WIDTH // S5_GROUP
S5_STATE = 64
S5_DT_MIN = 1e-3
S5_DT_MAX = 1e-1

C_HEADS = 8
C_KV_HEADS = 2
C_GROUP = C_HEADS // C_KV_HEADS
CMP_BLOCK = 32
CMP_STRIDE = 16
SEL_BLOCK = 64
SEL_TOPN = 16
SEL_FORCE = 1e9
WINDOW = 512

D_MIX = A_HEADS * A_VDIM + B_WIDTH + C_HEADS * HEAD_DIM
IN_SIZES = (
    A_HEADS * HEAD_DIM,
    A_KV_RANK,
    ROPE_DIM,
    IDX_HEADS * IDX_DIM,
    IDX_DIM,
    IDX_HEADS,
    B_WIDTH,
    C_HEADS * HEAD_DIM,
    6 * C_KV_HEADS * HEAD_DIM,
    3 * C_HEADS,
)
N_IN = sum(IN_SIZES)

kernel_name = "hybrid_dsa_s5_nsa_parallel_heads"

def rms_norm(x, g):
    xf = x.astype(jnp.float32)
    y = xf * lax.rsqrt(jnp.mean(xf * xf, axis=-1, keepdims=True) + NORM_EPS)
    return (y * g.astype(jnp.float32)).astype(x.dtype)

def rope_tables(positions, rot_dim):
    inv = ROPE_THETA ** (-jnp.arange(0, rot_dim, 2, dtype=jnp.float32) / rot_dim)
    ang = positions.astype(jnp.float32)[..., None] * inv
    return jnp.cos(ang), jnp.sin(ang)

def partial_rope(x, cos, sin):
    half = cos.shape[-1]
    shape = cos.shape[:2] + (1,) * (x.ndim - 3) + (half,)
    c = cos.reshape(shape).astype(x.dtype)
    s = sin.reshape(shape).astype(x.dtype)
    x1, x2, rest = x[..., :half], x[..., half:2 * half], x[..., 2 * half:]
    return jnp.concatenate([x1 * c - x2 * s, x2 * c + x1 * s, rest], axis=-1)

def masked_softmax(s, mask):
    s = jnp.where(mask, s.astype(jnp.float32), NEG)
    p = jax.nn.softmax(s, axis=-1)
    return jnp.where(mask, p, 0.0)

def to_blocks(a):
    b, l = a.shape[:2]
    return jnp.moveaxis(a.reshape((b, l // Q_BLOCK, Q_BLOCK) + a.shape[2:]), 1, 0)

def from_blocks(a):
    nb, b, q = a.shape[:3]
    return jnp.moveaxis(a, 0, 1).reshape((b, nb * q) + a.shape[3:])

def sel_overlap(n_cmp, n_blk):
    cs = np.arange(n_cmp)[:, None] * CMP_STRIDE
    ss = np.arange(n_blk)[None, :] * SEL_BLOCK
    ov = np.minimum(cs + CMP_BLOCK, ss + SEL_BLOCK) - np.maximum(cs, ss)
    return np.clip(ov, 0, None).astype(np.float32) / CMP_BLOCK

def dsa_mixer(q, ckv, k_rope, iq, ik, iw, cos, sin, cos_i, sin_i, kv_g, w_uk, w_uv):
    bsz, seq = q.shape[:2]
    k_top = min(DSA_TOPK, seq // 4)
    q = partial_rope(q.reshape(bsz, seq, A_HEADS, HEAD_DIM), cos, sin)
    q_rope, q_nope = q[..., :ROPE_DIM], q[..., ROPE_DIM:]
    q_lat = jnp.einsum('bthn,rhn->bthr', q_nope, w_uk)
    c = rms_norm(ckv, kv_g)
    k_rope = partial_rope(k_rope, cos, sin)
    iq = partial_rope(iq.reshape(bsz, seq, IDX_HEADS, IDX_DIM), cos_i, sin_i)
    ik = partial_rope(ik, cos_i, sin_i)
    iw = iw.astype(jnp.float32) * IDX_HEADS ** -0.5
    key_pos = jnp.arange(seq)
    take = jax.vmap(lambda a, i: a[i])

    def block(args):
        ql, qr, iqb, iwb, t = args
        rel = jax.nn.relu(jnp.einsum('bqhd,bsd->bqhs', iqb, ik).astype(jnp.float32) * IDX_DIM ** -0.5)
        score = jnp.einsum('bqhs,bqh->bqs', rel, iwb)
        score = jnp.where(key_pos[None, None, :] <= t[None, :, None], score, -jnp.inf)
        _, sel = lax.top_k(score, k_top)
        c_sel = take(c, sel)
        kr_sel = take(k_rope, sel)
        s = (jnp.einsum('bqhr,bqkr->bqhk', ql, c_sel)
             + jnp.einsum('bqhd,bqkd->bqhk', qr, kr_sel)) * HEAD_DIM ** -0.5
        p = masked_softmax(s, (sel <= t[None, :, None])[:, :, None, :])
        o_lat = jnp.einsum('bqhk,bqkr->bqhr', p.astype(c.dtype), c_sel)
        return jnp.einsum('bqhr,rhv->bqhv', o_lat, w_uv)

    t_blocks = key_pos.reshape(-1, Q_BLOCK)
    out = lax.map(block, (to_blocks(q_lat), to_blocks(q_rope), to_blocks(iq), to_blocks(iw), t_blocks))
    return from_blocks(out).reshape(bsz, seq, A_HEADS * A_VDIM)

def _complex_linear_combine(e1, e2):
    a1r, a1i, b1r, b1i = e1
    a2r, a2i, b2r, b2i = e2
    return (a2r * a1r - a2i * a1i, a2r * a1i + a2i * a1r,
            a2r * b1r - a2i * b1i + b2r, a2r * b1i + a2i * b1r + b2i)

def s5_mixer(u, lam_re, lam_im, log_step, b_re, b_im, c_re, c_im, d, glu_w, glu_b):
    f32 = jnp.float32
    bsz, seq, _ = u.shape
    ug = u.astype(f32).reshape(bsz, seq, S5_GROUPS, S5_GROUP)
    lr, li = lam_re.astype(f32), lam_im.astype(f32)
    step = jnp.exp(log_step.astype(f32))[:, None]
    mag = jnp.exp(lr * step)
    ar, ai = mag * jnp.cos(li * step), mag * jnp.sin(li * step)
    den = lr * lr + li * li
    zr = ((ar - 1.0) * lr + ai * li) / den
    zi = (ai * lr - (ar - 1.0) * li) / den
    br, bi = b_re.astype(f32), b_im.astype(f32)
    bbr = zr[..., None] * br - zi[..., None] * bi
    bbi = zr[..., None] * bi + zi[..., None] * br
    xr = jnp.einsum('blgh,gph->lbgp', ug, bbr)
    xi = jnp.einsum('blgh,gph->lbgp', ug, bbi)
    a_shape = (seq, 1) + ar.shape
    _, _, hr, hi = lax.associative_scan(
        _complex_linear_combine,
        (jnp.broadcast_to(ar, a_shape), jnp.broadcast_to(ai, a_shape), xr, xi), axis=0)
    y = (jnp.einsum('lbgp,ghp->blgh', hr, c_re.astype(f32))
         - jnp.einsum('lbgp,ghp->blgh', hi, c_im.astype(f32))
         + d.astype(f32) * ug)
    y = jax.nn.gelu(y.reshape(bsz, seq, B_WIDTH))
    y = y * jax.nn.sigmoid(y @ glu_w.astype(f32) + glu_b.astype(f32))
    return y.astype(u.dtype)

def nsa_mixer(q, kv, gate, cos, sin, pos_k, pos_v, k_w1, k_w2, v_w1, v_w2):
    bsz, seq = q.shape[:2]
    G, HG, DH = C_KV_HEADS, C_GROUP, HEAD_DIM
    q = q.reshape(bsz, seq, G, HG, DH)
    q_rot = partial_rope(q, cos, sin)
    kv = kv.reshape(bsz, seq, 6, G, DH)
    k_c, v_c, k_s, v_s, k_w, v_w = (kv[:, :, i] for i in range(6))
    k_s = partial_rope(k_s, cos, sin)
    k_w = partial_rope(k_w, cos, sin)
    gate = jax.nn.sigmoid(gate.astype(jnp.float32)).reshape(bsz, seq, G, HG, 3)

    n_cmp = (seq - CMP_BLOCK) // CMP_STRIDE + 1
    n_blk = seq // SEL_BLOCK
    n_top = min(SEL_TOPN, n_blk)
    cmp_tok = np.arange(n_cmp)[:, None] * CMP_STRIDE + np.arange(CMP_BLOCK)[None, :]
    cmp_end = jnp.asarray(cmp_tok[:, -1])
    overlap = jnp.asarray(sel_overlap(n_cmp, n_blk))

    def compress(a, pos, w1, w2):
        blk = a[:, cmp_tok] + pos[:, None, :]
        blk = jnp.moveaxis(blk, 3, 2).reshape(bsz, n_cmp, G, CMP_BLOCK * DH)
        return jax.nn.gelu(blk @ w1) @ w2

    k_cmp = compress(k_c, pos_k, k_w1, k_w2)
    v_cmp = compress(v_c, pos_v, v_w1, v_w2)
    pad = ((0, 0), (WINDOW, 0), (0, 0), (0, 0))
    k_wp, v_wp = jnp.pad(k_w, pad), jnp.pad(v_w, pad)
    blk_id = jnp.arange(n_blk)
    tok_in_blk = jnp.arange(SEL_BLOCK)
    slab = jnp.arange(WINDOW + Q_BLOCK)
    b_idx = jnp.arange(bsz)[:, None, None, None]
    g_idx = jnp.arange(G)[None, None, :, None]
    scale = DH ** -0.5

    def block(args):
        qb, qrb, gb, t = args
        s_c = jnp.einsum('bqghd,bngd->bqghn', qb, k_cmp) * scale
        p_c = masked_softmax(s_c, (cmp_end[None, :] <= t[:, None])[None, :, None, None, :])
        o_c = jnp.einsum('bqghn,bngd->bqghd', p_c.astype(v_cmp.dtype), v_cmp)
        imp = jnp.einsum('bqghn,nm->bqgm', p_c, overlap)
        cur = (t // SEL_BLOCK)[:, None]
        forced = (blk_id[None] == 0) | (blk_id[None] == cur) | (blk_id[None] == cur - 1)
        imp = jnp.where(forced[None, :, None, :], SEL_FORCE, imp)
        imp = jnp.where((blk_id[None] * SEL_BLOCK <= t[:, None])[None, :, None, :], imp, -jnp.inf)
        _, sel = lax.top_k(imp, n_top)
        tok = (sel[..., None] * SEL_BLOCK + tok_in_blk).reshape(bsz, Q_BLOCK, G, n_top * SEL_BLOCK)
        ks = k_s[b_idx, tok, g_idx]
        vs = v_s[b_idx, tok, g_idx]
        s_s = jnp.einsum('bqghd,bqgtd->bqght', qrb, ks) * scale
        p_s = masked_softmax(s_s, (tok <= t[None, :, None, None])[:, :, :, None, :])
        o_s = jnp.einsum('bqght,bqgtd->bqghd', p_s.astype(vs.dtype), vs)
        q0 = t[0]
        kw = lax.dynamic_slice_in_dim(k_wp, q0, WINDOW + Q_BLOCK, axis=1)
        vw = lax.dynamic_slice_in_dim(v_wp, q0, WINDOW + Q_BLOCK, axis=1)
        s_pos = q0 - WINDOW + slab
        win = ((s_pos[None] <= t[:, None]) & (s_pos[None] > t[:, None] - WINDOW)
               & (s_pos[None] >= 0))
        s_w = jnp.einsum('bqghd,bsgd->bqghs', qrb, kw) * scale
        p_w = masked_softmax(s_w, win[None, :, None, None, :])
        o_w = jnp.einsum('bqghs,bsgd->bqghd', p_w.astype(vw.dtype), vw)
        o = gb[..., 0:1] * o_c + gb[..., 1:2] * o_s + gb[..., 2:3] * o_w
        return o.astype(qb.dtype)

    t_blocks = jnp.arange(seq).reshape(-1, Q_BLOCK)
    out = lax.map(block, (to_blocks(q), to_blocks(q_rot), to_blocks(gate), t_blocks))
    return from_blocks(out).reshape(bsz, seq, C_HEADS * HEAD_DIM)

def setup_inputs(seed: int = 0) -> dict:
    key = jax.random.key(seed)
    ks = iter(jax.random.split(key, 32))
    f32 = jnp.float32

    def nrm(shape, scale):
        return jax.random.normal(next(ks), shape, f32) * scale

    def gain(shape):
        return 1.0 + 0.02 * jax.random.normal(next(ks), shape, f32)

    x = nrm((BATCH, SEQ, D_MODEL), 1.0)
    start = jax.random.randint(next(ks), (BATCH, 1), 0, 1024, dtype=jnp.int32)
    positions = start + jnp.arange(SEQ, dtype=jnp.int32)[None, :]
    gp = (DEPTH, S5_GROUPS, S5_STATE)
    return {
        'x': x,
        'positions': positions,
        'ln1_g': gain((DEPTH, D_MODEL)),
        'w_in': nrm((DEPTH, D_MODEL, N_IN), D_MODEL ** -0.5),
        'kv_norm_g': gain((DEPTH, A_KV_RANK)),
        'w_uk': nrm((DEPTH, A_KV_RANK, A_HEADS, A_NOPE), A_KV_RANK ** -0.5),
        'w_uv': nrm((DEPTH, A_KV_RANK, A_HEADS, A_VDIM), A_KV_RANK ** -0.5),
        's5_lambda_re': -0.5 + nrm(gp, 0.01),
        's5_lambda_im': math.pi * jnp.arange(S5_STATE, dtype=f32) + nrm(gp, 0.01),
        's5_log_step': jax.random.uniform(next(ks), (DEPTH, S5_GROUPS), f32,
                                          math.log(S5_DT_MIN), math.log(S5_DT_MAX)),
        's5_b_re': nrm((DEPTH, S5_GROUPS, S5_STATE, S5_GROUP), (2 * S5_GROUP) ** -0.5),
        's5_b_im': nrm((DEPTH, S5_GROUPS, S5_STATE, S5_GROUP), (2 * S5_GROUP) ** -0.5),
        's5_c_re': nrm((DEPTH, S5_GROUPS, S5_GROUP, S5_STATE), (2 * S5_STATE) ** -0.5),
        's5_c_im': nrm((DEPTH, S5_GROUPS, S5_GROUP, S5_STATE), (2 * S5_STATE) ** -0.5),
        's5_d': nrm((DEPTH, S5_GROUPS, S5_GROUP), 1.0),
        's5_glu_w': nrm((DEPTH, B_WIDTH, B_WIDTH), B_WIDTH ** -0.5),
        's5_glu_b': nrm((DEPTH, B_WIDTH), 0.01),
        'cmp_pos_k': nrm((DEPTH, CMP_BLOCK, HEAD_DIM), 0.02),
        'cmp_pos_v': nrm((DEPTH, CMP_BLOCK, HEAD_DIM), 0.02),
        'cmp_k_w1': nrm((DEPTH, CMP_BLOCK * HEAD_DIM, HEAD_DIM), (CMP_BLOCK * HEAD_DIM) ** -0.5),
        'cmp_k_w2': nrm((DEPTH, HEAD_DIM, HEAD_DIM), HEAD_DIM ** -0.5),
        'cmp_v_w1': nrm((DEPTH, CMP_BLOCK * HEAD_DIM, HEAD_DIM), (CMP_BLOCK * HEAD_DIM) ** -0.5),
        'cmp_v_w2': nrm((DEPTH, HEAD_DIM, HEAD_DIM), HEAD_DIM ** -0.5),
        'gain_a': gain((DEPTH, A_HEADS * A_VDIM)),
        'gain_b': gain((DEPTH, B_WIDTH)),
        'gain_c': gain((DEPTH, C_HEADS * HEAD_DIM)),
        'w_out': nrm((DEPTH, D_MIX, D_MODEL), D_MIX ** -0.5),
        'ln2_g': gain((DEPTH, D_MODEL)),
        'w_up': nrm((DEPTH, D_MODEL, D_FF), D_MODEL ** -0.5),
        'w_down': nrm((DEPTH, D_FF, D_MODEL), D_FF ** -0.5),
        'final_g': gain((D_MODEL,)),
    }

def reference(x, positions, ln1_g, w_in, kv_norm_g, w_uk, w_uv,
              s5_lambda_re, s5_lambda_im, s5_log_step, s5_b_re, s5_b_im,
              s5_c_re, s5_c_im, s5_d, s5_glu_w, s5_glu_b,
              cmp_pos_k, cmp_pos_v, cmp_k_w1, cmp_k_w2, cmp_v_w1, cmp_v_w2,
              gain_a, gain_b, gain_c, w_out, ln2_g, w_up, w_down, final_g):
    cos, sin = rope_tables(positions, ROPE_DIM)
    cos_i, sin_i = rope_tables(positions, IDX_ROPE)
    offsets = np.cumsum(IN_SIZES)[:-1].tolist()
    for layer in range(DEPTH):
        h = rms_norm(x, ln1_g[layer])
        (a_q, a_ckv, a_kr, i_q, i_k, i_w, b_u, c_q, c_kv, c_gate) = jnp.split(
            h @ w_in[layer], offsets, axis=-1)
        a_out = dsa_mixer(a_q, a_ckv, a_kr, i_q, i_k, i_w, cos, sin, cos_i, sin_i,
                          kv_norm_g[layer], w_uk[layer], w_uv[layer])
        b_out = s5_mixer(b_u, s5_lambda_re[layer], s5_lambda_im[layer], s5_log_step[layer],
                         s5_b_re[layer], s5_b_im[layer], s5_c_re[layer], s5_c_im[layer],
                         s5_d[layer], s5_glu_w[layer], s5_glu_b[layer])
        c_out = nsa_mixer(c_q, c_kv, c_gate, cos, sin, cmp_pos_k[layer], cmp_pos_v[layer],
                          cmp_k_w1[layer], cmp_k_w2[layer], cmp_v_w1[layer], cmp_v_w2[layer])
        mixed = jnp.concatenate([rms_norm(a_out, gain_a[layer]),
                                 rms_norm(b_out, gain_b[layer]),
                                 rms_norm(c_out, gain_c[layer])], axis=-1)
        x = x + mixed @ w_out[layer]
        z = rms_norm(x, ln2_g[layer]) @ w_up[layer]
        x = x + jnp.square(jax.nn.relu(z)) @ w_down[layer]
    return rms_norm(x, final_g)


_drawn_inputs = setup_inputs


def setup_inputs(seed=0):
    import zlib

    import numpy as np

    out = dict(_drawn_inputs(seed))
    spreads = {}
    factors = {'kv_norm_g': 4.069,
     's5_lambda_re': 8.0,
     's5_glu_b': 8.0,
     'cmp_pos_k': 8.0,
     'cmp_pos_v': 3.755,
     'gain_a': 4.827,
     'gain_b': 5.001,
     'gain_c': 3.593,
     'final_g': 2.768}
    for name, (base, spread) in spreads.items():
        noise = np.random.default_rng([zlib.crc32(name.encode()), seed]).standard_normal(out[name].shape)
        drawn = base * np.exp(spread * noise) if base else spread * noise
        out[name] = __import__('jax').numpy.asarray(drawn.astype(out[name].dtype))
    for name, factor in factors.items():
        out[name] = (out[name] * factor).astype(out[name].dtype)
    return out
```

```python
from contextlib import ExitStack

import numpy as np

import concourse.bass as bass
from concourse import mybir

F32 = mybir.dt.float32
F32R = mybir.dt.float32r
I32 = mybir.dt.int32
ALU = mybir.AluOpType
ACT = mybir.ActivationFunctionType
AX = mybir.AxisListType

PART = 128
D_MODEL = 1024
SEQ = 256
DEPTH = 2
TT = SEQ // PART
KB = D_MODEL // PART
D_FF = 4 * D_MODEL
EPS = 1e-6
NEG = -1e30

HD = 64
ROT = HD // 4
HALF = ROT // 2
A_HEADS, A_RANK, A_NOPE = 4, 128, HD - ROT
I_HEADS, I_DIM = 4, 32
I_HALF = I_DIM // 8
TOPK = min(256, SEQ // 4)
THETA = 500000.0

S5_W, S5_G, S5_GRP, S5_P = 256, 16, 16, 64
PAIRS = S5_G // 2
ROUNDS = 4
C_HEADS, C_KV, C_GRP = 8, 2, 4
CMP, CSTR = 32, 16
N_CMP = (SEQ - CMP) // CSTR + 1

O_AQ = 0
O_CKV = O_AQ + A_HEADS * HD
O_KR = O_CKV + A_RANK
O_IQ = O_KR + ROT
O_IK = O_IQ + I_HEADS * I_DIM
O_IW = O_IK + I_DIM
O_U = O_IW + I_HEADS
O_CQ = O_U + S5_W
O_KC = O_CQ + C_HEADS * HD
O_VC = O_KC + C_KV * HD
O_KS = O_VC + C_KV * HD
O_VS = O_KS + C_KV * HD
O_KW = O_VS + C_KV * HD
O_VW = O_KW + C_KV * HD
O_GT = O_VW + C_KV * HD
N_IN = O_GT + 3 * C_HEADS

RING = 4
PIECE = 1024
TILES = [(O_CQ - 512, 512), (0, O_CQ - 512), (O_CQ, 512), (O_KC, 512), (O_KC + 512, N_IN - O_KC - 512)]
P_IN = 4 * len(TILES)
P_OUT = 8
CHUNK = 512
CHUNKS = D_FF // CHUNK
LOOPED = (CHUNKS - 4) // 2
PIECES = P_IN + P_OUT + 8 * CHUNKS
P_UP0 = P_IN + P_OUT
assert PIECES % RING == 0 and DEPTH == 2


def width(n):
    return 2 * TILES[n // 4][1] if n < P_IN else PIECE


N_PARAMS = 27
PI2 = 2 * float(np.pi)
C1 = 6.28125
C2 = float(np.float32(0.0019350051879882812))
C3 = PI2 - C1 - C2
MAGIC = 1.5 * 2.0 ** 23
GELU_A = float(np.sqrt(2 / np.pi))


class Signal:

    def __init__(self, sem, per, seed=0):
        self.sem, self.per, self.seed, self.made = sem, per, seed, 0

    def by(self, ins, n=1):
        ins.then_inc(self.sem, n)
        self.made += n
        return ins

    def at(self, layer, k):
        return layer * self.per + (self.seed + k)


class Steps:

    def __init__(self, eng, signal, before=0):
        self.eng, self.s, self.n, self.base, self.before = eng, signal, 0, 0, before

    def start(self, layer, extra=0):
        self.base = layer * self.s.per + self.before + extra

    def __call__(self, ins, wait=True):
        ins.then_inc(self.s.sem, 1)
        self.n += 1
        if wait:
            self.eng.wait_ge(self.s.sem, self.base + self.n)


def trunk(nc, x_in, positions, ln1_g, w_in, kv_norm_g, w_uk, w_uv, s5_lambda_re, s5_lambda_im,
          s5_log_step, s5_b_re, s5_b_im, s5_c_re, s5_c_im, s5_d, s5_glu_w, s5_glu_b, cmp_pos_k,
          cmp_pos_v, cmp_k_w1, cmp_k_w2, cmp_v_w1, cmp_v_w2, gain_a, gain_b, gain_c, w_out, ln2_g,
          w_up, w_down, final_g, out, VS, AS, PS):
    ctx = ExitStack()
    with ctx:
        def sb(name, shape, dt=F32):
            return ctx.enter_context(nc.sbuf_tensor(name, shape, dt))

        def sig(name, per, seed=0):
            return Signal(ctx.enter_context(nc.semaphore(name)), per, seed)

        with ExitStack() as split:
            h_hi, h_lo, z_hi, z_lo = (split.enter_context(nc.sbuf_tensor(name, shape, F32R)) for name, shape in (
                ("h_hi", [PART, KB, SEQ]), ("h_lo", [PART, KB, SEQ]),
                ("z_hi", [PART, 2, 4, SEQ]), ("z_lo", [PART, 2, 4, SEQ])))
        ikT = sb("ikT", [PART, 4, SEQ])
        iqT = sb("iqT", [PART, SEQ])
        cT = sb("cT", [PART, SEQ])
        kvc = sb("kvc", [PART, 2, C_KV, PART])
        cqr = sb("cqr", [PART, TT, C_HEADS * HD])
        aqT = sb("aqT", [PART, 2, SEQ])
        vbd = sb("vbd", [PART, C_HEADS, HD])
        akT = sb("akT", [PART, 4, SEQ])
        cqT = sb("cqT", [PART, 4, SEQ])
        cqrT = sb("cqrT", [PART, 4, SEQ])
        kT = sb("kT", [PART, 2, C_KV, SEQ])
        x = sb("x", [PART, TT, D_MODEL])
        raw = sb("raw", [PART, RING, PIECE])
        w_hi = sb("w_hi", [PART, RING, PIECE], F32R)
        w_lo = sb("w_lo", [PART, RING, PIECE], F32R)
        proj = sb("proj", [PART, TT, N_IN])
        projf = proj[:].rearrange("p t n -> p (t n)")
        z_relu = projf[:, 0:4 * SEQ]
        z_sq = projf[:, 4 * SEQ:8 * SEQ]
        o_sq = projf[:, 0:KB * SEQ].rearrange("p (k t) -> p k t", k=KB)
        ident = sb("ident", [PART, PART])
        inv = sb("inv", [PART, 2])
        cmask = sb("cmask", [PART, 384])
        mask8 = sb("mask8", [PART, 8])
        mhalf = sb("mhalf", [PART, 2])
        mquart = sb("mquart", [PART, 4])
        cmcol = sb("cmcol", [PART, 4, PART])
        cadd = sb("cadd", [PART, TT, 16])
        cone = sb("cone", [PART, TT, 16])
        half_neg = sb("half_neg", [PART, 8])
        pos_i = sb("pos_i", [PART, TT], I32)
        pos_f = sb("pos_f", [PART, TT])
        ang = sb("ang", [PART, TT, HALF + I_HALF])
        ang2 = sb("ang2", [PART, TT, HALF + I_HALF])
        ang3 = sb("ang3", [PART, TT, HALF + I_HALF])
        freq = sb("freq", [PART, HALF + I_HALF])
        rc = sb("rc", [PART, TT, ROT])
        rs = sb("rs", [PART, TT, ROT])
        ric = sb("ric", [PART, TT, 2 * I_HALF])
        ris = sb("ris", [PART, TT, 2 * I_HALF])
        g1 = sb("g1", [PART, KB])
        g2 = sb("g2", [PART, KB])
        gm = sb("gm", [PART, KB])
        kvg = sb("kvg", [PART, 1])
        ukv = sb("ukv", [PART, 448])
        glw = sb("glw", [PART, 2, S5_W])
        glb = sb("glb", [PART, 2])
        s5d = sb("s5d", [PART, 2])
        w1 = sb("w1", [PART, 2, 16, HD])
        w2 = sb("w2", [HD, 2, HD])
        lam = sb("lam", [PART, 3, PAIRS])
        braw = sb("braw", [PART, 2, PAIRS, 16])
        craw = sb("craw", [PART, 2, 2, 2, HD])
        sp = sb("sp", [PART, 24, PAIRS])
        e1 = sb("e1", [PART, 2, PAIRS, 17])
        e2 = sb("e2", [PART, 2, PAIRS, 16])
        bb = sb("bb", [PART, 2, PAIRS, 2, 16])
        bt = sb("bt", [PART, 3, 16 * PAIRS])
        et = sb("et", [PART, 2, PAIRS, SEQ])
        btab = sb("btab", [PART, 2, PAIRS, PART])
        ctab = sb("ctab", [PART, 2, PAIRS, PART])
        r1 = sb("r1", [PART, TT])
        r2 = sb("r2", [PART, TT])
        rkv = sb("rkv", [PART, TT])
        rg = sb("rg", [PART, 6])
        stat = sb("stat", [PART, 16])
        pst = sb("pst", [PART, 16])
        uT = sb("uT", [PART, 2, SEQ])
        ptmp = sb("ptmp", [PART, 2, 512])
        scan = sb("scan", [PART, 2, 2, 512])
        dtmp = sb("dtmp", [PART, 6, 512])
        iqr = sb("iqr", [PART, TT, PART])
        ikr = sb("ikr", [PART, TT, 4, I_DIM])
        cn = sb("cn", [PART, TT, A_RANK])
        ak = sb("ak", [PART, TT, A_HEADS, HD])
        av = sb("av", [PART, TT, A_HEADS, PART])
        vpad = sb("vpad", [PART, TT, 2, C_KV, 192])
        cx = dtmp[:, 0:2, :].rearrange("p v (q g n) -> p v q g n", q=16, g=C_KV)
        posT = sb("posT", [PART, 2, 16])
        gk = sb("gk", [HD, 2, C_KV, 16])
        gt = sb("gt", [HD, 3, 2 * C_KV * 16])
        gvr = sb("gvr", [HD, C_HEADS, 16])
        kbd = sb("kbd", [PART, C_KV, 16])
        w2d = sb("w2d", [HD, PART])
        pc, pc2 = (scan[:, 1, 0, i * SEQ:(i + 1) * SEQ].rearrange("p (t h n) -> p t h n", t=TT, h=C_HEADS)
                   for i in range(2))
        cs = sb("cs", [PART, 4, TT * C_HEADS])
        pcT = scan[:, 1, 1, 0:SEQ]
        gate = sb("gate", [PART, TT, 3 * C_HEADS])
        rel = dtmp[:, 0:3, :].rearrange("p a b -> p (a b)").rearrange("p (h n) -> p h n", h=4)
        isc = dtmp[:, 3, 0:384]
        top8 = sb("top8", [PART, 16])
        abias = isc
        tab_zone = [t[:].rearrange("p i j s -> p (i j s)") for t in (btab, ctab)]
        ex = tab_zone[0][:, 0:3 * 384].rearrange("p (b n) -> p b n", b=3)
        sc = tab_zone[0][:, 3 * 384:5 * 384].rearrange("p (b n) -> p b n", b=2)
        pn = tab_zone[1][:, 0:2 * 384].rearrange("p (b n) -> p b n", b=2)
        pT = tab_zone[1][:, 2 * 384:4 * 384].rearrange("p (b n) -> p b n", b=2)
        nmx = sb("nmx", [PART, 2, TT])
        sm = sb("sm", [PART, 3, TT])
        cf = sb("cf", [PART, 2, TT])
        yT = dtmp[:, 4, :]
        yg = dtmp[:, 5, :]
        yt = scan[:, 0, 0, :]
        y2 = scan[:, 0, 1, :]
        pb = [ctx.enter_context(nc.psum_tensor(f"pb{i}", [PART, 512], F32)) for i in range(8)]

        x_loaded = sig("x_loaded", 0)
        consts = sig("consts", 0)
        params = sig("params", 0)
        raw_in = [sig(f"raw_in{i}", 16 * PIECES // RING) for i in range(RING)]
        hi_made = sig("hi_made", PIECES)
        lo_made = sig("lo_made", PIECES, RING)
        used = sig("used", PIECES, RING)
        x_new = sig("x_new", 16, 1)
        xT_ps = sig("xT_ps", 8)
        h_hi_made = sig("h_hi_made", 24)
        h_lo_made = sig("h_lo_made", 24)
        sq_sum = sig("sq_sum", 4)
        r_made = sig("r_made", 4)
        tile_ps = sig("tile_ps", len(TILES))
        tile_sb = sig("tile_sb", len(TILES))
        prep_b = sig("prep_b", 1)
        prep_e = sig("prep_e", ROUNDS)
        step_s5 = sig("step_s5", 1)
        lrs_s5 = sig("lrs_s5", 1)
        mag_s5 = sig("mag_s5", 1)
        ang_rope = sig("ang_rope", 0)
        trig_rope = sig("trig_rope", 0)
        fg_in = sig("fg_in", 0)
        trig_s5 = sig("trig_s5", 1)
        den_s5 = sig("den_s5", 1)
        rden_s5 = sig("rden_s5", 1)
        tab_ps = sig("tab_ps", 2)
        tab_sb = sig("tab_sb", 2)
        uT_ps = sig("uT_ps", 1)
        uT_sb = sig("uT_sb", 1)
        bu_ps = sig("bu_ps", ROUNDS)
        bu_read = sig("bu_read", ROUNDS)
        scanned = sig("scanned", ROUNDS)
        h_made = sig("h_made", ROUNDS)
        roped = sig("roped", 4)
        qcopy = sig("qcopy", 1)
        cn_made = sig("cn_made", 1)
        cT_ps = sig("cT_ps", 1)
        cT_sb = sig("cT_sb", 1)
        ix_ps = sig("ix_ps", 1)
        ix_sb = sig("ix_sb", 1)
        is_ps = sig("is_ps", 4)
        rel_sb = sig("rel_sb", 4)
        kv_ps = sig("kv_ps", 2)
        kv_sb = sig("kv_sb", 2)
        v_sb = sig("v_sb", 1)
        qk_ps = sig("qk_ps", 8)
        qk_sb = sig("qk_sb", 8)
        cx_made = sig("cx_made", 1)
        c1_ps = sig("c1_ps", 1)
        gelu_c = sig("gelu_c", 1)
        tanh_in = sig("tanh_in", 1)
        tanh_c = sig("tanh_c", 1)
        c2_ps = sig("c2_ps", 1)
        c2_sb = sig("c2_sb", 1)
        cs_ps = sig("cs_ps", 1)
        cs_max = sig("cs_max", 1)
        cs_exp = sig("cs_exp", 1)
        pc_made = sig("pc_made", 1)
        pcT_ps = sig("pcT_ps", 1)
        pcT_sb = sig("pcT_sb", 1)
        gate_in = sig("gate_in", 1)
        gate_sb = sig("gate_sb", 1)
        abias_sb = sig("abias_sb", 1)
        UNITS = 2 * C_HEADS + A_HEADS
        s_ps = sig("s_ps", UNITS)
        s_sb = sig("s_sb", UNITS)
        e_sb = sig("e_sb", UNITS)
        pn_sb = sig("pn_sb", UNITS)
        pT_ps = sig("pT_ps", UNITS)
        pT_sb = sig("pT_sb", UNITS)
        pv_done = sig("pv_done", UNITS)
        y_ps = sig("y_ps", 1)
        y_in = sig("y_in", 1)
        y_th = sig("y_th", 1)
        y_g = sig("y_g", 1)
        glu_ps = sig("glu_ps", 1)
        glu_th = sig("glu_th", 1)
        b_made = sig("b_made", 1)
        osq = sig("osq", 1)
        st_ps = sig("st_ps", 1)
        o_ps = sig("o_ps", 6)
        up_ps = sig("up_ps", CHUNKS)
        relu_sb = sig("relu_sb", CHUNKS)
        zsq_sb = sig("zsq_sb", CHUNKS)
        zhi_sb = sig("zhi_sb", CHUNKS)
        zlo_sb = sig("zlo_sb", CHUNKS)
        down_ps = sig("down_ps", 1)
        fin_st = sig("fin_st", 0)
        fin_r = sig("fin_r", 0)
        fin_x = sig("fin_x", 0)
        stored = sig("stored", 0)
        v_steps = sig("v_steps", VS[1])
        a_steps = sig("a_steps", AS[1])
        p_steps = sig("p_steps", PS[1])

        def need(eng, s, layer, k):
            eng.wait_ge(s.sem, s.at(layer, k))

        units = []
        for b in range(4):
            for h in (2 * b, 2 * b + 1):
                for br in range(2):
                    units.append(("C", h, br, b))
        for h in range(A_HEADS):
            units.append(("A", h, 0, h // 2))

        n_params = [0]

        def load_params(pool, lyr):
            def ld(dst, src):
                pool.dma_start(dst, src).then_inc(params.sem, 16)
                n_params[0] += 1
            ld(lam[:, 0, :], s5_lambda_re[lyr].rearrange("(j g) p -> (g p) j", g=2))
            ld(lam[:, 1, :], s5_lambda_im[lyr].rearrange("(j g) p -> (g p) j", g=2))
            st = s5_log_step[lyr].rearrange("(o j g) -> o g j", g=2, o=1)
            for g in range(2):
                ld(lam[64 * g:64 * g + 64, 2, :], st[:, g, :].to_broadcast([64, PAIRS]))
            for i, bsrc in enumerate((s5_b_re, s5_b_im)):
                ld(braw[:, i], bsrc[lyr].rearrange("(j g) p h -> (g p) j h", g=2))
            for i, csrc in enumerate((s5_c_re, s5_c_im)):
                for d in range(2):
                    ld(craw[:, i, :, d, :], csrc[lyr].rearrange("(a g) h p -> (g h) a p", a=2))
            ld(g1[:], ln1_g[lyr].rearrange("(k p) -> p k", p=PART))
            ld(g2[:], ln2_g[lyr].rearrange("(k p) -> p k", p=PART))
            ld(gm[:, 0:2], gain_a[lyr].rearrange("(k p) -> p k", p=PART))
            ld(gm[:, 2:4], gain_b[lyr].rearrange("(k p) -> p k", p=PART))
            ld(gm[:, 4:8], gain_c[lyr].rearrange("(k p) -> p k", p=PART))
            ld(kvg[:], kv_norm_g[lyr].rearrange("(k p) -> p k", p=PART))
            ld(ukv[:, 0:192], w_uk[lyr].rearrange("r h n -> r (h n)"))
            ld(ukv[:, 192:448], w_uv[lyr].rearrange("r h n -> r (h n)"))
            ld(glw[:], s5_glu_w[lyr].rearrange("(k p) n -> p k n", p=PART))
            ld(glb[:], s5_glu_b[lyr].rearrange("(k p) -> p k", p=PART))
            ld(s5d[:], s5_d[lyr].rearrange("(k g) h -> (g h) k", k=2))
            for i, (a, b, c) in enumerate(((cmp_k_w1, cmp_k_w2, cmp_pos_k), (cmp_v_w1, cmp_v_w2, cmp_pos_v))):
                ld(w1[:, i], a[lyr].rearrange("(q p) e -> p q e", p=PART))
                ld(w2[:, i], b[lyr])
                ld(posT[:, i, :], c[lyr].rearrange("(q r) d -> (r d) q", r=2))

        def out_rows(k):
            src = {0: pb[4], 1: yg, 2: pb[5], 3: pb[6]}[k // 2]
            return src[:, (k % 2) * SEQ:(k % 2 + 1) * SEQ]

        ctx.enter_context(nc.allow_non_contiguous_dma(reason="vectors of parameters, one element a partition"))
        block = ctx.enter_context(nc.Block())

        @block.sync
        def _(sp):
            sp.dma_start(pos_i[:], positions.rearrange("o (t p) -> p (o t)", p=PART)).then_inc(x_loaded.sem, 16)
            sp.dma_start(x[:], x_in.rearrange("o (t p) d -> p (o t) d", p=PART)).then_inc(x_loaded.sem, 16)
            with sp.Fori(0, DEPTH) as L:
                def piece(n, dst, src, more=0):
                    sp.wait_ge(lo_made.sem, lo_made.at(L, n + 1 - RING) + more)
                    sp.nop(nofuse=True)
                    raw_in[n % RING].by(sp.dma_start(dst, src), 16)

                w_l = w_in[L].rearrange("(k p) n -> p k n", p=PART)
                n = 0
                for c0, w in TILES:
                    for q in range(4):
                        piece(n, raw[:, n % RING, 0:2 * w].rearrange("p (k n) -> p k n", k=2),
                              w_l[:, 2 * q:2 * q + 2, c0:c0 + w])
                        n += 1
                wo_l = w_out[L].rearrange("(k p) n -> p k n", p=PART)
                for half in range(2):
                    for q in range(4):
                        piece(n, raw[:, n % RING, :].rearrange("p (k n) -> p k n", k=2),
                              wo_l[:, 2 * q:2 * q + 2, half * 512:half * 512 + 512])
                        n += 1
                up_l = w_up[L].rearrange("(k p) n -> p k n", p=PART)
                down_l = w_down[L].rearrange("(f p) n -> p f n", p=PART)

                def up(c, n, more=0):
                    for q in range(4):
                        piece(n + q, raw[:, q, :].rearrange("p (k n) -> p k n", k=2),
                              up_l[:, 2 * q:2 * q + 2, bass.ds(c * CHUNK, CHUNK)], more)

                def down(c, n, more=0):
                    for q in range(4):
                        piece(n + q, raw[:, q, :],
                              down_l[:, bass.ds(c * 4 + q, 1), :].rearrange("p f n -> p (f n)"), more)

                up(0, n)
                with sp.Fori(1, CHUNKS) as c:
                    up(c, n + 4, (c - 1) * 8)
                    down(c - 1, n + 8, (c - 1) * 8)
                down(CHUNKS - 1, PIECES - 4)
            sp.wait_ge(x_new.sem, x_new.at(DEPTH, 0))
            sp.dma_start(proj[:, 1, 0:D_MODEL], final_g.rearrange("(o d) -> o d", o=1).to_broadcast([PART, D_MODEL])).then_inc(fg_in.sem, 16)
            sp.wait_ge(fin_x.sem, 2)
            sp.dma_start(out.rearrange("o (t p) d -> p (o t) d", p=PART), x[:]).then_inc(stored.sem, 16)
            sp.wait_ge(stored.sem, 16)

        @block.gpsimd
        def _(pool):
            step = Steps(pool, p_steps, PS[0])
            for t, v in ((ident, 0.0), (cmask, 0.0), (mask8, 1.0), (mhalf, 1.0), (mquart, 1.0),
                         (cmcol, 1.0), (cadd, 0.0), (cone, 1.0), (half_neg, -0.5), (av, 0.0), (vpad, 0.0),
                         (gk, 0.0), (gvr, 0.0)):
                m = pool.memset(t[:], v)
            pool.memset(inv[:, 0:1], 1.0 / 256)
            pool.memset(inv[:, 1:2], 1.0 / 512)
            for i in range(HALF):
                pool.memset(freq[:, i:i + 1], float(np.float32(THETA ** (-(2.0 * i) / ROT))))
            for i in range(I_HALF):
                m = pool.memset(freq[:, HALF + i:HALF + i + 1], float(np.float32(THETA ** (-(2.0 * i) / (2 * I_HALF)))))
            step(m)

            def select(t, pattern, op, fill, base, mul):
                step(pool.affine_select(out=t, in_=t, compare_op=op, fill=fill, base=base,
                                        pattern=pattern, channel_multiplier=mul))
            select(ident[:], [[-1, PART]], ALU.not_equal, 1.0, 0, 1)
            for a in (0, 256):
                select(cmask[:, a:a + PART], [[-1, PART]], ALU.is_ge, NEG, 0, 1)
            select(mask8[:], [[-16, 8]], ALU.is_ge, 0.0, 0, 1)
            select(mask8[:], [[16, 8]], ALU.is_ge, 0.0, 15, -1)
            select(mhalf[:], [[-64, 2]], ALU.is_ge, 0.0, 0, 1)
            select(mhalf[:], [[64, 2]], ALU.is_ge, 0.0, 63, -1)
            select(mquart[:], [[-32, 4]], ALU.is_ge, 0.0, 0, 1)
            select(mquart[:], [[32, 4]], ALU.is_ge, 0.0, 31, -1)
            for g in range(2):
                v = cmcol[64 * g:64 * g + 64]
                select(v, [[-32, 4], [1, PART]], ALU.is_ge, 0.0, -16 * g, 0)
                select(v, [[32, 4], [-1, PART]], ALU.is_ge, 0.0, 16 * g + 15, 0)
            for t, fill in ((cadd, NEG), (cone, 0.0)):
                select(t[:], [[PART, TT], [-CSTR, 16]], ALU.is_ge, fill, -(CMP - 1), 1)
            step(pool.memset(cadd[:, :, N_CMP:16], NEG))
            consts.by(pool.memset(cone[:, :, N_CMP:16], 0.0))

            def tt(o, a, b, op):
                step(pool.tensor_tensor(o, a, b, op))

            def ts(o, a, s1, s2, op0, op1=ALU.bypass):
                pool.nop(nofuse=True)
                step(pool.tensor_scalar(o, a, s1, s2, op0, op1) if s2 is not None
                     else pool.tensor_scalar(o, a, s1, None, op0))

            def cmul(oc, os, ac, as_, bc, bs, t):
                tt(oc, ac, bc, ALU.mult)
                tt(t, as_, bs, ALU.mult)
                tt(oc, oc, t, ALU.subtract)
                tt(os, as_, bc, ALU.mult)
                tt(t, ac, bs, ALU.mult)
                tt(os, os, t, ALU.add)

            def prep(occ):
                pool.wait_ge(params.sem, (occ + 1) * 16 * N_PARAMS)
                lr, li = lam[:, 0, :], lam[:, 1, :]
                S = lambda i: sp[:, i, :]
                need(pool, step_s5, occ, 1)
                lrs_s5.by(pool.tensor_tensor(S(21), lr, S(0), ALU.mult))
                tt(S(2), li, S(0), ALU.mult)
                ts(S(3), S(2), 1.0 / PI2, MAGIC, ALU.mult, ALU.add)
                ts(S(3), S(3), -MAGIC, None, ALU.add)
                for c in (C1, C2, C3):
                    ts(S(4), S(3), c, None, ALU.mult)
                    tt(S(2), S(2), S(4), ALU.subtract)
                ts(S(2), S(2), 3.1415925, -3.1415925, ALU.min, ALU.max)
                ts(S(4), S(2), PI2 / 4, PI2, ALU.is_gt, ALU.mult)
                ts(S(3), S(2), PI2 / 4, None, ALU.add)
                tt(S(3), S(3), S(4), ALU.subtract)
                tt(S(5), lr, lr, ALU.mult)
                tt(S(6), li, li, ALU.mult)
                den_s5.by(pool.tensor_tensor(S(7), S(5), S(6), ALU.add))
                need(pool, trig_s5, occ, 1)
                need(pool, rden_s5, occ, 1)
                tt(S(11), S(1), S(9), ALU.mult)
                tt(S(12), S(1), S(8), ALU.mult)
                ts(S(11), S(11), -1.0, None, ALU.add)
                tt(S(13), S(11), lr, ALU.mult)
                tt(S(14), S(12), li, ALU.mult)
                tt(S(13), S(13), S(14), ALU.add)
                tt(S(13), S(13), S(10), ALU.mult)
                tt(S(15), S(12), lr, ALU.mult)
                tt(S(14), S(11), li, ALU.mult)
                tt(S(15), S(15), S(14), ALU.subtract)
                tt(S(15), S(15), S(10), ALU.mult)
                zr = S(13).unsqueeze(2).to_broadcast([PART, PAIRS, 16])
                zi = S(15).unsqueeze(2).to_broadcast([PART, PAIRS, 16])
                T = [bt[:, i, :].rearrange("p (j h) -> p j h", j=PAIRS) for i in range(3)]
                for i, op in ((0, ALU.subtract), (1, ALU.add)):
                    tt(T[0], zr, braw[:, i], ALU.mult)
                    tt(T[1], zi, braw[:, 1 - i], ALU.mult)
                    tt(bb[:, i, :, 0, :], T[0], T[1], op)
                    m = pool.tensor_tensor(bb[:, i, :, 1, :], T[0], T[1], op)
                    if i == 0:
                        step(m)
                prep_b.by(m)
                pool.nop(nofuse=True)
                for e in (e1, e2):
                    pool.memset(e[:, 0, :, 0:1], 1.0)
                    pool.memset(e[:, 1, :, 0:1], 0.0)
                pool.tensor_copy(e1[:, 0, :, 1], S(9))
                step(pool.tensor_copy(e1[:, 1, :, 1], S(8)))

                def double(e, n, m):
                    w = [e[:, i, :, n:n + 1].to_broadcast([PART, PAIRS, m]) for i in range(2)]
                    cmul(e[:, 0, :, n + 1:n + 1 + m], e[:, 1, :, n + 1:n + 1 + m], e[:, 0, :, 1:1 + m],
                         e[:, 1, :, 1:1 + m], w[0], w[1],
                         bt[:, 0, 0:PAIRS * m].rearrange("p (j m) -> p j m", m=m))
                for n in (1, 2, 4, 8):
                    double(e1, n, n)
                pool.nop(nofuse=True)
                pool.tensor_copy(e2[:, 0, :, 1], e1[:, 0, :, 16])
                step(pool.tensor_copy(e2[:, 1, :, 1], e1[:, 1, :, 16]))
                for n, m in ((1, 1), (2, 2), (4, 4), (8, 7)):
                    double(e2, n, m)
                for r in range(ROUNDS):
                    for j in (2 * r, 2 * r + 1):
                        A = [e2[:, i, j, :].unsqueeze(2).to_broadcast([PART, 16, 16]) for i in range(2)]
                        B = [e1[:, i, j, 0:16].unsqueeze(1).to_broadcast([PART, 16, 16]) for i in range(2)]
                        O = [et[:, i, j, :].rearrange("p (a b) -> p a b", a=16) for i in range(2)]
                        t = ptmp[:, 0, 0:SEQ].rearrange("p (a b) -> p a b", a=16)
                        tt(O[0], A[0], B[0], ALU.mult)
                        tt(t, A[1], B[1], ALU.mult)
                        tt(O[0], O[0], t, ALU.subtract)
                        tt(O[1], A[1], B[0], ALU.mult)
                        tt(t, A[0], B[1], ALU.mult)
                        m = pool.tensor_tensor(O[1], O[1], t, ALU.add)
                        if j == 2 * r:
                            step(m)
                    prep_e.by(m)

            def rstd(L, k, o, ss, n, scale=1.0):
                need(pool, sq_sum, L, k)
                w = o.shape[1]
                ts(pst[:, 0:w], ss, scale / n, EPS, ALU.mult, ALU.add)
                r_made.by(pool.tensor_tensor(o, pst[:, 0:w], half_neg[:, 0:w], ALU.pow))

            load_params(pool, 0)
            assert n_params[0] == N_PARAMS
            prep(0)
            n0 = step.n
            with pool.Fori(0, DEPTH) as L:
                step.n = 0
                step.before = PS[0]
                step.start(L)
                rstd(L, 1, r1[:], stat[:, 0:2], D_MODEL)
                rstd(L, 2, rkv[:], stat[:, 2:4], A_RANK)
                for r in range(ROUNDS):
                    need(pool, scanned, L, r + 1)
                    ec = et[:, 0, 2 * r:2 * r + 2, :].rearrange("p j t -> p (j t)")
                    es = et[:, 1, 2 * r:2 * r + 2, :].rearrange("p j t -> p (j t)")
                    gr, gi = scan[:, r % 2, 0, :], scan[:, r % 2, 1, :]
                    tt(ptmp[:, 0, :], es, gi, ALU.mult)
                    tt(ptmp[:, 1, :], ec, gi, ALU.mult)
                    tt(ec, ec, gr, ALU.mult)
                    tt(es, es, gr, ALU.mult)
                    tt(ec, ec, ptmp[:, 0, :], ALU.subtract)
                    h_made.by(pool.tensor_tensor(es, es, ptmp[:, 1, :], ALU.add))
                rstd(L, 3, rg[:], stat[:, 4:10], 1.0)
                rstd(L, 4, r2[:], stat[:, 10:12], D_MODEL)
                need(pool, h_lo_made, L, 24)
                need(pool, h_hi_made, L, 24)
                pool.nop(nofuse=True)
                load_params(pool, DEPTH - 1)
                prep(L + 1)
            assert PS == (n0, step.n), f"PSTEPS = {(n0, step.n)}"
            pool.wait_ge(fin_st.sem, 1)
            step.n = 0
            step.start(DEPTH)
            ts(pst[:, 0:2], stat[:, 12:14], 1.0 / D_MODEL, EPS, ALU.mult, ALU.add)
            pool.tensor_tensor(r1[:], pst[:, 0:2], half_neg[:, 0:2], ALU.pow).then_inc(fin_r.sem, 1)

        @block.scalar
        def _(act):
            step = Steps(act, a_steps, AS[0])

            def s5_exp(occ):
                act.wait_ge(params.sem, (occ + 1) * 16 * N_PARAMS)
                step_s5.by(act.activation(sp[:, 0, :], lam[:, 2, :], ACT.Exp))
                need(act, lrs_s5, occ, 1)
                mag_s5.by(act.activation(sp[:, 1, :], sp[:, 21, :], ACT.Exp))
                need(act, den_s5, occ, 1)
                step(act.activation(sp[:, 8, :], sp[:, 2, :], ACT.Sin))
                trig_s5.by(act.activation(sp[:, 9, :], sp[:, 3, :], ACT.Sin))

            def h_parts(L, stage, gains):
                for k in range(KB):
                    need(act, xT_ps, L, (4 if stage == 2 else 0) + k // 2 + 1)
                    h_hi_made.by(act.activation(h_hi[:, k, :], pb[k // 2][:, (k % 2) * SEQ:(k % 2 + 1) * SEQ],
                                                ACT.Copy, scale=gains[:, k:k + 1]))

            def hi(L, n, more=0):
                act.wait_ge(raw_in[n % RING].sem, raw_in[0].at(L, 16 * (n // RING + 1)) + more * 4)
                act.wait_ge(used.sem, used.at(L, n + 1 - RING) + more)
                hi_made.by(act.activation(w_hi[:, n % RING, 0:width(n)], raw[:, n % RING, 0:width(n)], ACT.Copy))

            def sums(L, c, s):
                for t in range(TT):
                    m = act.activation(projf[:, 0:D_MODEL], x[:, t, :], ACT.Square, accum_out=stat[:, c + t:c + t + 1])
                    if t < TT - 1:
                        step(m)
                s(m)

            act.wait_ge(ang_rope.sem, 1)
            step(act.activation(ang2[:], ang[:], ACT.Sin))
            act.activation(ang[:], ang3[:], ACT.Sin).then_inc(trig_rope.sem, 1)
            s5_exp(0)
            n0 = step.n
            with act.Fori(0, DEPTH) as L:
                step.n = 0
                step.before = AS[0]
                step.start(L)
                h_parts(L, 0, g1)
                sums(L, 0, sq_sum.by)
                for n in range(8):
                    hi(L, n)

                def tile_out(i):
                    c0, w = TILES[i]
                    need(act, tile_ps, L, i + 1)
                    for t in range(TT):
                        src = pb[4 + 2 * (i % 2) + t][:, 0:w]
                        dst = proj[:, t, c0:c0 + w]
                        if c0 == O_CQ:
                            src = src.rearrange("p (g j d) -> p g j d", g=2, d=HD)
                            dst = dst.rearrange("p (j g d) -> p g j d", g=2, d=HD)
                        m = act.activation(dst, src, ACT.Copy, scale=r1[:, t:t + 1])
                        if t < TT - 1:
                            step(m)
                    tile_sb.by(m)

                need(act, r_made, L, 1)
                tile_out(0)
                for n in range(8, 12):
                    hi(L, n)
                tile_out(1)
                need(act, tile_sb, L, 2)
                for t in range(TT):
                    m = act.activation(cn[:, t, :], proj[:, t, O_CKV:O_CKV + A_RANK], ACT.Square,
                                       accum_out=stat[:, 2 + t:3 + t])
                    if t < TT - 1:
                        step(m)
                sq_sum.by(m)
                need(act, uT_ps, L, 1)
                uT_sb.by(act.activation(uT[:].rearrange("p a b -> p (a b)"), pb[0][:], ACT.Copy))
                for n in range(12, 16):
                    hi(L, n)
                tile_out(2)
                for n in range(16, 20):
                    hi(L, n)
                tile_out(3)
                tile_out(4)
                for n in range(20, 24):
                    hi(L, n)
                need(act, tile_sb, L, 5)
                gate_in.by(act.activation(gate[:], proj[:, :, O_GT:O_GT + 24], ACT.Tanh, scale=0.5))
                step(act.activation(cqr[:], proj[:, :, O_CQ:O_CQ + 512], ACT.Copy))
                qcopy.by(act.activation(vpad[:, :, 0, :, 64:128],
                                        proj[:, :, O_VS:O_VS + 128].rearrange("p t (g d) -> p t g d", g=2), ACT.Copy))
                v_sb.by(act.activation(vpad[:, :, 1, :, 64:128],
                                       proj[:, :, O_VW:O_VW + 128].rearrange("p t (g d) -> p t g d", g=2), ACT.Copy))
                need(act, ix_ps, L, 1)
                step(act.activation(iqT[:], pb[3][:, 0:SEQ], ACT.Copy))
                for h in range(I_HEADS):
                    m = act.activation(ikT[:, h, :], pb[3][:, SEQ:2 * SEQ], ACT.Copy, scale=mquart[:, h:h + 1])
                    if h < I_HEADS - 1:
                        step(m)
                ix_sb.by(m)
                need(act, cT_ps, L, 1)
                cT_sb.by(act.activation(cT[:], pb[0][:, 0:SEQ], ACT.Copy, scale=kvg[:]))
                need(act, scanned, L, ROUNDS)
                for h in range(I_HEADS):
                    need(act, is_ps, L, h + 1)
                    rel_sb.by(act.activation(rel[:, h, :], pb[4 + h][:, 0:384], ACT.Relu, scale=I_DIM ** -0.5))
                for t in range(TT):
                    need(act, kv_ps, L, t + 1)
                    step(act.activation(ak[:, t, :, ROT:HD], pb[1 + t][:, 0:192].rearrange("p (h n) -> p h n", h=4),
                                        ACT.Copy))
                    vsrc = pb[1 + t][:, 192:448].rearrange("p (a b d) -> p b a d", b=2, d=HD)
                    step(act.activation(av[:, t, 0::2, 0:HD], vsrc[:, 0], ACT.Copy))
                    kv_sb.by(act.activation(av[:, t, 1::2, HD:PART], vsrc[:, 1], ACT.Copy))
                for i in range(8):
                    need(act, qk_ps, L, i + 1)
                    src = pb[i % 4]
                    if i in (0, 1):
                        m = act.activation(cqT[:, 2 * i:2 * i + 2, :].rearrange("p a b -> p (a b)"), src[:], ACT.Copy)
                    elif i == 2:
                        for kv in range(2):
                            for g in range(2):
                                for par in range(2):
                                    m = act.activation(
                                        kvc[64 * par:64 * par + 64, kv, g, :],
                                        src[64 * g:64 * g + 64, kv * SEQ + par:(kv + 1) * SEQ:2], ACT.Copy)
                                    if (kv, g, par) != (1, 1, 1):
                                        step(m)
                    elif i in (3, 4):
                        m = act.activation(cqrT[:, 2 * (i - 3):2 * (i - 3) + 2, :].rearrange("p a b -> p (a b)"),
                                           src[:], ACT.Copy)
                    elif i == 5:
                        for g in range(2):
                            m = act.activation(kT[:, :, g, :], src[:].rearrange("p (b n) -> p b n", b=2), ACT.Copy,
                                               scale=mhalf[:, g:g + 1])
                            if g == 0:
                                step(m)
                    elif i == 6:
                        m = act.activation(aqT[:].rearrange("p a b -> p (a b)"), src[:], ACT.Copy)
                    else:
                        for g in range(2):
                            m = act.activation(akT[:, g::2, :], src[:].rearrange("p (b n) -> p b n", b=2), ACT.Copy,
                                               scale=mhalf[:, g:g + 1])
                            if g == 0:
                                step(m)
                    qk_sb.by(m)
                need(act, y_in, L, 1)
                y_th.by(act.activation(y2, y2, ACT.Tanh, scale=GELU_A))
                need(act, tanh_in, L, 1)
                tanh_c.by(act.activation(gt[:, 2, :], gt[:, 1, :], ACT.Tanh, scale=GELU_A))
                need(act, glu_ps, L, 1)
                for k in range(2):
                    m = act.activation(y2[:, k * SEQ:(k + 1) * SEQ], pb[3][:, k * SEQ:(k + 1) * SEQ], ACT.Tanh,
                                       scale=0.5, bias=glb[:, k:k + 1])
                    if k == 0:
                        step(m)
                glu_th.by(m)
                need(act, cs_max, L, 1)
                cs_exp.by(act.activation(pc2[:], pc2[:], ACT.Exp))
                for i in range(UNITS + 2):
                    if i < UNITS:
                        need(act, s_sb, L, i + 1)
                        if i >= 3:
                            need(act, pn_sb, L, i - 2)
                        step(act.activation(ex[:, i % 3, 0:PART], sc[:, i % 2, 0:PART], ACT.Exp, scale=-1.0,
                                            bias=nmx[:, i % 2, 0:1], accum_out=sm[:, i % 3, 0:1]))
                        e_sb.by(act.activation(ex[:, i % 3, PART:384], sc[:, i % 2, PART:384], ACT.Exp, scale=-1.0,
                                               bias=nmx[:, i % 2, 1:2], accum_out=sm[:, i % 3, 1:2]))
                    if i == 1:
                        need(act, pcT_ps, L, 1)
                        pcT_sb.by(act.activation(pcT[:], pb[3][:, 0:SEQ], ACT.Copy))
                    if i >= 2:
                        need(act, pT_ps, L, i - 1)
                        if i >= 4:
                            need(act, pv_done, L, i - 3)
                        pT_sb.by(act.activation(pT[:, i % 2, :], pb[2 + i % 2][:, 0:384], ACT.Copy))
                need(act, pv_done, L, UNITS)
                need(act, b_made, L, 1)
                for k in range(KB):
                    src = out_rows(k)
                    m = act.activation(o_sq[:, k, :], src, ACT.Square)
                    if k < KB - 1:
                        step(m)
                osq.by(m)
                for k in range(KB):
                    h_hi_made.by(act.activation(h_hi[:, k, :], out_rows(k), ACT.Copy, scale=gm[:, k:k + 1]))
                need(act, st_ps, L, 1)
                sq_sum.by(act.activation(stat[:, 4:10], pb[0][:, 0:6], ACT.Copy))
                for n in range(24, P_UP0 + 4):
                    hi(L, n)
                h_parts(L, 2, g2)
                sums(L, 10, sq_sum.by)

                def relu(c, par):
                    act.wait_ge(up_ps.sem, up_ps.at(L, 1) + c)
                    for i in range(2):
                        m = act.activation(z_relu[:, i * 512:(i + 1) * 512], pb[2 * par + i][:], ACT.Relu)
                        if i == 0:
                            step(m)
                    relu_sb.by(m)
                    act.wait_ge(zsq_sb.sem, zsq_sb.at(L, 1) + c)
                    zhi_sb.by(act.activation(z_hi[:, par].rearrange("p f t -> p (f t)"), z_sq, ACT.Copy))

                def chunk(c, par, more):
                    for n in range(P_UP0 + 4, P_UP0 + 12):
                        hi(L, n, more=more)
                    relu(c, par)

                need(act, sq_sum, L, 4)
                relu(0, 0)
                chunk(1, 1, 0)
                before = step.n
                with act.Fori(0, LOOPED) as cc:
                    step.start(L, cc * AS[2])
                    chunk(cc * 2 + 2, 0, cc * 16 + 8)
                    chunk(cc * 2 + 3, 1, cc * 16 + 16)
                    inner = step.n - before
                step.start(L)
                step.n = before + inner * LOOPED
                s5_exp(L + 1)
                chunk(CHUNKS - 2, 0, CHUNKS * 8 - 24)
                chunk(CHUNKS - 1, 1, CHUNKS * 8 - 16)
                for n in range(PIECES - 4, PIECES):
                    hi(L, n)
            assert AS == (n0, step.n, inner), f"ASTEPS = {(n0, step.n, inner)}"
            step.n = 0
            step.start(DEPTH)
            need(act, x_new, DEPTH, 0)
            sums(DEPTH, 12, lambda m: m.then_inc(fin_st.sem, 1))

        @block.vector
        def _(dve):
            step = Steps(dve, v_steps, VS[0])

            def tt(o, a, b, op, wait=True):
                step(dve.tensor_tensor(o, a, b, op), wait)

            def ts(o, a, s1, s2, op0, op1=ALU.bypass, wait=True):
                step(dve.tensor_scalar(o, a, s1, s2, op0, op1) if s2 is not None
                     else dve.tensor_scalar(o, a, s1, None, op0), wait)

            def stt(o, a, s, b, op0, op1):
                return dve.scalar_tensor_tensor(out=o, in0=a, scalar=s, in1=b, op0=op0, op1=op1)

            dve.memset(nmx[:], 0.0).then_inc(lo_made.sem, RING)
            dve.wait_ge(x_loaded.sem, 32)
            dve.memset(cf[:], 0.0).then_inc(x_new.sem, 1)
            dve.wait_ge(consts.sem, 1)
            step(dve.tensor_copy(pos_f[:], pos_i[:]))
            nf = HALF + I_HALF
            tt(ang[:], pos_f[:].unsqueeze(2).to_broadcast([PART, TT, nf]),
               freq[:].unsqueeze(1).to_broadcast([PART, TT, nf]), ALU.mult)
            ts(ang3[:], ang[:], 1.0 / PI2, MAGIC, ALU.mult, ALU.add)
            ts(ang3[:], ang3[:], -MAGIC, None, ALU.add)
            for c in (C1, C2, C3):
                ts(ang2[:], ang3[:], c, None, ALU.mult)
                tt(ang[:], ang[:], ang2[:], ALU.subtract)
            ts(ang[:], ang[:], 3.1415925, -3.1415925, ALU.min, ALU.max)
            ts(ang2[:], ang[:], PI2 / 4, PI2, ALU.is_gt, ALU.mult)
            ts(ang3[:], ang[:], PI2 / 4, None, ALU.add)
            dve.tensor_tensor(ang3[:], ang3[:], ang2[:], ALU.subtract).then_inc(ang_rope.sem, 1)
            dve.wait_ge(trig_rope.sem, 1)
            for cos_t, sin_t, a, n in ((rc, rs, 0, HALF), (ric, ris, HALF, I_HALF)):
                for d in range(2):
                    step(dve.tensor_copy(cos_t[:, :, d * n:(d + 1) * n], ang[:, :, a:a + n]))
                ts(sin_t[:, :, 0:n], ang2[:, :, a:a + n], -1.0, None, ALU.mult)
                step(dve.tensor_copy(sin_t[:, :, n:2 * n], ang2[:, :, a:a + n]))

            def den(occ):
                need(dve, den_s5, occ, 1)
                rden_s5.by(dve.reciprocal(sp[:, 10, :], sp[:, 7, :]))

            den(0)
            n0 = step.n

            def rope(o, src, heads, cos_t, sin_t, n):
                m = 2 * n
                c4 = cos_t[:].unsqueeze(2).to_broadcast([PART, TT, heads, m])
                s4 = sin_t[:].unsqueeze(2).to_broadcast([PART, TT, heads, m])
                A, B = [dtmp[:, i, 0:TT * heads * m].rearrange("p (t h m) -> p t h m", t=TT, h=heads)
                        for i in range(2)]
                tt(A, src, c4, ALU.mult, False)
                tt(B[:, :, :, 0:n], src[:, :, :, n:m], s4[:, :, :, 0:n], ALU.mult, False)
                tt(B[:, :, :, n:m], src[:, :, :, 0:n], s4[:, :, :, n:m], ALU.mult)
                return A, B

            def heads_of(t, off, n, w):
                return t[:, :, off:off + n * w].rearrange("p t (h w) -> p t h w", w=w)

            with dve.Fori(0, DEPTH) as L:
                step.n = 0
                step.start(L)

                def lo(n, more=0):
                    dve.wait_ge(hi_made.sem, hi_made.at(L, n + 1) + more)
                    lo_made.by(dve.tensor_tensor(w_lo[:, n % RING, 0:width(n)], raw[:, n % RING, 0:width(n)],
                                                 w_hi[:, n % RING, 0:width(n)].bitcast(F32), ALU.subtract))

                def h_rest(base, gains, src_of):
                    for k in range(KB):
                        need(dve, h_hi_made, L, base + (k | 1) + 1)
                        h_lo_made.by(stt(h_lo[:, k, :], src_of(k), gains[:, k:k + 1],
                                         h_hi[:, k, :].bitcast(F32), ALU.mult, ALU.subtract))

                def xT_rows(k):
                    return pb[k // 2][:, (k % 2) * SEQ:(k % 2 + 1) * SEQ]

                h_rest(0, g1, xT_rows)
                ts(glb[:], glb[:], 0.5, None, ALU.mult)
                for d in range(2):
                    step(dve.tensor_copy(w2d[:, d * HD:(d + 1) * HD], w2[:, 0, :]))
                for n in range(8):
                    lo(n)

                need(dve, tab_ps, L, 1)
                for i in range(2):
                    for a in range(2):
                        src = pb[0][:, (2 * i + a) * PART:(2 * i + a + 1) * PART].rearrange("p (g s) -> p g s", g=2)
                        m = dve.tensor_tensor(
                            btab[:, i, 4 * a:4 * a + 4, :].rearrange("p j (g s) -> p j g s", g=2),
                            src.unsqueeze(1).to_broadcast([PART, 4, 2, HD]),
                            mask8[:].rearrange("p (j g) -> p j g", g=2).unsqueeze(3).to_broadcast([PART, 4, 2, HD]),
                            ALU.mult)
                        if (i, a) != (1, 1):
                            step(m, False)
                tab_sb.by(m)
                need(dve, tab_ps, L, 2)
                for i in range(2):
                    for a in range(2):
                        src = pb[1][:, (2 * i + a) * PART:(2 * i + a + 1) * PART]
                        m = stt(ctab[:, i, 4 * a:4 * a + 4, :], src.unsqueeze(1).to_broadcast([PART, 4, PART]),
                                1.0 - 2 * i, cmcol[:], ALU.mult, ALU.mult)
                        if (i, a) != (1, 1):
                            step(m, False)
                tab_sb.by(m)
                for n in range(8, 12):
                    lo(n)

                def s5_round(r):
                    need(dve, bu_ps, L, r + 1)
                    need(dve, prep_e, L, r + 1)
                    ec = et[:, 0, 2 * r:2 * r + 2, :].rearrange("p j t -> p (j t)")
                    es = et[:, 1, 2 * r:2 * r + 2, :].rearrange("p j t -> p (j t)")
                    tt(dtmp[:, 0, :], ec, pb[1][:], ALU.mult, False)
                    tt(dtmp[:, 1, :], es, pb[2][:], ALU.mult, False)
                    tt(dtmp[:, 2, :], ec, pb[2][:], ALU.mult, False)
                    bu_read.by(dve.tensor_tensor(dtmp[:, 3, :], es, pb[1][:], ALU.mult))
                    need(dve, bu_read, L, r + 1)
                    dve.wait_ge(v_steps.sem, step.base + step.n)
                    tt(dtmp[:, 4, :], dtmp[:, 0, :], dtmp[:, 1, :], ALU.add, False)
                    tt(dtmp[:, 5, :], dtmp[:, 2, :], dtmp[:, 3, :], ALU.subtract)
                    if r >= 2:
                        need(dve, h_made, L, r - 1)
                    for j in range(2):
                        mag = sp[:, 1, 2 * r + j:2 * r + j + 1].to_broadcast([PART, SEQ])
                        for i in range(2):
                            m = dve.tensor_tensor_scan(scan[:, r % 2, i, j * SEQ:(j + 1) * SEQ], mag,
                                                       dtmp[:, 4 + i, j * SEQ:(j + 1) * SEQ], 0.0, ALU.mult, ALU.add)
                            if (j, i) != (1, 1):
                                step(m, False)
                    scanned.by(m)
                    need(dve, scanned, L, r + 1)

                s5_round(0)
                need(dve, tile_sb, L, 2)
                step(dve.tensor_copy(iqr[:], proj[:, :, O_IQ:O_IQ + PART]))
                step(dve.tensor_copy(ikr[:], proj[:, :, O_IK:O_IK + I_DIM].unsqueeze(2).to_broadcast(
                    [PART, TT, 4, I_DIM])))
                A, B = rope(None, heads_of(proj, O_IQ, 4, I_DIM)[:, :, :, 0:2 * I_HALF], 4, ric, ris, I_HALF)
                tt(heads_of(iqr, 0, 4, I_DIM)[:, :, :, 0:2 * I_HALF], A, B, ALU.add)
                A, B = rope(None, heads_of(proj, O_IK, 1, I_DIM)[:, :, :, 0:2 * I_HALF], 1, ric, ris, I_HALF)
                roped.by(dve.tensor_tensor(ikr[:, :, :, 0:2 * I_HALF],
                                           A.to_broadcast([PART, TT, 4, 2 * I_HALF]),
                                           B.to_broadcast([PART, TT, 4, 2 * I_HALF]), ALU.add))
                need(dve, roped, L, 1)
                A, B = rope(None, heads_of(proj, O_AQ, 4, HD)[:, :, :, 0:ROT], 4, rc, rs, HALF)
                tt(heads_of(proj, O_AQ, 4, HD)[:, :, :, 0:ROT], A, B, ALU.add)
                A, B = rope(None, heads_of(proj, O_KR, 1, ROT), 1, rc, rs, HALF)
                roped.by(dve.tensor_tensor(ak[:, :, :, 0:ROT], A.to_broadcast([PART, TT, 4, ROT]),
                                           B.to_broadcast([PART, TT, 4, ROT]), ALU.add))
                need(dve, roped, L, 2)
                need(dve, r_made, L, 2)
                for t in range(TT):
                    m = dve.tensor_scalar(cn[:, t, :], proj[:, t, O_CKV:O_CKV + A_RANK], rkv[:, t:t + 1], None, ALU.mult)
                    if t == 0:
                        step(m, False)
                cn_made.by(m)
                for n in range(12, 16):
                    lo(n)
                s5_round(1)
                for n in range(16, 20):
                    lo(n)
                s5_round(2)
                need(dve, tile_sb, L, 5)
                for o in (O_KS, O_KW):
                    v = heads_of(proj, o, 2, HD)[:, :, :, 0:ROT]
                    A, B = rope(None, v, 2, rc, rs, HALF)
                    m = dve.tensor_tensor(v, A, B, ALU.add)
                    if o == O_KS:
                        step(m)
                    else:
                        roped.by(m)
                need(dve, roped, L, 3)
                need(dve, v_sb, L, 1)
                A, B = rope(None, heads_of(proj, O_CQ, 8, HD)[:, :, :, 0:ROT], 8, rc, rs, HALF)
                roped.by(dve.tensor_tensor(heads_of(cqr, 0, 8, HD)[:, :, :, 0:ROT], A, B, ALU.add))
                need(dve, roped, L, 4)
                s5_round(3)
                for n in range(20, 24):
                    lo(n)
                need(dve, gate_in, L, 1)
                gate_sb.by(dve.tensor_scalar(gate[:], gate[:], 0.5, 0.5, ALU.mult, ALU.add))
                need(dve, gate_sb, L, 1)

                ts(cs[:, 3, 0:8].rearrange("p (t h) -> p t h", t=TT), proj[:, :, O_IW:O_IW + 4],
                   I_HEADS ** -0.5, None, ALU.mult)
                for h in range(I_HEADS):
                    need(dve, rel_sb, L, h + 1)
                    for t, (a, b) in enumerate(((0, PART), (PART, 384))):
                        if h == 0:
                            ts(isc[:, a:b], rel[:, 0, a:b], cs[:, 3, 4 * t:4 * t + 1], None, ALU.mult)
                        else:
                            step(stt(isc[:, a:b], rel[:, h, a:b], cs[:, 3, 4 * t + h:4 * t + h + 1], isc[:, a:b],
                                     ALU.mult, ALU.add))
                tt(isc, isc, cmask[:], ALU.add)
                for i in range(TOPK // 8):
                    dve.nop(nofuse=True)
                    for a, b, c in ((0, PART, 0), (PART, 384, 8)):
                        step(dve.max(top8[:, c:c + 8], isc[:, a:b]), False)
                    dve.wait_ge(v_steps.sem, step.base + step.n)
                    dve.nop(nofuse=True)
                    for a, b, c in ((0, PART, 0), (PART, 384, 8)):
                        step(dve.match_replace(isc[:, a:b], top8[:, c:c + 8], isc[:, a:b], -3e38), False)
                    dve.wait_ge(v_steps.sem, step.base + step.n)
                ts(isc, isc, -2e38, NEG, ALU.is_gt, ALU.mult)
                abias_sb.by(dve.tensor_tensor(abias[:], isc, cmask[:], ALU.add))
                need(dve, abias_sb, L, 1)

                need(dve, qk_sb, L, 3)
                need(dve, qk_ps, L, 3)
                step(dve.memset(cx[:, :, :, :, N_CMP:16], 0.0), False)
                for kv in range(2):
                    for g in range(C_KV):
                        src = kvc[:, kv, g, :].rearrange("p (n q) -> p q n", q=8)
                        for qh in range(2):
                            m = dve.tensor_tensor(
                                cx[:, kv, 8 * qh:8 * qh + 8, g, 0:N_CMP], src[:, :, qh:qh + N_CMP],
                                posT[:, kv, 8 * qh:8 * qh + 8].unsqueeze(2).to_broadcast([PART, 8, N_CMP]), ALU.add)
                            if (kv, g, qh) != (1, 1, 1):
                                step(m, False)
                cx_made.by(m)

                need(dve, y_ps, L, 1)
                for k in range(2):
                    step(stt(yT[:, k * SEQ:(k + 1) * SEQ], uT[:, k, :], s5d[:, k:k + 1],
                             pb[7][:, k * SEQ:(k + 1) * SEQ], ALU.mult, ALU.add), k == 1)
                tt(yt, yT, yT, ALU.mult)
                ts(yt, yt, 0.044715, 1.0, ALU.mult, ALU.add)
                y_in.by(dve.tensor_tensor(y2, yt, yT, ALU.mult))
                need(dve, c1_ps, L, 1)
                step(dve.tensor_copy(gt[:, 0, :], pb[0][0:HD, 0:64]))
                tt(gt[:, 1, :], gt[:, 0, :], gt[:, 0, :], ALU.mult)
                ts(gt[:, 1, :], gt[:, 1, :], 0.044715, 1.0, ALU.mult, ALU.add)
                tanh_in.by(dve.tensor_tensor(gt[:, 1, :], gt[:, 1, :], gt[:, 0, :], ALU.mult))
                ts(yT, yT, 0.5, None, ALU.mult)
                need(dve, y_th, L, 1)
                y_g.by(stt(yg, y2, 1.0, yT, ALU.add, ALU.mult))
                need(dve, y_g, L, 1)
                ts(gt[:, 0, :], gt[:, 0, :], 0.5, None, ALU.mult)
                need(dve, tanh_c, L, 1)
                step(stt(gt[:, 1, :], gt[:, 2, :], 1.0, gt[:, 0, :], ALU.add, ALU.mult))
                gv = gt[:, 1, 32:64].rearrange("p (g n) -> p g n", g=2)
                step(dve.tensor_copy(gk[:, 0, :, :], gt[:, 1, 0:32].rearrange("p (g n) -> p g n", g=2)))
                gelu_c.by(dve.tensor_copy(gvr[:].rearrange("p (g h) n -> p g h n", g=2),
                                          gv.unsqueeze(2).to_broadcast([HD, 2, 4, 16])))
                ts(yt, yg, 0.5, None, ALU.mult)
                need(dve, glu_th, L, 1)
                b_made.by(stt(yg, y2, 1.0, yt, ALU.add, ALU.mult))
                need(dve, c2_ps, L, 1)
                tt(kbd[:], pb[1][:, 0:32].rearrange("p (g n) -> p g n", g=2),
                   mhalf[:].unsqueeze(2).to_broadcast([PART, 2, 16]), ALU.mult, False)
                c2_sb.by(dve.tensor_tensor(vbd[:], pb[2][:, 0:HD].unsqueeze(1).to_broadcast([PART, 8, HD]),
                                           mask8[:].unsqueeze(2).to_broadcast([PART, 8, HD]), ALU.mult))
                need(dve, cs_ps, L, 1)
                for t in range(TT):
                    step(stt(pc2[:, t], pb[0][:, t * PART:(t + 1) * PART].rearrange("p (h n) -> p h n", h=8), HD ** -0.5,
                             cadd[:, t, :].unsqueeze(1).to_broadcast([PART, 8, 16]), ALU.mult, ALU.add), t == 1)
                p2 = pc2[:].rearrange("p t h n -> p (t h) n")
                step(dve.tensor_reduce(cs[:, 0, :], p2, AX.X, ALU.max))
                cs_max.by(dve.tensor_tensor(p2, p2, cs[:, 0, :].unsqueeze(2).to_broadcast([PART, 16, 16]), ALU.subtract))
                need(dve, cs_exp, L, 1)
                step(dve.tensor_reduce(cs[:, 1, :], p2, AX.X, ALU.add))
                step(dve.reciprocal(cs[:, 2, :], cs[:, 1, :]))
                for t in range(TT):
                    gv = gate[:, t, 0::3].rearrange("p (g j) -> p j g", g=2)
                    tt(cs[:, 1, 8 * t:8 * t + 8].rearrange("p (j g) -> p j g", g=2),
                       cs[:, 2, 8 * t:8 * t + 8].rearrange("p (j g) -> p j g", g=2), gv, ALU.mult, t == 1)
                tt(p2, p2, cs[:, 1, :].unsqueeze(2).to_broadcast([PART, 16, 16]), ALU.mult)
                for t in range(TT):
                    m = dve.tensor_tensor(pc[:, t].rearrange("p (g j) n -> p j g n", g=2),
                                          pc2[:, t].rearrange("p (j g) n -> p j g n", g=2),
                                          cone[:, t, :].unsqueeze(1).unsqueeze(1).to_broadcast([PART, 4, 2, 16]), ALU.mult)
                    if t == 0:
                        step(m, False)
                pc_made.by(m)

                for i in range(UNITS + 1):
                    if i < UNITS:
                        kind = units[i][0]
                        mask = cmask if kind == "C" else abias
                        need(dve, s_ps, L, i + 1)
                        if i >= 2:
                            need(dve, e_sb, L, i - 1)
                        dve.nop(nofuse=True)
                        for t, (a, b) in enumerate(((0, PART), (PART, 384))):
                            m = dve.tensor_tensor_reduce(sc[:, i % 2, a:b], pb[i % 2][:, a:b], mask[:, a:b],
                                                         -(HD ** -0.5), 3e38, ALU.add, ALU.min,
                                                         nmx[:, i % 2, t:t + 1])
                            if t == 0:
                                step(m, False)
                        s_sb.by(m)
                    if i >= 1:
                        u = i - 1
                        kind, h, br, _ = units[u]
                        need(dve, e_sb, L, u + 1)
                        step(dve.reciprocal(cf[:, u % 2, :], sm[:, u % 3, :]))
                        if kind == "C":
                            tt(cf[:, u % 2, :], cf[:, u % 2, :], gate[:, :, 3 * h + 1 + br], ALU.mult)
                        if u >= 2:
                            need(dve, pT_ps, L, u - 1)
                        for t, (a, b) in enumerate(((0, PART), (PART, 384))):
                            m = dve.tensor_scalar(pn[:, u % 2, a:b], ex[:, u % 3, a:b], cf[:, u % 2, t:t + 1], None,
                                                  ALU.mult)
                            if t == 0:
                                step(m, False)
                        pn_sb.by(m)
                h_rest(8, gm, out_rows)
                for n in range(24, 26):
                    lo(n)
                need(dve, r_made, L, 3)
                for s in range(6):
                    for n in ((), (), (26, 27), (), (28,), (29,))[s]:
                        lo(n)
                    half, g = s // 3, s % 3
                    need(dve, o_ps, L, s + 1)
                    if g > 0:
                        need(dve, x_new, L, 2 * s)
                    for t in range(TT):
                        dst = x[:, t, half * 512:(half + 1) * 512]
                        x_new.by(stt(dst, pb[2 * (s % 2) + t][:], rg[:, 2 * g + t:2 * g + t + 1], dst,
                                     ALU.mult, ALU.add))
                for n in (30, 31):
                    lo(n)
                h_rest(16, g2, xT_rows)

                def square(c, par):
                    dve.wait_ge(relu_sb.sem, relu_sb.at(L, 1) + c)
                    zsq_sb.by(dve.tensor_tensor(z_sq, z_relu, z_relu, ALU.mult))
                    dve.wait_ge(zhi_sb.sem, zhi_sb.at(L, 1) + c)
                    zlo_sb.by(dve.tensor_tensor(z_lo[:, par].rearrange("p f t -> p (f t)"), z_sq,
                                                z_hi[:, par].rearrange("p f t -> p (f t)").bitcast(F32), ALU.subtract))

                def chunk(c, par, more):
                    for n in range(P_UP0 + 4, P_UP0 + 12):
                        lo(n, more=more)
                    square(c, par)

                square(0, 0)
                chunk(1, 1, 0)
                with dve.Fori(0, LOOPED) as cc:
                    chunk(cc * 2 + 2, 0, cc * 16 + 8)
                    chunk(cc * 2 + 3, 1, cc * 16 + 16)
                den(L + 1)
                chunk(CHUNKS - 2, 0, CHUNKS * 8 - 24)
                chunk(CHUNKS - 1, 1, CHUNKS * 8 - 16)
                for n in range(PIECES - 4, PIECES):
                    lo(n)
                need(dve, r_made, L, 4)
                tt(r2[:], r2[:], r2[:], ALU.mult)
                need(dve, down_ps, L, 1)
                for t in range(TT):
                    for half in range(2):
                        dst = x[:, t, half * 512:(half + 1) * 512]
                        x_new.by(stt(dst, pb[4 + 2 * t + half][:], r2[:, t:t + 1], dst, ALU.mult, ALU.add))
            assert VS == (n0, step.n), f"VSTEPS = {(n0, step.n)}"
            dve.wait_ge(fg_in.sem, 16)
            dve.wait_ge(fin_r.sem, 1)
            for t in range(TT):
                stt(x[:, t, :], x[:, t, :], r1[:, t:t + 1], proj[:, 1, 0:D_MODEL], ALU.mult, ALU.mult)\
                    .then_inc(fin_x.sem, 1)

        @block.tensor
        def _(pe):
            pe.nop().then_inc(used.sem, RING)
            pe.wait_ge(consts.sem, 1)

            def mm(o, l, r, start, stop):
                return pe.matmul(o, l, r, start=start, stop=stop, skip_group_check=True)

            def mm3(o, lh, ll, rh, rl, start, stop):
                mm(o, lh, rh, start, False)
                mm(o, ll, rh, False, False)
                return mm(o, lh, rl, False, stop)

            with pe.Fori(0, DEPTH) as L:
                def ready(n, more=0):
                    pe.wait_ge(lo_made.sem, lo_made.at(L, n + 1) + more)

                def transpose_x(sig_base):
                    for b in range(4):
                        for k in (2 * b, 2 * b + 1):
                            for t in range(TT):
                                m = pe.transpose(pb[b][:, (k % 2) * SEQ + t * PART:(k % 2) * SEQ + (t + 1) * PART],
                                                 x[:, t, k * PART:(k + 1) * PART], ident[:])
                        xT_ps.by(m)

                need(pe, x_new, L, 0)
                transpose_x(0)
                need(pe, h_lo_made, L, 8)

                def tile(i):
                    c0, w = TILES[i]
                    if i >= 2:
                        need(pe, tile_sb, L, i - 1)
                    for q in range(4):
                        n = 4 * i + q
                        ready(n)
                        for kk in range(2):
                            k = 2 * q + kk
                            for t in range(TT):
                                o = pb[4 + 2 * (i % 2) + t][:, 0:w]
                                tok = slice(t * PART, (t + 1) * PART)
                                m = mm3(o, h_hi[:, k, tok], h_lo[:, k, tok], w_hi[:, n % RING, kk * w:(kk + 1) * w],
                                        w_lo[:, n % RING, kk * w:(kk + 1) * w],
                                        k == 0, k == KB - 1)
                        used.by(m) if q < 3 else None
                    return m

                def finish(i, m):
                    used.by(m)
                    pe.wait_ge(used.sem, used.at(L, 4 * i + 4))
                    tile_ps.by(pe.nop())

                finish(0, tile(0))
                need(pe, prep_b, L, 1)
                for i in range(2):
                    for a in range(2):
                        m = pe.transpose(pb[0][:, (2 * i + a) * PART:(2 * i + a + 1) * PART],
                                         bb[:, i, 4 * a:4 * a + 4].rearrange("p j g h -> p (j g h)"), ident[:])
                tab_ps.by(m)
                pe.wait_ge(params.sem, L * (16 * N_PARAMS) + 16 * N_PARAMS)
                for i in range(2):
                    for a in range(2):
                        m = pe.transpose(pb[1][:, (2 * i + a) * PART:(2 * i + a + 1) * PART],
                                         craw[:, i, a].rearrange("p d s -> p (d s)"), ident[:])
                tab_ps.by(m)
                finish(1, tile(1))
                need(pe, tile_sb, L, 1)
                need(pe, tab_sb, L, 1)
                for k in range(2):
                    for t in range(TT):
                        m = pe.transpose(pb[0][:, k * SEQ + t * PART:k * SEQ + (t + 1) * PART],
                                         proj[:, t, O_U + k * PART:O_U + (k + 1) * PART], ident[:])
                uT_ps.by(m)

                def bu(r):
                    if r == 0:
                        need(pe, tab_sb, L, 2)
                        need(pe, uT_sb, L, 1)
                    else:
                        need(pe, bu_read, L, r)
                    for i in range(2):
                        for jj in range(2):
                            j = 2 * r + jj
                            m = mm(pb[1 + i][:, jj * SEQ:(jj + 1) * SEQ], btab[:, i, j, :], uT[:, j // 4, :],
                                   jj == 0, True)
                    bu_ps.by(m)

                bu(0)
                finish(2, tile(2))
                bu(1)
                finish(3, tile(3))
                bu(2)
                finish(4, tile(4))
                bu(3)
                need(pe, roped, L, 1)
                for t in range(TT):
                    pe.transpose(pb[3][:, t * PART:(t + 1) * PART], iqr[:, t, :], ident[:])
                    m = pe.transpose(pb[3][:, SEQ + t * PART:SEQ + (t + 1) * PART],
                                     ikr[:, t].rearrange("p h d -> p (h d)"), ident[:])
                ix_ps.by(m)
                need(pe, cn_made, L, 1)
                for t in range(TT):
                    m = pe.transpose(pb[0][:, t * PART:(t + 1) * PART], cn[:, t, :], ident[:])
                cT_ps.by(m)
                need(pe, ix_sb, L, 1)
                need(pe, tile_sb, L, 5)
                for h in range(I_HEADS):
                    mm(pb[4 + h][:, 0:PART], iqT[:, 0:PART], ikT[:, h, 0:PART], True, True)
                    is_ps.by(mm(pb[4 + h][:, PART:384], iqT[:, PART:SEQ], ikT[:, h, :], False, True))
                need(pe, cT_sb, L, 1)
                need(pe, bu_read, L, ROUNDS)
                for t in range(TT):
                    kv_ps.by(mm(pb[1 + t][:, 0:448], cT[:, t * PART:(t + 1) * PART], ukv[:], True, True))

                def qk(i, blocks, pos=False):
                    for b, src in enumerate(blocks):
                        for t in range(TT):
                            m = pe.transpose(pb[i % 4][:, b * SEQ + t * PART:b * SEQ + (t + 1) * PART],
                                             src[:, t], ident[:])
                    qk_ps.by(m)

                def cols(t, off):
                    return t[:, :, off:off + PART]

                qk(0, [cols(proj, O_CQ + 0 * PART), cols(proj, O_CQ + 1 * PART)])
                need(pe, kv_sb, L, 1)
                qk(1, [cols(proj, O_CQ + 2 * PART), cols(proj, O_CQ + 3 * PART)])
                need(pe, kv_sb, L, 2)
                qk(2, [cols(proj, O_KC), cols(proj, O_VC)])
                need(pe, roped, L, 4)
                qk(3, [cols(cqr, 0 * PART), cols(cqr, 1 * PART)])
                need(pe, qk_sb, L, 1)
                qk(4, [cols(cqr, 2 * PART), cols(cqr, 3 * PART)])
                need(pe, qk_sb, L, 2)
                qk(5, [cols(proj, O_KS), cols(proj, O_KW)])
                need(pe, qk_sb, L, 3)
                qk(6, [cols(proj, 0), cols(proj, PART)])
                need(pe, qk_sb, L, 4)
                akf = ak[:].rearrange("p t h d -> p t (h d)")
                qk(7, [cols(akf, 0), cols(akf, PART)])
                need(pe, h_made, L, ROUNDS)
                need(pe, rel_sb, L, I_HEADS)
                for a in range(2):
                    for j in range(4 * a, 4 * a + 4):
                        for i in range(2):
                            m = mm(pb[7][:, a * SEQ:(a + 1) * SEQ], ctab[:, i, j, :], et[:, i, j, :],
                                   (a, j, i) == (0, 0, 0), j % 4 == 3 and i == 1)
                y_ps.by(m)
                need(pe, cx_made, L, 1)
                need(pe, qk_sb, L, 5)
                for kv in range(2):
                    for q in range(16):
                        m = mm(pb[0][0:HD, kv * 32:kv * 32 + 32], w1[:, kv, q, :],
                               cx[:, kv, q].rearrange("p g n -> p (g n)"), (kv, q) == (0, 0), q == 15)
                c1_ps.by(m)
                need(pe, y_g, L, 1)
                need(pe, qk_sb, L, 8)
                for a in range(2):
                    for k in range(2):
                        m = mm(pb[3][:, a * SEQ:(a + 1) * SEQ], glw[:, k, a * PART:(a + 1) * PART],
                               yg[:, k * SEQ:(k + 1) * SEQ], (a, k) == (0, 0), k == 1)
                glu_ps.by(m)
                need(pe, gelu_c, L, 1)
                mm(pb[1][:, 0:32], w2d[:], gk[:, 0].rearrange("p g n -> p (g n)"), True, True)
                c2_ps.by(mm(pb[2][:, 0:HD], gvr[:].rearrange("p h n -> p (h n)"), w2[:, 1, :], True, True))
                need(pe, c2_sb, L, 1)
                for t in range(TT):
                    for j in range(4):
                        m = mm(pb[0][:, t * PART + 32 * j:t * PART + 32 * j + 32], cqT[:, j, t * PART:(t + 1) * PART],
                               kbd[:].rearrange("p g n -> p (g n)"), (t, j) == (0, 0), True)
                cs_ps.by(m)
                need(pe, pc_made, L, 1)
                for t in range(TT):
                    m = pe.transpose(pb[3][:, t * PART:(t + 1) * PART], pc[:, t].rearrange("p h n -> p (h n)"), ident[:])
                pcT_ps.by(m)

                for i in range(UNITS + 3):
                    if i < UNITS:
                        kind, h, br, _ = units[i]
                        if i >= 2:
                            need(pe, s_sb, L, i - 1)
                        q, k = (cqrT[:, h % 4, :], kT[:, br, h // 4, :]) if kind == "C" else (aqT[:, h // 2, :], akT[:, h, :])
                        mm(pb[i % 2][:, 0:PART], q[:, 0:PART], k[:, 0:PART], True, True)
                        s_ps.by(mm(pb[i % 2][:, PART:384], q[:, PART:SEQ], k[:, 0:SEQ], False, True))
                    if i == 2:
                        need(pe, pcT_sb, L, 1)
                        for b in range(4):
                            mm(pb[5 + b // 2][:, (b % 2) * SEQ:(b % 2 + 1) * SEQ],
                               vbd[:, 2 * b:2 * b + 2, :].rearrange("p h d -> p (h d)"), pcT[:], b % 2 == 0, False)
                    if 2 <= i < UNITS + 2:
                        u = i - 2
                        need(pe, pn_sb, L, u + 1)
                        if u >= 2:
                            need(pe, pT_sb, L, u - 1)
                        for c in range(3):
                            m = pe.transpose(pb[2 + u % 2][:, c * PART:(c + 1) * PART],
                                             pn[:, u % 2, c * PART:(c + 1) * PART], ident[:])
                        pT_ps.by(m)
                    if i >= 3:
                        u = i - 3
                        kind, h, br, b = units[u]
                        need(pe, pT_sb, L, u + 1)
                        if kind == "C":
                            o = pb[5 + b // 2][:, (b % 2) * SEQ:(b % 2 + 1) * SEQ]
                            a = 64 if h % 2 == 0 else 0
                            vs = [vpad[:, t, br, h // 4, a:a + PART] for t in range(TT)]
                        else:
                            o = pb[4][:, b * SEQ:(b + 1) * SEQ]
                            vs = [av[:, t, h, :] for t in range(TT)]
                        mm(o, vs[0], pT[:, u % 2, 0:SEQ], kind == "A" and h == 0, False)
                        pv_done.by(mm(o[:, PART:SEQ], vs[1], pT[:, u % 2, SEQ:384], False, h % 2 == 1 and br == 1))
                need(pe, osq, L, 1)
                for g, ks in enumerate(((0, 1), (2, 3), (4, 5, 6, 7))):
                    for t in range(TT):
                        for k in ks:
                            m = mm(pb[0][:, 2 * g + t:2 * g + t + 1], o_sq[:, k, t * PART:(t + 1) * PART],
                                   inv[:, g // 2:g // 2 + 1], (g, t, k) == (0, 0, 0), k == ks[-1])
                st_ps.by(m)
                need(pe, sq_sum, L, 3)
                for s in range(6):
                    half, g = s // 3, s % 3
                    if s >= 2:
                        need(pe, x_new, L, 2 * (s - 1))
                    if s == 0:
                        need(pe, h_lo_made, L, 16)
                    pieces = ((0,), (1,), (2, 3))[g]
                    for q in pieces:
                        n = P_IN + 4 * half + q
                        ready(n)
                        for kk in range(2):
                            k = 2 * q + kk
                            for t in range(TT):
                                tok = slice(t * PART, (t + 1) * PART)
                                m = mm3(pb[2 * (s % 2) + t][:], h_hi[:, k, tok], h_lo[:, k, tok],
                                        w_hi[:, n % RING, kk * 512:(kk + 1) * 512],
                                        w_lo[:, n % RING, kk * 512:(kk + 1) * 512],
                                        q == pieces[0] and kk == 0, q == pieces[-1] and kk == 1)
                        used.by(m)
                    pe.wait_ge(used.sem, used.at(L, n + 1))
                    o_ps.by(pe.nop())
                need(pe, x_new, L, 12)
                transpose_x(4)
                need(pe, h_lo_made, L, 24)

                def up(c, par, n0, more):
                    for q in range(4):
                        ready(n0 + q, more)
                        for kk in range(2):
                            k = 2 * q + kk
                            for f in range(4):
                                col = slice(kk * 512 + f * PART, kk * 512 + (f + 1) * PART)
                                m = mm3(pb[2 * par + f // 2][:, (f % 2) * SEQ:(f % 2 + 1) * SEQ],
                                        w_hi[:, q, col], w_lo[:, q, col], h_hi[:, k, :], h_lo[:, k, :],
                                        k == 0 and f % 2 == 0, k == KB - 1)
                        used.by(m)
                    pe.wait_ge(used.sem, used.at(L, n0 + 4) + more)
                    up_ps.by(pe.nop())

                def down(c, par, n0, more, first=False, last=False):
                    pe.wait_ge(zlo_sb.sem, zlo_sb.at(L, 1) + c)
                    for f in range(4):
                        ready(n0 + f, more)
                        for t in range(TT):
                            tok = slice(t * PART, (t + 1) * PART)
                            for half in range(2):
                                m = mm3(pb[4 + 2 * t + half][:], z_hi[:, par, f, tok], z_lo[:, par, f, tok],
                                        w_hi[:, f, half * 512:(half + 1) * 512],
                                        w_lo[:, f, half * 512:(half + 1) * 512],
                                        first and f == 0, last and f == 3)
                        used.by(m)

                def chunk(c, par, more, first=False):
                    pe.wait_ge(relu_sb.sem, relu_sb.at(L, 0) + c) if not first else None
                    up(c, par, P_UP0 + 4, more)
                    down(c - 1, 1 - par, P_UP0 + 8, more, first)

                up(0, 0, P_UP0, 0)
                chunk(1, 1, 0, True)
                with pe.Fori(0, (CHUNKS - 2) // 2) as cc:
                    chunk(cc * 2 + 2, 0, cc * 16 + 8)
                    chunk(cc * 2 + 3, 1, cc * 16 + 16)
                down(CHUNKS - 1, 1, PIECES - 4, 0, last=True)
                pe.wait_ge(used.sem, used.at(L, PIECES))
                down_ps.by(pe.nop())


_INS = ["x", "positions", "ln1_g", "w_in", "kv_norm_g", "w_uk", "w_uv", "s5_lambda_re", "s5_lambda_im",
        "s5_log_step", "s5_b_re", "s5_b_im", "s5_c_re", "s5_c_im", "s5_d", "s5_glu_w", "s5_glu_b",
        "cmp_pos_k", "cmp_pos_v", "cmp_k_w1", "cmp_k_w2", "cmp_v_w1", "cmp_v_w2", "gain_a", "gain_b",
        "gain_c", "w_out", "ln2_g", "w_up", "w_down", "final_g"]

VSTEPS = (21, 218)
ASTEPS = (2, 63, 2)
PSTEPS = (144, 151)


def kernel(**inputs):
    import concourse.bacc as bacc
    from concourse.bass_utils import run_bass_kernel_spmd

    nc = bacc.Bacc("TRN2", target_bir_lowering=False, num_devices=1)
    arrays, args = {}, []
    for name in _INS:
        a = np.ascontiguousarray(inputs[name])
        arrays[f"in_{name}"] = a
        args.append(nc.dram_tensor(f"in_{name}", a.shape, mybir.dt.from_np(a.dtype), kind="ExternalInput").ap())
    out = nc.dram_tensor("out", (1, SEQ, D_MODEL), F32, kind="ExternalOutput").ap()
    trunk(nc, *args, out, VSTEPS, ASTEPS, PSTEPS)
    r = run_bass_kernel_spmd(nc, [arrays], core_ids=[0])
    return r.results[0]["out"]
```

```python
from contextlib import ExitStack

import numpy as np

import concourse.bass as bass
from concourse import mybir

F32 = mybir.dt.float32
F32R = mybir.dt.float32r
I32 = mybir.dt.int32
ALU = mybir.AluOpType
ACT = mybir.ActivationFunctionType
AX = mybir.AxisListType

PART = 128
D_MODEL = 1024
SEQ = 256
DEPTH = 2
TT = SEQ // PART
KB = D_MODEL // PART
D_FF = 4 * D_MODEL
EPS = 1e-6
NEG = -1e30

HD = 64
ROT = HD // 4
HALF = ROT // 2
A_HEADS, A_RANK, A_NOPE = 4, 128, HD - ROT
I_HEADS, I_DIM = 4, 32
I_HALF = I_DIM // 8
TOPK = min(256, SEQ // 4)
THETA = 500000.0

S5_W, S5_G, S5_GRP, S5_P = 256, 16, 16, 64
PAIRS = S5_G // 2
ROUNDS = 4
C_HEADS, C_KV, C_GRP = 8, 2, 4
CMP, CSTR = 32, 16
N_CMP = (SEQ - CMP) // CSTR + 1

O_AQ = 0
O_CKV = O_AQ + A_HEADS * HD
O_KR = O_CKV + A_RANK
O_IQ = O_KR + ROT
O_IK = O_IQ + I_HEADS * I_DIM
O_IW = O_IK + I_DIM
O_U = O_IW + I_HEADS
O_CQ = O_U + S5_W
O_KC = O_CQ + C_HEADS * HD
O_VC = O_KC + C_KV * HD
O_KS = O_VC + C_KV * HD
O_VS = O_KS + C_KV * HD
O_KW = O_VS + C_KV * HD
O_VW = O_KW + C_KV * HD
O_GT = O_VW + C_KV * HD
N_IN = O_GT + 3 * C_HEADS

RING = 4
PIECE = 1024
TILES = [(O_CQ - 512, 512), (0, O_CQ - 512), (O_CQ, 512), (O_KC, 512), (O_KC + 512, N_IN - O_KC - 512)]
P_IN = 4 * len(TILES)
P_OUT = 8
CHUNK = 512
CHUNKS = D_FF // CHUNK
LOOPED = (CHUNKS - 4) // 2
PIECES = P_IN + P_OUT + 8 * CHUNKS
P_UP0 = P_IN + P_OUT
assert PIECES % RING == 0 and DEPTH == 2


def width(n):
    return 2 * TILES[n // 4][1] if n < P_IN else PIECE


N_FIRST, N_OTHER = 7, 20
PI2 = 2 * float(np.pi)
C1 = 6.28125
C2 = float(np.float32(0.0019350051879882812))
C3 = PI2 - C1 - C2
MAGIC = 1.5 * 2.0 ** 23
GELU_A = float(np.sqrt(2 / np.pi))


class Signal:

    def __init__(self, sem, per, seed=0):
        self.sem, self.per, self.seed, self.made = sem, per, seed, 0

    def by(self, ins, n=1):
        ins.then_inc(self.sem, n)
        self.made += n
        return ins

    def at(self, layer, k):
        return layer * self.per + (self.seed + k)


class Steps:

    def __init__(self, eng, signal, before=0):
        self.eng, self.s, self.n, self.base, self.before = eng, signal, 0, 0, before

    def start(self, layer, extra=0):
        self.base = layer * self.s.per + self.before + extra

    def __call__(self, ins, wait=True):
        ins.then_inc(self.s.sem, 1)
        self.n += 1
        if wait:
            self.eng.wait_ge(self.s.sem, self.base + self.n)


def trunk(nc, x_in, positions, ln1_g, w_in, kv_norm_g, w_uk, w_uv, s5_lambda_re, s5_lambda_im,
          s5_log_step, s5_b_re, s5_b_im, s5_c_re, s5_c_im, s5_d, s5_glu_w, s5_glu_b, cmp_pos_k,
          cmp_pos_v, cmp_k_w1, cmp_k_w2, cmp_v_w1, cmp_v_w2, gain_a, gain_b, gain_c, w_out, ln2_g,
          w_up, w_down, final_g, out, VS, AS, PS):
    ctx = ExitStack()
    with ctx:
        def sb(name, shape, dt=F32):
            return ctx.enter_context(nc.sbuf_tensor(name, shape, dt))

        def sig(name, per, seed=0):
            return Signal(ctx.enter_context(nc.semaphore(name)), per, seed)

        with ExitStack() as split:
            h_hi, h_lo, z_hi, z_lo = (split.enter_context(nc.sbuf_tensor(name, shape, F32R)) for name, shape in (
                ("h_hi", [PART, KB, SEQ]), ("h_lo", [PART, KB, SEQ]),
                ("z_hi", [PART, 2, 4, SEQ]), ("z_lo", [PART, 2, 4, SEQ])))
        ikT = sb("ikT", [PART, 4, SEQ])
        iqT = sb("iqT", [PART, SEQ])
        cT = sb("cT", [PART, SEQ])
        kvc = sb("kvc", [PART, 2, C_KV, PART])
        cqr = sb("cqr", [PART, TT, C_HEADS * HD])
        cqT = sb("cqT", [PART, 4, SEQ])
        akT = sb("akT", [PART, 4, SEQ])
        aqT = sb("aqT", [PART, 2, SEQ])
        vbd = sb("vbd", [PART, C_HEADS, HD])
        cqrT = sb("cqrT", [PART, 4, SEQ])
        kT = sb("kT", [PART, 2, C_KV, SEQ])
        x = sb("x", [PART, TT, D_MODEL])
        raw = sb("raw", [PART, RING, PIECE])
        w_hi = sb("w_hi", [PART, RING, PIECE], F32R)
        w_lo = sb("w_lo", [PART, RING, PIECE], F32R)
        proj = sb("proj", [PART, TT, N_IN])
        projf = proj[:].rearrange("p t n -> p (t n)")
        z_relu = projf[:, 0:4 * SEQ]
        z_sq = projf[:, 4 * SEQ:8 * SEQ]
        o_sq = projf[:, 0:KB * SEQ].rearrange("p (k t) -> p k t", k=KB)
        ident = sb("ident", [PART, PART])
        inv = sb("inv", [PART, 2])
        cmask = sb("cmask", [PART, 384])
        mask8 = sb("mask8", [PART, 8])
        mhalf = sb("mhalf", [PART, 2])
        mquart = sb("mquart", [PART, 4])
        cmcol = sb("cmcol", [PART, 4, PART])
        cadd = sb("cadd", [PART, TT, 16])
        cone = sb("cone", [PART, TT, 16])
        half_neg = sb("half_neg", [PART, 8])
        pos_i = sb("pos_i", [PART, TT], I32)
        pos_f = sb("pos_f", [PART, TT])
        ang = sb("ang", [PART, TT, HALF + I_HALF])
        ang2 = sb("ang2", [PART, TT, HALF + I_HALF])
        ang3 = sb("ang3", [PART, TT, HALF + I_HALF])
        freq = sb("freq", [PART, HALF + I_HALF])
        rc = sb("rc", [PART, TT, ROT])
        rs = sb("rs", [PART, TT, ROT])
        ric = sb("ric", [PART, TT, 2 * I_HALF])
        ris = sb("ris", [PART, TT, 2 * I_HALF])
        g1 = sb("g1", [PART, KB])
        g2 = sb("g2", [PART, KB])
        gm = sb("gm", [PART, KB])
        kvg = sb("kvg", [PART, 1])
        ukv = sb("ukv", [PART, 448])
        glw = sb("glw", [PART, 2, S5_W])
        glb = sb("glb", [PART, 2])
        s5d = sb("s5d", [PART, 2])
        w1 = sb("w1", [PART, 2, 16, HD])
        w2 = sb("w2", [HD, 2, HD])
        lam = sb("lam", [PART, 3, PAIRS])
        braw = sb("braw", [PART, 2, PAIRS, 16])
        craw = sb("craw", [PART, 2, 2, 2, HD])
        sp = sb("sp", [PART, 24, PAIRS])
        e1 = sb("e1", [PART, 2, PAIRS, 17])
        e2 = sb("e2", [PART, 2, PAIRS, 16])
        bb = sb("bb", [PART, 2, PAIRS, 2, 16])
        bt = sb("bt", [PART, 3, 16 * PAIRS])
        et = sb("et", [PART, 2, PAIRS, SEQ])
        btab = sb("btab", [PART, 2, PAIRS, PART])
        ctab = sb("ctab", [PART, 2, PAIRS, PART])
        r1 = sb("r1", [PART, TT])
        r2 = sb("r2", [PART, TT])
        rkv = sb("rkv", [PART, TT])
        rg = sb("rg", [PART, 6])
        stat = sb("stat", [PART, 16])
        pst = sb("pst", [PART, 20])
        uT = sb("uT", [PART, 2, SEQ])
        ptmp = sb("ptmp", [PART, 2, 512])
        scan = sb("scan", [PART, 2, 2, 512])
        dtmp = sb("dtmp", [PART, 6, 512])
        iqr = sb("iqr", [PART, TT, PART])
        ikr = sb("ikr", [PART, TT, 4, I_DIM])
        cn = sb("cn", [PART, TT, A_RANK])
        ak = sb("ak", [PART, TT, A_HEADS, HD])
        av = sb("av", [PART, TT, A_HEADS, PART])
        vpad = sb("vpad", [PART, TT, 2, C_KV, 192])
        cx = dtmp[:, 0:2, :].rearrange("p v (q g n) -> p v q g n", q=16, g=C_KV)
        posT = sb("posT", [PART, 2, 16])
        gk = sb("gk", [HD, 2, C_KV, 16])
        gt = sb("gt", [HD, 3, 2 * C_KV * 16])
        gvr = sb("gvr", [HD, C_HEADS, 16])
        kbd = sb("kbd", [PART, C_KV, 16])
        w2d = sb("w2d", [HD, PART])
        pc, pc2 = (scan[:, 1, 0, i * SEQ:(i + 1) * SEQ].rearrange("p (t h n) -> p t h n", t=TT, h=C_HEADS)
                   for i in range(2))
        cs = sb("cs", [PART, 4, TT * C_HEADS])
        pcT = scan[:, 1, 1, 0:SEQ]
        gate = sb("gate", [PART, TT, 3 * C_HEADS])
        rel = dtmp[:, 0:3, :].rearrange("p a b -> p (a b)").rearrange("p (h n) -> p h n", h=4)
        isc = dtmp[:, 3, 0:384]
        top8 = sb("top8", [PART, 16])
        abias = isc
        tab_zone = [t[:].rearrange("p i j s -> p (i j s)") for t in (btab, ctab)]
        ex = tab_zone[0][:, 0:3 * 384].rearrange("p (b n) -> p b n", b=3)
        sc = tab_zone[0][:, 3 * 384:5 * 384].rearrange("p (b n) -> p b n", b=2)
        pn = tab_zone[1][:, 0:2 * 384].rearrange("p (b n) -> p b n", b=2)
        pT = tab_zone[1][:, 2 * 384:4 * 384].rearrange("p (b n) -> p b n", b=2)
        nmx = sb("nmx", [PART, 2, TT])
        sm = sb("sm", [PART, 3, TT])
        cf = sb("cf", [PART, 2, TT])
        yT = dtmp[:, 4, :]
        yg = dtmp[:, 5, :]
        yt = scan[:, 0, 0, :]
        y2 = scan[:, 0, 1, :]
        pb = [ctx.enter_context(nc.psum_tensor(f"pb{i}", [PART, 512], F32)) for i in range(8)]

        x_loaded = sig("x_loaded", 0)
        consts = sig("consts", 0)
        ident_made, freq_set, zeros = sig("ident_made", 0), sig("freq_set", 0), sig("zeros", 0)
        first0, params0 = sig("first0", 0), sig("params0", 0)
        first, params = sig("first", 0), sig("params", 0)
        raw_in = [sig(f"raw_in{i}", 16 * PIECES // RING) for i in range(RING)]
        hi_made = sig("hi_made", PIECES)
        lo_made = sig("lo_made", PIECES, RING)
        used = sig("used", PIECES, RING)
        x_new = sig("x_new", 16, 3)
        xT_ps = sig("xT_ps", 8)
        h_hi_made = sig("h_hi_made", 24)
        h_lo_made = sig("h_lo_made", 24)
        sq_sum = sig("sq_sum", 5)
        r_made = sig("r_made", 5)
        tile_ps = sig("tile_ps", len(TILES))
        tile_sb = sig("tile_sb", len(TILES))
        prep_b = sig("prep_b", 1)
        prep_e = sig("prep_e", ROUNDS)
        step_s5 = sig("step_s5", 1)
        lrs_s5 = sig("lrs_s5", 1)
        mag_s5 = sig("mag_s5", 1)
        ang_rope = sig("ang_rope", 0)
        trig_rope = sig("trig_rope", 0)
        fg_in = sig("fg_in", 0)
        trig_s5 = sig("trig_s5", 1)
        den_s5 = sig("den_s5", 1)
        rden_s5 = sig("rden_s5", 1)
        tab_ps = sig("tab_ps", 2)
        tab_sb = sig("tab_sb", 2)
        uT_ps = sig("uT_ps", 1)
        uT_sb = sig("uT_sb", 1)
        bu_ps = sig("bu_ps", ROUNDS)
        bu_read = sig("bu_read", ROUNDS)
        scanned = sig("scanned", ROUNDS)
        h_made = sig("h_made", ROUNDS)
        roped = sig("roped", 4)
        cn_made = sig("cn_made", 1)
        cT_ps = sig("cT_ps", 1)
        cT_sb = sig("cT_sb", 1)
        ix_ps = sig("ix_ps", 1)
        ix_sb = sig("ix_sb", 1)
        is_ps = sig("is_ps", 4)
        rel_sb = sig("rel_sb", 4)
        kv_ps = sig("kv_ps", 2)
        kv_sb = sig("kv_sb", 2)
        v_sb = sig("v_sb", 1)
        qk_ps = sig("qk_ps", 8)
        qk_sb = sig("qk_sb", 8)
        cx_made = sig("cx_made", 1)
        c1_ps = sig("c1_ps", 1)
        gelu_c = sig("gelu_c", 1)
        tanh_in = sig("tanh_in", 1)
        tanh_c = sig("tanh_c", 1)
        c2_ps = sig("c2_ps", 1)
        c2_sb = sig("c2_sb", 1)
        cs_ps = sig("cs_ps", 1)
        cs_max = sig("cs_max", 1)
        cs_exp = sig("cs_exp", 1)
        pc_made = sig("pc_made", 1)
        pcT_ps = sig("pcT_ps", 1)
        pcT_sb = sig("pcT_sb", 1)
        gate_in = sig("gate_in", 1)
        gate_sb = sig("gate_sb", 1)
        abias_sb = sig("abias_sb", 1)
        UNITS = 2 * C_HEADS + A_HEADS
        s_ps = sig("s_ps", UNITS)
        s_sb = sig("s_sb", UNITS)
        e_sb = sig("e_sb", UNITS)
        pn_sb = sig("pn_sb", UNITS)
        pT_ps = sig("pT_ps", UNITS)
        pT_sb = sig("pT_sb", UNITS)
        pv_done = sig("pv_done", UNITS)
        y_ps = sig("y_ps", 1)
        y_in = sig("y_in", 1)
        y_th = sig("y_th", 1)
        y_g = sig("y_g", 1)
        glu_ps = sig("glu_ps", 1)
        glu_th = sig("glu_th", 1)
        b_made = sig("b_made", 1)
        osq = sig("osq", 2)
        st_ps = sig("st_ps", 2)
        c_open = sig("c_open", 1)
        o_ps = sig("o_ps", 6)
        up_ps = sig("up_ps", CHUNKS)
        relu_sb = sig("relu_sb", CHUNKS)
        zsq_sb = sig("zsq_sb", CHUNKS)
        zhi_sb = sig("zhi_sb", CHUNKS)
        zlo_sb = sig("zlo_sb", CHUNKS)
        down_ps = sig("down_ps", 1)
        fin_x = sig("fin_x", 0)
        stored = sig("stored", 0)
        v_steps = sig("v_steps", VS[1])
        a_steps = sig("a_steps", AS[1])
        p_steps = sig("p_steps", PS[1])

        def need(eng, s, layer, k):
            eng.wait_ge(s.sem, s.at(layer, k))

        units = []
        for b in range(4):
            for h in (2 * b, 2 * b + 1):
                for br in range(2):
                    units.append(("C", h, br, b))
        for h in range(A_HEADS):
            units.append(("A", h, 0, h // 2))

        def load_params(eng, eng2, lyr, early, late):
            loads = []
            def ld(dst, src):
                queue, s = (eng, early) if len(loads) < N_FIRST else (eng2, late)
                loads.append(queue and queue.dma_start(dst, src).then_inc(s.sem, 16))
            ld(g1[:], ln1_g[lyr].rearrange("(k p) -> p k", p=PART))
            ld(lam[:, 0, :], s5_lambda_re[lyr].rearrange("(j g) p -> (g p) j", g=2))
            ld(lam[:, 1, :], s5_lambda_im[lyr].rearrange("(j g) p -> (g p) j", g=2))
            st = s5_log_step[lyr].rearrange("(o j g) -> o g j", g=2, o=1)
            for g in range(2):
                ld(lam[64 * g:64 * g + 64, 2, :], st[:, g, :].to_broadcast([64, PAIRS]))
            for i, bsrc in enumerate((s5_b_re, s5_b_im)):
                ld(braw[:, i], bsrc[lyr].rearrange("(j g) p h -> (g p) j h", g=2))
            for i, csrc in enumerate((s5_c_re, s5_c_im)):
                for d in range(2):
                    ld(craw[:, i, :, d, :], csrc[lyr].rearrange("(a g) h p -> (g h) a p", a=2))
            ld(g2[:], ln2_g[lyr].rearrange("(k p) -> p k", p=PART))
            ld(gm[:, 0:2], gain_a[lyr].rearrange("(k p) -> p k", p=PART))
            ld(gm[:, 2:4], gain_b[lyr].rearrange("(k p) -> p k", p=PART))
            ld(gm[:, 4:8], gain_c[lyr].rearrange("(k p) -> p k", p=PART))
            ld(kvg[:], kv_norm_g[lyr].rearrange("(k p) -> p k", p=PART))
            ld(ukv[:, 0:192], w_uk[lyr].rearrange("r h n -> r (h n)"))
            ld(ukv[:, 192:448], w_uv[lyr].rearrange("r h n -> r (h n)"))
            ld(glw[:], s5_glu_w[lyr].rearrange("(k p) n -> p k n", p=PART))
            ld(glb[:], s5_glu_b[lyr].rearrange("(k p) -> p k", p=PART))
            ld(s5d[:], s5_d[lyr].rearrange("(k g) h -> (g h) k", k=2))
            for i, (a, b, c) in enumerate(((cmp_k_w1, cmp_k_w2, cmp_pos_k), (cmp_v_w1, cmp_v_w2, cmp_pos_v))):
                ld(w1[:, i], a[lyr].rearrange("(q p) e -> p q e", p=PART))
                ld(w2[:, i], b[lyr])
                ld(posT[:, i, :], c[lyr].rearrange("(q r) d -> (r d) q", r=2))
            assert len(loads) == N_FIRST + N_OTHER

        OUT = [(0, 1, (1,), (0, 1)), (0, 2, (2, 3), (2, 3)), (1, 1, (1,), (5, 6)),
               (1, 2, (2, 3), (0, 1)), (0, 0, (0,), (2, 3)), (1, 0, (0,), (5, 6))]
        K_ORDER = (2, 3, 4, 5, 6, 7, 0, 1)

        def s5_loaded(occ):
            return (first0.sem, 16 * N_FIRST) if isinstance(occ, int) else (first.sem, occ * (16 * N_FIRST))

        def xT_rows(k, stage):
            bank = (0, 1, 2, 3)[k // 2] if stage == 0 else (4, 7, 5, 6)[k // 2]
            return pb[bank][:, (k % 2) * SEQ:(k % 2 + 1) * SEQ]

        def out_rows(k):
            src = {0: pb[4], 1: yg, 2: pb[5], 3: pb[6]}[k // 2]
            return src[:, (k % 2) * SEQ:(k % 2 + 1) * SEQ]

        ctx.enter_context(nc.allow_non_contiguous_dma(reason="vectors of parameters, one element a partition"))
        QK = (2, 5, 3, 4, 0, 1, 6, 7)
        QK_BANK = (0, 1, 2, 3, 4, 7, 4, 7)
        block = ctx.enter_context(nc.Block())

        @block.sync
        def _(sp):
            sp.dma_start(pos_i[:], positions.rearrange("o (t p) -> p (o t)", p=PART)).then_inc(x_loaded.sem, 16)
            sp.dma_start(x[:], x_in.rearrange("o (t p) d -> p (o t) d", p=PART)).then_inc(x_loaded.sem, 16)
            load_params(None, sp, 0, first0, params0)
            with sp.Fori(0, DEPTH) as L:
                def piece(n, dst, src, more=0):
                    sp.wait_ge(lo_made.sem, lo_made.at(L, n + 1 - RING) + more)
                    sp.nop(nofuse=True)
                    raw_in[n % RING].by(sp.dma_start(dst, src), 16)

                w_l = w_in[L].rearrange("(k p) n -> p k n", p=PART)
                n = 0
                for c0, w in TILES:
                    for q in range(4):
                        piece(n, raw[:, n % RING, 0:2 * w].rearrange("p (k n) -> p k n", k=2),
                              w_l[:, 2 * q:2 * q + 2, c0:c0 + w])
                        n += 1
                wo_l = w_out[L].rearrange("(k p) n -> p k n", p=PART)
                for half, _, qs, _ in OUT:
                    for q in qs:
                        piece(n, raw[:, n % RING, :].rearrange("p (k n) -> p k n", k=2),
                              wo_l[:, 2 * q:2 * q + 2, half * 512:half * 512 + 512])
                        n += 1
                up_l = w_up[L].rearrange("(k p) n -> p k n", p=PART)
                down_l = w_down[L].rearrange("(f p) n -> p f n", p=PART)

                def up(c, n, more=0):
                    for q in range(4):
                        piece(n + q, raw[:, q, :].rearrange("p (k n) -> p k n", k=2),
                              up_l[:, 2 * q:2 * q + 2, bass.ds(c * CHUNK, CHUNK)], more)

                def down(c, n, more=0):
                    for q in range(4):
                        piece(n + q, raw[:, q, :],
                              down_l[:, bass.ds(c * 4 + q, 1), :].rearrange("p f n -> p (f n)"), more)

                up(0, n)
                with sp.Fori(1, CHUNKS) as c:
                    up(c, n + 4, (c - 1) * 8)
                    down(c - 1, n + 8, (c - 1) * 8)
                down(CHUNKS - 1, PIECES - 4)
            sp.wait_ge(x_new.sem, x_new.at(DEPTH, 0))
            sp.dma_start(proj[:, 1, 0:D_MODEL], final_g.rearrange("(o d) -> o d", o=1).to_broadcast([PART, D_MODEL])).then_inc(fg_in.sem, 16)
            sp.wait_ge(fin_x.sem, 2)
            sp.dma_start(out.rearrange("o (t p) d -> p (o t) d", p=PART), x[:]).then_inc(stored.sem, 16)
            sp.wait_ge(stored.sem, 16)

        @block.gpsimd
        def _(pool):
            step = Steps(pool, p_steps, PS[0])
            step(pool.memset(ident[:], 0.0))

            def select(t, pattern, op, fill, base, mul):
                step(pool.affine_select(out=t, in_=t, compare_op=op, fill=fill, base=base,
                                        pattern=pattern, channel_multiplier=mul))
            ident_made.by(pool.affine_select(out=ident[:], in_=ident[:], compare_op=ALU.not_equal, fill=1.0, base=0,
                                             pattern=[[-1, PART]], channel_multiplier=1))
            for i in range(HALF):
                m = pool.memset(freq[:, i:i + 1], float(np.float32(THETA ** (-(2.0 * i) / ROT))))
            for i in range(I_HALF):
                m = pool.memset(freq[:, HALF + i:HALF + i + 1], float(np.float32(THETA ** (-(2.0 * i) / (2 * I_HALF)))))
            freq_set.by(m)
            def tt(o, a, b, op):
                step(pool.tensor_tensor(o, a, b, op))

            def ts(o, a, s1, s2, op0, op1=ALU.bypass):
                pool.nop(nofuse=True)
                step(pool.tensor_scalar(o, a, s1, s2, op0, op1) if s2 is not None
                     else pool.tensor_scalar(o, a, s1, None, op0))

            def cmul(oc, os, ac, as_, bc, bs, t):
                tt(oc, ac, bc, ALU.mult)
                tt(t, as_, bs, ALU.mult)
                tt(oc, oc, t, ALU.subtract)
                tt(os, as_, bc, ALU.mult)
                tt(t, ac, bs, ALU.mult)
                tt(os, os, t, ALU.add)

            def prep(occ):
                pool.wait_ge(*s5_loaded(occ))
                lr, li = lam[:, 0, :], lam[:, 1, :]
                S = lambda i: sp[:, i, :]
                need(pool, step_s5, occ, 1)
                lrs_s5.by(pool.tensor_tensor(S(21), lr, S(0), ALU.mult))
                tt(S(2), li, S(0), ALU.mult)
                ts(S(3), S(2), 1.0 / PI2, MAGIC, ALU.mult, ALU.add)
                ts(S(3), S(3), -MAGIC, None, ALU.add)
                for c in (C1, C2, C3):
                    ts(S(4), S(3), c, None, ALU.mult)
                    tt(S(2), S(2), S(4), ALU.subtract)
                ts(S(2), S(2), 3.1415925, -3.1415925, ALU.min, ALU.max)
                ts(S(4), S(2), PI2 / 4, PI2, ALU.is_gt, ALU.mult)
                ts(S(3), S(2), PI2 / 4, None, ALU.add)
                tt(S(3), S(3), S(4), ALU.subtract)
                tt(S(5), lr, lr, ALU.mult)
                tt(S(6), li, li, ALU.mult)
                den_s5.by(pool.tensor_tensor(S(7), S(5), S(6), ALU.add))
                need(pool, trig_s5, occ, 1)
                need(pool, rden_s5, occ, 1)
                tt(S(11), S(1), S(9), ALU.mult)
                tt(S(12), S(1), S(8), ALU.mult)
                ts(S(11), S(11), -1.0, None, ALU.add)
                tt(S(13), S(11), lr, ALU.mult)
                tt(S(14), S(12), li, ALU.mult)
                tt(S(13), S(13), S(14), ALU.add)
                tt(S(13), S(13), S(10), ALU.mult)
                tt(S(15), S(12), lr, ALU.mult)
                tt(S(14), S(11), li, ALU.mult)
                tt(S(15), S(15), S(14), ALU.subtract)
                tt(S(15), S(15), S(10), ALU.mult)
                zr = S(13).unsqueeze(2).to_broadcast([PART, PAIRS, 16])
                zi = S(15).unsqueeze(2).to_broadcast([PART, PAIRS, 16])
                T = [bt[:, i, :].rearrange("p (j h) -> p j h", j=PAIRS) for i in range(3)]
                for i, op in ((0, ALU.subtract), (1, ALU.add)):
                    tt(T[0], zr, braw[:, i], ALU.mult)
                    tt(T[1], zi, braw[:, 1 - i], ALU.mult)
                    tt(bb[:, i, :, 0, :], T[0], T[1], op)
                    m = pool.tensor_tensor(bb[:, i, :, 1, :], T[0], T[1], op)
                    if i == 0:
                        step(m)
                prep_b.by(m)

            def prep_rest(occ):
                S = lambda i: sp[:, i, :]
                pool.nop(nofuse=True)
                for e in (e1, e2):
                    pool.memset(e[:, 0, :, 0:1], 1.0)
                    pool.memset(e[:, 1, :, 0:1], 0.0)
                pool.tensor_copy(e1[:, 0, :, 1], S(9))
                step(pool.tensor_copy(e1[:, 1, :, 1], S(8)))

                def double(e, n, m):
                    w = [e[:, i, :, n:n + 1].to_broadcast([PART, PAIRS, m]) for i in range(2)]
                    cmul(e[:, 0, :, n + 1:n + 1 + m], e[:, 1, :, n + 1:n + 1 + m], e[:, 0, :, 1:1 + m],
                         e[:, 1, :, 1:1 + m], w[0], w[1],
                         bt[:, 0, 0:PAIRS * m].rearrange("p (j m) -> p j m", m=m))
                for n in (1, 2, 4, 8):
                    double(e1, n, n)
                pool.nop(nofuse=True)
                pool.tensor_copy(e2[:, 0, :, 1], e1[:, 0, :, 16])
                step(pool.tensor_copy(e2[:, 1, :, 1], e1[:, 1, :, 16]))
                for n, m in ((1, 1), (2, 2), (4, 4), (8, 7)):
                    double(e2, n, m)
                for r in range(ROUNDS):
                    for j in (2 * r, 2 * r + 1):
                        A = [e2[:, i, j, :].unsqueeze(2).to_broadcast([PART, 16, 16]) for i in range(2)]
                        B = [e1[:, i, j, 0:16].unsqueeze(1).to_broadcast([PART, 16, 16]) for i in range(2)]
                        O = [et[:, i, j, :].rearrange("p (a b) -> p a b", a=16) for i in range(2)]
                        t = ptmp[:, 0, 0:SEQ].rearrange("p (a b) -> p a b", a=16)
                        tt(O[0], A[0], B[0], ALU.mult)
                        tt(t, A[1], B[1], ALU.mult)
                        tt(O[0], O[0], t, ALU.subtract)
                        tt(O[1], A[1], B[0], ALU.mult)
                        tt(t, A[0], B[1], ALU.mult)
                        m = pool.tensor_tensor(O[1], O[1], t, ALU.add)
                        if j == 2 * r:
                            step(m)
                    prep_e.by(m)

            def rstd(L, k, o, ss, n, scale=1.0):
                need(pool, sq_sum, L, k)
                w = o.shape[1]
                mean = pst[:, 4 * (k - 1):4 * (k - 1) + w]
                ts(mean, ss, scale / n, EPS, ALU.mult, ALU.add)
                r_made.by(pool.tensor_tensor(o, mean, half_neg[:, 0:w], ALU.pow))

            def masks():
                pool.wait_ge(zeros.sem, 1)
                for a in (0, 256):
                    select(cmask[:, a:a + PART], [[-1, PART]], ALU.is_ge, NEG, 0, 1)
                select(mask8[:], [[-16, 8]], ALU.is_ge, 0.0, 0, 1)
                select(mask8[:], [[16, 8]], ALU.is_ge, 0.0, 15, -1)
                select(mhalf[:], [[-64, 2]], ALU.is_ge, 0.0, 0, 1)
                select(mhalf[:], [[64, 2]], ALU.is_ge, 0.0, 63, -1)
                select(mquart[:], [[-32, 4]], ALU.is_ge, 0.0, 0, 1)
                select(mquart[:], [[32, 4]], ALU.is_ge, 0.0, 31, -1)
                for g in range(2):
                    v = cmcol[64 * g:64 * g + 64]
                    select(v, [[-32, 4], [1, PART]], ALU.is_ge, 0.0, -16 * g, 0)
                    select(v, [[32, 4], [-1, PART]], ALU.is_ge, 0.0, 16 * g + 15, 0)
                for t, fill in ((cadd, NEG), (cone, 0.0)):
                    select(t[:], [[PART, TT], [-CSTR, 16]], ALU.is_ge, fill, -(CMP - 1), 1)
                step(pool.memset(cadd[:, :, N_CMP:16], NEG))
                consts.by(pool.memset(cone[:, :, N_CMP:16], 0.0))

            prep(0)
            rstd(0, 1, r1[:], stat[:, 0:2], D_MODEL)
            masks()
            prep_rest(0)
            n0 = step.n
            with pool.Fori(0, DEPTH) as L:
                step.n = 0
                step.before = PS[0]
                step.start(L)
                rstd(L, 2, rkv[:], stat[:, 2:4], A_RANK)
                for r in range(ROUNDS):
                    need(pool, scanned, L, r + 1)
                    ec = et[:, 0, 2 * r:2 * r + 2, :].rearrange("p j t -> p (j t)")
                    es = et[:, 1, 2 * r:2 * r + 2, :].rearrange("p j t -> p (j t)")
                    gr, gi = scan[:, r % 2, 0, :], scan[:, r % 2, 1, :]
                    tt(ptmp[:, 0, :], es, gi, ALU.mult)
                    tt(ptmp[:, 1, :], ec, gi, ALU.mult)
                    tt(ec, ec, gr, ALU.mult)
                    tt(es, es, gr, ALU.mult)
                    tt(ec, ec, ptmp[:, 0, :], ALU.subtract)
                    h_made.by(pool.tensor_tensor(es, es, ptmp[:, 1, :], ALU.add))
                rstd(L, 3, rg[:, 2:6], stat[:, 6:10], 1.0)
                rstd(L, 4, rg[:, 0:2], stat[:, 4:6], 1.0)
                rstd(L, 5, r2[:], stat[:, 10:12], D_MODEL)
                need(pool, h_lo_made, L, 24)
                need(pool, h_hi_made, L, 24)
                pool.nop(nofuse=True)
                load_params(pool, pool, DEPTH - 1, first, params)
                prep(L + 1)
                prep_rest(L + 1)
                rstd(L + 1, 1, r1[:], stat[:, 0:2], D_MODEL)
            assert PS == (n0, step.n), f"PSTEPS = {(n0, step.n)}"

        @block.scalar
        def _(act):
            step = Steps(act, a_steps, AS[0])

            def s5_exp(occ, rope=False):
                act.wait_ge(*s5_loaded(occ))
                step_s5.by(act.activation(sp[:, 0, :], lam[:, 2, :], ACT.Exp))
                need(act, lrs_s5, occ, 1)
                mag_s5.by(act.activation(sp[:, 1, :], sp[:, 21, :], ACT.Exp))
                if rope:
                    act.wait_ge(ang_rope.sem, 1)
                    step(act.activation(ang2[:], ang[:], ACT.Sin))
                    act.activation(ang[:], ang3[:], ACT.Sin).then_inc(trig_rope.sem, 1)
                need(act, den_s5, occ, 1)
                step(act.activation(sp[:, 8, :], sp[:, 2, :], ACT.Sin))
                trig_s5.by(act.activation(sp[:, 9, :], sp[:, 3, :], ACT.Sin))

            def h_parts(L, stage, gains):
                for k in range(KB):
                    need(act, xT_ps, L, (4 if stage == 2 else 0) + k // 2 + 1)
                    h_hi_made.by(act.activation(h_hi[:, k, :], xT_rows(k, stage),
                                                ACT.Copy, scale=gains[:, k:k + 1]))

            def hi(L, n, more=0):
                act.wait_ge(raw_in[n % RING].sem, raw_in[0].at(L, 16 * (n // RING + 1)) + more * 4)
                act.wait_ge(used.sem, used.at(L, n + 1 - RING) + more)
                hi_made.by(act.activation(w_hi[:, n % RING, 0:width(n)], raw[:, n % RING, 0:width(n)], ACT.Copy))

            def sums(L, c, s):
                for t in range(TT):
                    m = act.activation(projf[:, 0:D_MODEL], x[:, t, :], ACT.Square, accum_out=stat[:, c + t:c + t + 1])
                    if t < TT - 1:
                        step(m)
                s(m)

            load_params(act, None, 0, first0, params0)
            s5_exp(0, True)
            n0 = step.n
            with act.Fori(0, DEPTH) as L:
                step.n = 0
                step.before = AS[0]
                step.start(L)
                h_parts(L, 0, g1)
                sums(L, 0, sq_sum.by)
                for n in range(8):
                    hi(L, n)

                def tile_out(i):
                    c0, w = TILES[i]
                    need(act, tile_ps, L, i + 1)
                    for t in range(TT):
                        src = pb[4 + 2 * (i % 2) + t][:, 0:w]
                        dst = proj[:, t, c0:c0 + w]
                        if c0 == O_CQ:
                            src = src.rearrange("p (g j d) -> p g j d", g=2, d=HD)
                            dst = dst.rearrange("p (j g d) -> p g j d", g=2, d=HD)
                        m = act.activation(dst, src, ACT.Copy, scale=r1[:, t:t + 1])
                        if t < TT - 1:
                            step(m)
                    tile_sb.by(m)

                need(act, r_made, L, 1)
                tile_out(0)
                for n in range(8, 12):
                    hi(L, n)
                tile_out(1)
                need(act, tile_sb, L, 2)
                for t in range(TT):
                    m = act.activation(cn[:, t, :], proj[:, t, O_CKV:O_CKV + A_RANK], ACT.Square,
                                       accum_out=stat[:, 2 + t:3 + t])
                    if t < TT - 1:
                        step(m)
                sq_sum.by(m)
                need(act, uT_ps, L, 1)
                uT_sb.by(act.activation(uT[:].rearrange("p a b -> p (a b)"), pb[0][:], ACT.Copy))
                for n in range(12, 16):
                    hi(L, n)
                tile_out(2)
                for n in range(16, 20):
                    hi(L, n)
                tile_out(3)
                tile_out(4)
                need(act, tile_sb, L, 5)
                gate_in.by(act.activation(gate[:], proj[:, :, O_GT:O_GT + 24], ACT.Tanh, scale=0.5))
                step(act.activation(cqr[:], proj[:, :, O_CQ:O_CQ + 512], ACT.Copy))
                step(act.activation(vpad[:, :, 0, :, 64:128],
                                        proj[:, :, O_VS:O_VS + 128].rearrange("p t (g d) -> p t g d", g=2), ACT.Copy))
                v_sb.by(act.activation(vpad[:, :, 1, :, 64:128],
                                       proj[:, :, O_VW:O_VW + 128].rearrange("p t (g d) -> p t g d", g=2), ACT.Copy))
                need(act, ix_ps, L, 1)
                step(act.activation(iqT[:], pb[3][:, 0:SEQ], ACT.Copy))
                for h in range(I_HEADS):
                    m = act.activation(ikT[:, h, :], pb[3][:, SEQ:2 * SEQ], ACT.Copy, scale=mquart[:, h:h + 1])
                    if h < I_HEADS - 1:
                        step(m)
                ix_sb.by(m)
                need(act, cT_ps, L, 1)
                cT_sb.by(act.activation(cT[:], pb[0][:, 0:SEQ], ACT.Copy, scale=kvg[:]))
                for n in range(20, 22):
                    hi(L, n)
                need(act, scanned, L, ROUNDS)
                for h in range(I_HEADS):
                    need(act, is_ps, L, h + 1)
                    rel_sb.by(act.activation(rel[:, h, :], pb[4 + h][:, 0:384], ACT.Relu, scale=I_DIM ** -0.5))
                for t in range(TT):
                    need(act, kv_ps, L, t + 1)
                    step(act.activation(ak[:, t, :, ROT:HD], pb[1 + t][:, 0:192].rearrange("p (h n) -> p h n", h=4),
                                        ACT.Copy))
                    vsrc = pb[1 + t][:, 192:448].rearrange("p (a b d) -> p b a d", b=2, d=HD)
                    step(act.activation(av[:, t, 0::2, 0:HD], vsrc[:, 0], ACT.Copy))
                    kv_sb.by(act.activation(av[:, t, 1::2, HD:PART], vsrc[:, 1], ACT.Copy))
                for n in range(22, 24):
                    hi(L, n)
                for i in (2, 5, 3, 4, 0, 1, 6, 7):
                    need(act, qk_ps, L, QK.index(i) + 1)
                    src = pb[QK_BANK[QK.index(i)]]
                    if i in (0, 1):
                        m = act.activation(cqT[:, 2 * i:2 * i + 2, :].rearrange("p a b -> p (a b)"), src[:], ACT.Copy)
                    elif i == 2:
                        for kv in range(2):
                            for g in range(2):
                                for par in range(2):
                                    m = act.activation(
                                        kvc[64 * par:64 * par + 64, kv, g, :],
                                        src[64 * g:64 * g + 64, kv * SEQ + par:(kv + 1) * SEQ:2], ACT.Copy)
                                    if (kv, g, par) != (1, 1, 1):
                                        step(m)
                    elif i in (3, 4):
                        m = act.activation(cqrT[:, 2 * (i - 3):2 * (i - 3) + 2, :].rearrange("p a b -> p (a b)"),
                                           src[:], ACT.Copy)
                    elif i == 5:
                        for g in range(2):
                            m = act.activation(kT[:, :, g, :], src[:].rearrange("p (b n) -> p b n", b=2), ACT.Copy,
                                               scale=mhalf[:, g:g + 1])
                            if g == 0:
                                step(m)
                    elif i == 6:
                        m = act.activation(aqT[:].rearrange("p a b -> p (a b)"), src[:], ACT.Copy)
                    else:
                        for g in range(2):
                            m = act.activation(akT[:, g::2, :], src[:].rearrange("p (b n) -> p b n", b=2), ACT.Copy,
                                               scale=mhalf[:, g:g + 1])
                            if g == 0:
                                step(m)
                    qk_sb.by(m)

                def split(first, count):
                    for k in K_ORDER[first:first + count]:
                        m = act.activation(o_sq[:, k, :], out_rows(k), ACT.Square)
                        if k not in (1, 7):
                            step(m)
                        else:
                            osq.by(m)
                    for k in K_ORDER[first:first + count]:
                        h_hi_made.by(act.activation(h_hi[:, k, :], out_rows(k), ACT.Copy, scale=gm[:, k:k + 1]))

                for i in range(UNITS + 2):
                    if i < UNITS:
                        need(act, s_sb, L, i + 1)
                        if i >= 3:
                            need(act, pn_sb, L, i - 2)
                        step(act.activation(ex[:, i % 3, 0:PART], sc[:, i % 2, 0:PART], ACT.Exp, scale=-1.0,
                                            bias=nmx[:, i % 2, 0:1], accum_out=sm[:, i % 3, 0:1]))
                        e_sb.by(act.activation(ex[:, i % 3, PART:384], sc[:, i % 2, PART:384], ACT.Exp, scale=-1.0,
                                               bias=nmx[:, i % 2, 1:2], accum_out=sm[:, i % 3, 1:2]))
                    if i >= 2:
                        need(act, pT_ps, L, i - 1)
                        if i >= 4:
                            need(act, pv_done, L, i - 3)
                        pT_sb.by(act.activation(pT[:, i % 2, :], pb[2 + i % 2][:, 0:384], ACT.Copy))
                    if i == 1:
                        need(act, y_in, L, 1)
                        y_th.by(act.activation(y2, y2, ACT.Tanh, scale=GELU_A))
                    if i == 2:
                        need(act, tanh_in, L, 1)
                        tanh_c.by(act.activation(gt[:, 2, :], gt[:, 1, :], ACT.Tanh, scale=GELU_A))
                    if i == 4:
                        need(act, glu_ps, L, 1)
                        for k in range(2):
                            m = act.activation(y2[:, k * SEQ:(k + 1) * SEQ], pb[7][:, k * SEQ:(k + 1) * SEQ],
                                               ACT.Tanh, scale=0.5, bias=glb[:, k:k + 1])
                            if k == 0:
                                step(m)
                        glu_th.by(m)
                    if i == 8:
                        need(act, cs_max, L, 1)
                        cs_exp.by(act.activation(pc2[:], pc2[:], ACT.Exp))
                    if i == 11:
                        need(act, pcT_ps, L, 1)
                        pcT_sb.by(act.activation(pcT[:], pb[4][:, 0:SEQ], ACT.Copy))
                    if i == 13:
                        need(act, b_made, L, 1)
                        split(0, 2)
                    if i == 15:
                        need(act, c_open, L, 1)
                        split(2, 2)
                    if i == 19:
                        need(act, pv_done, L, 2 * C_HEADS)
                        split(4, 2)
                need(act, pv_done, L, UNITS)
                split(6, 2)
                for i in range(2):
                    need(act, st_ps, L, i + 1)
                    a, b = ((6, 10), (4, 6))[i]
                    sq_sum.by(act.activation(stat[:, a:b], pb[7][:, a:b], ACT.Copy))
                for n in range(24, P_UP0 + 4):
                    hi(L, n)
                h_parts(L, 2, g2)
                sums(L, 10, sq_sum.by)

                def relu(c, par):
                    act.wait_ge(up_ps.sem, up_ps.at(L, 1) + c)
                    for i in range(2):
                        m = act.activation(z_relu[:, i * 512:(i + 1) * 512], pb[2 * par + i][:], ACT.Relu)
                        if i == 0:
                            step(m)
                    relu_sb.by(m)
                    act.wait_ge(zsq_sb.sem, zsq_sb.at(L, 1) + c)
                    zhi_sb.by(act.activation(z_hi[:, par].rearrange("p f t -> p (f t)"), z_sq, ACT.Copy))

                def chunk(c, par, more):
                    for n in range(P_UP0 + 4, P_UP0 + 12):
                        hi(L, n, more=more)
                    relu(c, par)

                for n in range(P_UP0 + 4, P_UP0 + 8):
                    hi(L, n)
                need(act, sq_sum, L, 5)
                relu(0, 0)
                for n in range(P_UP0 + 8, P_UP0 + 12):
                    hi(L, n)
                relu(1, 1)
                before = step.n
                with act.Fori(0, LOOPED) as cc:
                    step.start(L, cc * AS[2])
                    chunk(cc * 2 + 2, 0, cc * 16 + 8)
                    chunk(cc * 2 + 3, 1, cc * 16 + 16)
                    inner = step.n - before
                step.start(L)
                step.n = before + inner * LOOPED
                s5_exp(L + 1)
                chunk(CHUNKS - 2, 0, CHUNKS * 8 - 24)
                chunk(CHUNKS - 1, 1, CHUNKS * 8 - 16)
                for n in range(PIECES - 4, PIECES):
                    hi(L, n)
            assert AS == (n0, step.n, inner), f"ASTEPS = {(n0, step.n, inner)}"
            step.n = 0
            step.start(DEPTH)
            need(act, x_new, DEPTH, 0)
            sums(DEPTH, 0, sq_sum.by)

        @block.vector
        def _(dve):
            step = Steps(dve, v_steps, VS[0])

            def tt(o, a, b, op, wait=True):
                step(dve.tensor_tensor(o, a, b, op), wait)

            def ts(o, a, s1, s2, op0, op1=ALU.bypass, wait=True):
                step(dve.tensor_scalar(o, a, s1, s2, op0, op1) if s2 is not None
                     else dve.tensor_scalar(o, a, s1, None, op0), wait)

            def stt(o, a, s, b, op0, op1):
                return dve.scalar_tensor_tensor(out=o, in0=a, scalar=s, in1=b, op0=op0, op1=op1)

            dve.memset(nmx[:], 0.0).then_inc(lo_made.sem, RING)
            for t, v in ((half_neg, -0.5), (cmask, 0.0), (mask8, 1.0), (mhalf, 1.0), (mquart, 1.0),
                         (cmcol, 1.0), (cadd, 0.0), (cone, 1.0), (inv, 1.0 / 256)):
                m = dve.memset(t[:], v)
            zeros.by(m)
            dve.wait_ge(x_loaded.sem, 32)
            dve.memset(cf[:], 0.0).then_inc(x_new.sem, 3)
            dve.wait_ge(freq_set.sem, 1)
            step(dve.tensor_copy(pos_f[:], pos_i[:]))
            nf = HALF + I_HALF
            tt(ang[:], pos_f[:].unsqueeze(2).to_broadcast([PART, TT, nf]),
               freq[:].unsqueeze(1).to_broadcast([PART, TT, nf]), ALU.mult)
            ts(ang3[:], ang[:], 1.0 / PI2, MAGIC, ALU.mult, ALU.add)
            ts(ang3[:], ang3[:], -MAGIC, None, ALU.add)
            for c in (C1, C2, C3):
                ts(ang2[:], ang3[:], c, None, ALU.mult)
                tt(ang[:], ang[:], ang2[:], ALU.subtract)
            ts(ang[:], ang[:], 3.1415925, -3.1415925, ALU.min, ALU.max)
            ts(ang2[:], ang[:], PI2 / 4, PI2, ALU.is_gt, ALU.mult)
            ts(ang3[:], ang[:], PI2 / 4, None, ALU.add)
            dve.tensor_tensor(ang3[:], ang3[:], ang2[:], ALU.subtract).then_inc(ang_rope.sem, 1)
            for t in (av, vpad, gk, gvr):
                m = dve.memset(t[:], 0.0)
            step(m)
            dve.wait_ge(zeros.sem, 1)
            step(dve.memset(inv[:, 1:2], 1.0 / 512))
            dve.wait_ge(trig_rope.sem, 1)
            for cos_t, sin_t, a, n in ((rc, rs, 0, HALF), (ric, ris, HALF, I_HALF)):
                for d in range(2):
                    step(dve.tensor_copy(cos_t[:, :, d * n:(d + 1) * n], ang[:, :, a:a + n]))
                ts(sin_t[:, :, 0:n], ang2[:, :, a:a + n], -1.0, None, ALU.mult)
                step(dve.tensor_copy(sin_t[:, :, n:2 * n], ang2[:, :, a:a + n]))

            def den(occ):
                need(dve, den_s5, occ, 1)
                rden_s5.by(dve.reciprocal(sp[:, 10, :], sp[:, 7, :]))

            den(0)
            n0 = step.n

            def rope(o, src, heads, cos_t, sin_t, n):
                m = 2 * n
                c4 = cos_t[:].unsqueeze(2).to_broadcast([PART, TT, heads, m])
                s4 = sin_t[:].unsqueeze(2).to_broadcast([PART, TT, heads, m])
                A, B = [dtmp[:, i, 0:TT * heads * m].rearrange("p (t h m) -> p t h m", t=TT, h=heads)
                        for i in range(2)]
                tt(A, src, c4, ALU.mult, False)
                tt(B[:, :, :, 0:n], src[:, :, :, n:m], s4[:, :, :, 0:n], ALU.mult, False)
                tt(B[:, :, :, n:m], src[:, :, :, 0:n], s4[:, :, :, n:m], ALU.mult)
                return A, B

            def heads_of(t, off, n, w):
                return t[:, :, off:off + n * w].rearrange("p t (h w) -> p t h w", w=w)

            with dve.Fori(0, DEPTH) as L:
                step.n = 0
                step.start(L)

                def lo(n, more=0):
                    dve.wait_ge(hi_made.sem, hi_made.at(L, n + 1) + more)
                    lo_made.by(dve.tensor_tensor(w_lo[:, n % RING, 0:width(n)], raw[:, n % RING, 0:width(n)],
                                                 w_hi[:, n % RING, 0:width(n)].bitcast(F32), ALU.subtract))

                def h_rest(base, gains, src_of, order=range(KB), first=0, count=KB):
                    for i in range(first, first + count):
                        k = order[i]
                        need(dve, h_hi_made, L, base + (i | 1) + 1)
                        h_lo_made.by(stt(h_lo[:, k, :], src_of(k), gains[:, k:k + 1],
                                         h_hi[:, k, :].bitcast(F32), ALU.mult, ALU.subtract))

                h_rest(0, g1, lambda k: xT_rows(k, 0))
                for n in range(8):
                    lo(n)

                need(dve, tab_ps, L, 1)
                for i in range(2):
                    for a in range(2):
                        src = pb[0][:, (2 * i + a) * PART:(2 * i + a + 1) * PART].rearrange("p (g s) -> p g s", g=2)
                        m = dve.tensor_tensor(
                            btab[:, i, 4 * a:4 * a + 4, :].rearrange("p j (g s) -> p j g s", g=2),
                            src.unsqueeze(1).to_broadcast([PART, 4, 2, HD]),
                            mask8[:].rearrange("p (j g) -> p j g", g=2).unsqueeze(3).to_broadcast([PART, 4, 2, HD]),
                            ALU.mult)
                        if (i, a) != (1, 1):
                            step(m, False)
                tab_sb.by(m)
                need(dve, tab_ps, L, 2)
                for i in range(2):
                    for a in range(2):
                        src = pb[1][:, (2 * i + a) * PART:(2 * i + a + 1) * PART]
                        m = stt(ctab[:, i, 4 * a:4 * a + 4, :], src.unsqueeze(1).to_broadcast([PART, 4, PART]),
                                1.0 - 2 * i, cmcol[:], ALU.mult, ALU.mult)
                        if (i, a) != (1, 1):
                            step(m, False)
                tab_sb.by(m)
                ts(glb[:], glb[:], 0.5, None, ALU.mult)
                for d in range(2):
                    step(dve.tensor_copy(w2d[:, d * HD:(d + 1) * HD], w2[:, 0, :]))
                for n in range(8, 12):
                    lo(n)

                def s5_round(r):
                    need(dve, bu_ps, L, r + 1)
                    need(dve, prep_e, L, r + 1)
                    ec = et[:, 0, 2 * r:2 * r + 2, :].rearrange("p j t -> p (j t)")
                    es = et[:, 1, 2 * r:2 * r + 2, :].rearrange("p j t -> p (j t)")
                    tt(dtmp[:, 0, :], ec, pb[1][:], ALU.mult, False)
                    tt(dtmp[:, 1, :], es, pb[2][:], ALU.mult, False)
                    tt(dtmp[:, 2, :], ec, pb[2][:], ALU.mult, False)
                    bu_read.by(dve.tensor_tensor(dtmp[:, 3, :], es, pb[1][:], ALU.mult))
                    need(dve, bu_read, L, r + 1)
                    dve.wait_ge(v_steps.sem, step.base + step.n)
                    tt(dtmp[:, 4, :], dtmp[:, 0, :], dtmp[:, 1, :], ALU.add, False)
                    tt(dtmp[:, 5, :], dtmp[:, 2, :], dtmp[:, 3, :], ALU.subtract)
                    if r >= 2:
                        need(dve, h_made, L, r - 1)
                    for j in range(2):
                        mag = sp[:, 1, 2 * r + j:2 * r + j + 1].to_broadcast([PART, SEQ])
                        for i in range(2):
                            m = dve.tensor_tensor_scan(scan[:, r % 2, i, j * SEQ:(j + 1) * SEQ], mag,
                                                       dtmp[:, 4 + i, j * SEQ:(j + 1) * SEQ], 0.0, ALU.mult, ALU.add)
                            if (j, i) != (1, 1):
                                step(m, False)
                    scanned.by(m)
                    need(dve, scanned, L, r + 1)

                s5_round(0)
                need(dve, tile_sb, L, 2)
                step(dve.tensor_copy(iqr[:], proj[:, :, O_IQ:O_IQ + PART]))
                step(dve.tensor_copy(ikr[:], proj[:, :, O_IK:O_IK + I_DIM].unsqueeze(2).to_broadcast(
                    [PART, TT, 4, I_DIM])))
                A, B = rope(None, heads_of(proj, O_IQ, 4, I_DIM)[:, :, :, 0:2 * I_HALF], 4, ric, ris, I_HALF)
                tt(heads_of(iqr, 0, 4, I_DIM)[:, :, :, 0:2 * I_HALF], A, B, ALU.add)
                A, B = rope(None, heads_of(proj, O_IK, 1, I_DIM)[:, :, :, 0:2 * I_HALF], 1, ric, ris, I_HALF)
                roped.by(dve.tensor_tensor(ikr[:, :, :, 0:2 * I_HALF],
                                           A.to_broadcast([PART, TT, 4, 2 * I_HALF]),
                                           B.to_broadcast([PART, TT, 4, 2 * I_HALF]), ALU.add))
                need(dve, roped, L, 1)
                A, B = rope(None, heads_of(proj, O_AQ, 4, HD)[:, :, :, 0:ROT], 4, rc, rs, HALF)
                tt(heads_of(proj, O_AQ, 4, HD)[:, :, :, 0:ROT], A, B, ALU.add)
                A, B = rope(None, heads_of(proj, O_KR, 1, ROT), 1, rc, rs, HALF)
                roped.by(dve.tensor_tensor(ak[:, :, :, 0:ROT], A.to_broadcast([PART, TT, 4, ROT]),
                                           B.to_broadcast([PART, TT, 4, ROT]), ALU.add))
                need(dve, roped, L, 2)
                for n in range(12, 16):
                    lo(n)
                s5_round(1)
                for n in range(16, 20):
                    lo(n)
                s5_round(2)
                need(dve, r_made, L, 2)
                for t in range(TT):
                    m = dve.tensor_scalar(cn[:, t, :], proj[:, t, O_CKV:O_CKV + A_RANK], rkv[:, t:t + 1], None, ALU.mult)
                    if t == 0:
                        step(m, False)
                cn_made.by(m)
                need(dve, tile_sb, L, 5)
                for o in (O_KS, O_KW):
                    v = heads_of(proj, o, 2, HD)[:, :, :, 0:ROT]
                    A, B = rope(None, v, 2, rc, rs, HALF)
                    m = dve.tensor_tensor(v, A, B, ALU.add)
                    if o == O_KS:
                        step(m)
                    else:
                        roped.by(m)
                need(dve, roped, L, 3)
                need(dve, v_sb, L, 1)
                A, B = rope(None, heads_of(proj, O_CQ, 8, HD)[:, :, :, 0:ROT], 8, rc, rs, HALF)
                roped.by(dve.tensor_tensor(heads_of(cqr, 0, 8, HD)[:, :, :, 0:ROT], A, B, ALU.add))
                need(dve, roped, L, 4)
                s5_round(3)
                for n in range(20, 24):
                    lo(n)
                need(dve, gate_in, L, 1)
                gate_sb.by(dve.tensor_scalar(gate[:], gate[:], 0.5, 0.5, ALU.mult, ALU.add))
                need(dve, gate_sb, L, 1)

                ts(cs[:, 3, 0:8].rearrange("p (t h) -> p t h", t=TT), proj[:, :, O_IW:O_IW + 4],
                   I_HEADS ** -0.5, None, ALU.mult)
                for h in range(I_HEADS):
                    need(dve, rel_sb, L, h + 1)
                    for t, (a, b) in enumerate(((0, PART), (PART, 384))):
                        if h == 0:
                            ts(isc[:, a:b], rel[:, 0, a:b], cs[:, 3, 4 * t:4 * t + 1], None, ALU.mult)
                        else:
                            step(stt(isc[:, a:b], rel[:, h, a:b], cs[:, 3, 4 * t + h:4 * t + h + 1], isc[:, a:b],
                                     ALU.mult, ALU.add))
                tt(isc, isc, cmask[:], ALU.add)
                need(dve, qk_sb, L, 1)
                step(dve.memset(cx[:, :, :, :, N_CMP:16], 0.0), False)
                for kv in range(2):
                    for g in range(C_KV):
                        src = kvc[:, kv, g, :].rearrange("p (n q) -> p q n", q=8)
                        for qh in range(2):
                            m = dve.tensor_tensor(
                                cx[:, kv, 8 * qh:8 * qh + 8, g, 0:N_CMP], src[:, :, qh:qh + N_CMP],
                                posT[:, kv, 8 * qh:8 * qh + 8].unsqueeze(2).to_broadcast([PART, 8, N_CMP]), ALU.add)
                            if (kv, g, qh) != (1, 1, 1):
                                step(m, False)
                cx_made.by(m)
                for i in range(TOPK // 8):
                    dve.nop(nofuse=True)
                    for a, b, c in ((0, PART, 0), (PART, 384, 8)):
                        step(dve.max(top8[:, c:c + 8], isc[:, a:b]), False)
                    dve.wait_ge(v_steps.sem, step.base + step.n)
                    dve.nop(nofuse=True)
                    for a, b, c in ((0, PART, 0), (PART, 384, 8)):
                        step(dve.match_replace(isc[:, a:b], top8[:, c:c + 8], isc[:, a:b], -3e38), False)
                    dve.wait_ge(v_steps.sem, step.base + step.n)
                ts(isc, isc, -2e38, NEG, ALU.is_gt, ALU.mult)
                abias_sb.by(dve.tensor_tensor(abias[:], isc, cmask[:], ALU.add))
                need(dve, abias_sb, L, 1)


                def y_open():
                    need(dve, y_ps, L, 1)
                    for k in range(2):
                        step(stt(yT[:, k * SEQ:(k + 1) * SEQ], uT[:, k, :], s5d[:, k:k + 1],
                                 pb[7][:, k * SEQ:(k + 1) * SEQ], ALU.mult, ALU.add), k == 1)
                    tt(yt, yT, yT, ALU.mult)
                    ts(yt, yt, 0.044715, 1.0, ALU.mult, ALU.add)
                    y_in.by(dve.tensor_tensor(y2, yt, yT, ALU.mult))
                    ts(yT, yT, 0.5, None, ALU.mult, wait=False)

                def y_gelu():
                    dve.wait_ge(v_steps.sem, step.base + step.n)
                    need(dve, y_th, L, 1)
                    y_g.by(stt(yg, y2, 1.0, yT, ALU.add, ALU.mult))
                    need(dve, y_g, L, 1)
                    ts(yt, yg, 0.5, None, ALU.mult, wait=False)

                def y_glu():
                    dve.wait_ge(v_steps.sem, step.base + step.n)
                    need(dve, glu_th, L, 1)
                    b_made.by(stt(yg, y2, 1.0, yt, ALU.add, ALU.mult))

                def c_open1():
                    need(dve, c1_ps, L, 1)
                    step(dve.tensor_copy(gt[:, 0, :], pb[4][0:HD, 0:64]))
                    tt(gt[:, 1, :], gt[:, 0, :], gt[:, 0, :], ALU.mult)
                    ts(gt[:, 1, :], gt[:, 1, :], 0.044715, 1.0, ALU.mult, ALU.add)
                    tanh_in.by(dve.tensor_tensor(gt[:, 1, :], gt[:, 1, :], gt[:, 0, :], ALU.mult))
                    ts(gt[:, 0, :], gt[:, 0, :], 0.5, None, ALU.mult, wait=False)

                def c_gelu():
                    dve.wait_ge(v_steps.sem, step.base + step.n)
                    need(dve, tanh_c, L, 1)
                    step(stt(gt[:, 1, :], gt[:, 2, :], 1.0, gt[:, 0, :], ALU.add, ALU.mult))
                    gv = gt[:, 1, 32:64].rearrange("p (g n) -> p g n", g=2)
                    step(dve.tensor_copy(gk[:, 0, :, :], gt[:, 1, 0:32].rearrange("p (g n) -> p g n", g=2)), False)
                    gelu_c.by(dve.tensor_copy(gvr[:].rearrange("p (g h) n -> p g h n", g=2),
                                              gv.unsqueeze(2).to_broadcast([HD, 2, 4, 16])))

                def c_keys():
                    need(dve, c2_ps, L, 1)
                    tt(kbd[:], pb[4][:, 0:32].rearrange("p (g n) -> p g n", g=2),
                       mhalf[:].unsqueeze(2).to_broadcast([PART, 2, 16]), ALU.mult, False)
                    c2_sb.by(dve.tensor_tensor(vbd[:], pb[4][:, HD:2 * HD].unsqueeze(1).to_broadcast([PART, 8, HD]),
                                               mask8[:].unsqueeze(2).to_broadcast([PART, 8, HD]), ALU.mult))

                p2 = pc2[:].rearrange("p t h n -> p (t h) n")

                def c_max():
                    need(dve, cs_ps, L, 1)
                    for t in range(TT):
                        step(stt(pc2[:, t], pb[4][:, t * PART:(t + 1) * PART].rearrange("p (h n) -> p h n", h=8), HD ** -0.5,
                                 cadd[:, t, :].unsqueeze(1).to_broadcast([PART, 8, 16]), ALU.mult, ALU.add), t == 1)
                    step(dve.tensor_reduce(cs[:, 0, :], p2, AX.X, ALU.max))
                    cs_max.by(dve.tensor_tensor(p2, p2, cs[:, 0, :].unsqueeze(2).to_broadcast([PART, 16, 16]), ALU.subtract))

                def c_probs():
                    need(dve, cs_exp, L, 1)
                    step(dve.tensor_reduce(cs[:, 1, :], p2, AX.X, ALU.add))
                    step(dve.reciprocal(cs[:, 2, :], cs[:, 1, :]))
                    for t in range(TT):
                        gv = gate[:, t, 0::3].rearrange("p (g j) -> p j g", g=2)
                        tt(cs[:, 1, 8 * t:8 * t + 8].rearrange("p (j g) -> p j g", g=2),
                           cs[:, 2, 8 * t:8 * t + 8].rearrange("p (j g) -> p j g", g=2), gv, ALU.mult, t == 1)
                    tt(p2, p2, cs[:, 1, :].unsqueeze(2).to_broadcast([PART, 16, 16]), ALU.mult)
                    for t in range(TT):
                        m = dve.tensor_tensor(pc[:, t].rearrange("p (g j) n -> p j g n", g=2),
                                              pc2[:, t].rearrange("p (j g) n -> p j g n", g=2),
                                              cone[:, t, :].unsqueeze(1).unsqueeze(1).to_broadcast([PART, 4, 2, 16]), ALU.mult)
                        if t == 0:
                            step(m, False)
                    pc_made.by(m)

                between = {0: (y_open,), 1: (c_open1,), 2: (y_gelu,), 3: (c_gelu,), 5: (y_glu, c_keys), 7: (c_max,),
                           9: (c_probs,), 14: (lambda: h_rest(8, gm, out_rows, K_ORDER, 0, 2),),
                           16: (lambda: h_rest(8, gm, out_rows, K_ORDER, 2, 2),),
                           UNITS: (lambda: h_rest(8, gm, out_rows, K_ORDER, 4, 2),)}
                for i in range(UNITS + 1):
                    if i < UNITS:
                        kind = units[i][0]
                        mask = cmask if kind == "C" else abias
                        need(dve, s_ps, L, i + 1)
                        if i >= 2:
                            need(dve, e_sb, L, i - 1)
                        dve.nop(nofuse=True)
                        for t, (a, b) in enumerate(((0, PART), (PART, 384))):
                            m = dve.tensor_tensor_reduce(sc[:, i % 2, a:b], pb[i % 2][:, a:b], mask[:, a:b],
                                                         -(HD ** -0.5), 3e38, ALU.add, ALU.min,
                                                         nmx[:, i % 2, t:t + 1])
                            if t == 0:
                                step(m, False)
                        s_sb.by(m)
                    if i >= 1:
                        u = i - 1
                        kind, h, br, _ = units[u]
                        need(dve, e_sb, L, u + 1)
                        step(dve.reciprocal(cf[:, u % 2, :], sm[:, u % 3, :]))
                        if kind == "C":
                            tt(cf[:, u % 2, :], cf[:, u % 2, :], gate[:, :, 3 * h + 1 + br], ALU.mult)
                        if u >= 2:
                            need(dve, pT_ps, L, u - 1)
                        for t, (a, b) in enumerate(((0, PART), (PART, 384))):
                            m = dve.tensor_scalar(pn[:, u % 2, a:b], ex[:, u % 3, a:b], cf[:, u % 2, t:t + 1], None,
                                                  ALU.mult)
                            if t == 0:
                                step(m, False)
                        pn_sb.by(m)
                    for work in between.get(i, ()):
                        work()
                h_rest(8, gm, out_rows, K_ORDER, 6, 2)
                need(dve, r_made, L, 3)
                last = {}
                for s, (half, g, _, banks) in enumerate(OUT):
                    need(dve, o_ps, L, s + 1)
                    if g == 0:
                        need(dve, r_made, L, 4)
                    if half in last:
                        need(dve, x_new, L, 2 * last[half] + 2)
                    for t in range(TT):
                        dst = x[:, t, half * 512:(half + 1) * 512]
                        x_new.by(stt(dst, pb[banks[t]][:], rg[:, 2 * g + t:2 * g + t + 1], dst,
                                     ALU.mult, ALU.add))
                    last[half] = s
                    for n in ((24,), (25, 26), (27,), (28, 29), (30,), (31,))[s]:
                        lo(n)
                h_rest(16, g2, lambda k: xT_rows(k, 2))

                def square(c, par, first=False):
                    if not first:
                        dve.wait_ge(zlo_sb.sem, zlo_sb.at(L, 0) + c)
                    dve.wait_ge(relu_sb.sem, relu_sb.at(L, 1) + c)
                    zsq_sb.by(dve.tensor_tensor(z_sq, z_relu, z_relu, ALU.mult))
                    dve.wait_ge(zhi_sb.sem, zhi_sb.at(L, 1) + c)
                    zlo_sb.by(dve.tensor_tensor(z_lo[:, par].rearrange("p f t -> p (f t)"), z_sq,
                                                z_hi[:, par].rearrange("p f t -> p (f t)").bitcast(F32), ALU.subtract))

                def chunk(c, par, more):
                    for n in range(P_UP0 + 4, P_UP0 + 12):
                        lo(n, more=more)
                    square(c, par)

                for n in range(P_UP0 + 4, P_UP0 + 8):
                    lo(n)
                square(0, 0, True)
                for n in range(P_UP0 + 8, P_UP0 + 12):
                    lo(n)
                square(1, 1)
                with dve.Fori(0, LOOPED) as cc:
                    chunk(cc * 2 + 2, 0, cc * 16 + 8)
                    chunk(cc * 2 + 3, 1, cc * 16 + 16)
                den(L + 1)
                chunk(CHUNKS - 2, 0, CHUNKS * 8 - 24)
                chunk(CHUNKS - 1, 1, CHUNKS * 8 - 16)
                for n in range(PIECES - 4, PIECES):
                    lo(n)
                need(dve, r_made, L, 5)
                tt(r2[:], r2[:], r2[:], ALU.mult)
                need(dve, down_ps, L, 1)
                for half in range(2):
                    for t in range(TT):
                        dst = x[:, t, half * 512:(half + 1) * 512]
                        x_new.by(stt(dst, pb[4 + 2 * t + half][:], r2[:, t:t + 1], dst, ALU.mult, ALU.add))
            assert VS == (n0, step.n), f"VSTEPS = {(n0, step.n)}"
            dve.wait_ge(fg_in.sem, 16)
            need(dve, r_made, DEPTH, 1)
            for t in range(TT):
                stt(x[:, t, :], x[:, t, :], r1[:, t:t + 1], proj[:, 1, 0:D_MODEL], ALU.mult, ALU.mult)\
                    .then_inc(fin_x.sem, 1)

        @block.tensor
        def _(pe):
            pe.nop().then_inc(used.sem, RING)
            pe.wait_ge(ident_made.sem, 1)

            def mm(o, l, r, start, stop):
                return pe.matmul(o, l, r, start=start, stop=stop, skip_group_check=True)

            def mm3(o, lh, ll, rh, rl, start, stop):
                mm(o, lh, rh, start, False)
                mm(o, ll, rh, False, False)
                return mm(o, lh, rl, False, stop)

            with pe.Fori(0, DEPTH) as L:
                def ready(n, more=0):
                    pe.wait_ge(lo_made.sem, lo_made.at(L, n + 1) + more)

                def transpose_x(k_new, stage):
                    for b in range(4):
                        if b % 2 == 0:
                            need(pe, x_new, L, k_new - 2 + b)
                        for k in (2 * b, 2 * b + 1):
                            for t in range(TT):
                                m = pe.transpose(xT_rows(k, stage)[:, t * PART:(t + 1) * PART],
                                                 x[:, t, k * PART:(k + 1) * PART], ident[:])
                        xT_ps.by(m)

                transpose_x(0, 0)

                def tile(i):
                    c0, w = TILES[i]
                    if i >= 2:
                        need(pe, tile_sb, L, i - 1)
                    for q in range(4):
                        n = 4 * i + q
                        ready(n)
                        if i == 0:
                            need(pe, h_lo_made, L, 2 * q + 2)
                        for kk in range(2):
                            k = 2 * q + kk
                            for t in range(TT):
                                o = pb[4 + 2 * (i % 2) + t][:, 0:w]
                                tok = slice(t * PART, (t + 1) * PART)
                                m = mm3(o, h_hi[:, k, tok], h_lo[:, k, tok], w_hi[:, n % RING, kk * w:(kk + 1) * w],
                                        w_lo[:, n % RING, kk * w:(kk + 1) * w],
                                        k == 0, k == KB - 1)
                        used.by(m) if q < 3 else None
                    return m

                def finish(i, m):
                    used.by(m)
                    pe.wait_ge(used.sem, used.at(L, 4 * i + 4))
                    tile_ps.by(pe.nop())

                finish(0, tile(0))
                pe.wait_ge(consts.sem, 1)
                need(pe, prep_b, L, 1)
                for i in range(2):
                    for a in range(2):
                        m = pe.transpose(pb[0][:, (2 * i + a) * PART:(2 * i + a + 1) * PART],
                                         bb[:, i, 4 * a:4 * a + 4].rearrange("p j g h -> p (j g h)"), ident[:])
                tab_ps.by(m)
                pe.wait_ge(params0.sem, 16 * N_OTHER)
                for i in range(2):
                    for a in range(2):
                        m = pe.transpose(pb[1][:, (2 * i + a) * PART:(2 * i + a + 1) * PART],
                                         craw[:, i, a].rearrange("p d s -> p (d s)"), ident[:])
                tab_ps.by(m)
                finish(1, tile(1))
                need(pe, tile_sb, L, 1)
                need(pe, tab_sb, L, 1)
                for k in range(2):
                    for t in range(TT):
                        m = pe.transpose(pb[0][:, k * SEQ + t * PART:k * SEQ + (t + 1) * PART],
                                         proj[:, t, O_U + k * PART:O_U + (k + 1) * PART], ident[:])
                uT_ps.by(m)

                def bu(r):
                    if r == 0:
                        need(pe, tab_sb, L, 2)
                        need(pe, uT_sb, L, 1)
                    else:
                        need(pe, bu_read, L, r)
                    for i in range(2):
                        for jj in range(2):
                            j = 2 * r + jj
                            m = mm(pb[1 + i][:, jj * SEQ:(jj + 1) * SEQ], btab[:, i, j, :], uT[:, j // 4, :],
                                   jj == 0, True)
                    bu_ps.by(m)

                bu(0)
                finish(2, tile(2))
                bu(1)
                finish(3, tile(3))
                bu(2)
                finish(4, tile(4))
                bu(3)
                need(pe, roped, L, 1)
                for t in range(TT):
                    pe.transpose(pb[3][:, t * PART:(t + 1) * PART], iqr[:, t, :], ident[:])
                    m = pe.transpose(pb[3][:, SEQ + t * PART:SEQ + (t + 1) * PART],
                                     ikr[:, t].rearrange("p h d -> p (h d)"), ident[:])
                ix_ps.by(m)
                need(pe, cn_made, L, 1)
                for t in range(TT):
                    m = pe.transpose(pb[0][:, t * PART:(t + 1) * PART], cn[:, t, :], ident[:])
                cT_ps.by(m)
                need(pe, ix_sb, L, 1)
                need(pe, tile_sb, L, 5)
                for h in range(I_HEADS):
                    mm(pb[4 + h][:, 0:PART], iqT[:, 0:PART], ikT[:, h, 0:PART], True, True)
                    is_ps.by(mm(pb[4 + h][:, PART:384], iqT[:, PART:SEQ], ikT[:, h, :], False, True))
                need(pe, cT_sb, L, 1)
                need(pe, bu_read, L, ROUNDS)
                for t in range(TT):
                    kv_ps.by(mm(pb[1 + t][:, 0:448], cT[:, t * PART:(t + 1) * PART], ukv[:], True, True))

                def qk(i, blocks):
                    for b, src in enumerate(blocks):
                        for t in range(TT):
                            m = pe.transpose(pb[QK_BANK[i]][:, b * SEQ + t * PART:b * SEQ + (t + 1) * PART],
                                             src[:, t], ident[:])
                    qk_ps.by(m)

                def cols(t, off):
                    return t[:, :, off:off + PART]

                qk(0, [cols(proj, O_KC), cols(proj, O_VC)])
                need(pe, kv_sb, L, 1)
                need(pe, roped, L, 4)
                qk(1, [cols(proj, O_KS), cols(proj, O_KW)])
                need(pe, kv_sb, L, 2)
                qk(2, [cols(cqr, 0), cols(cqr, PART)])
                qk(3, [cols(cqr, 2 * PART), cols(cqr, 3 * PART)])
                need(pe, rel_sb, L, I_HEADS)
                qk(4, [cols(proj, O_CQ), cols(proj, O_CQ + PART)])
                qk(5, [cols(proj, O_CQ + 2 * PART), cols(proj, O_CQ + 3 * PART)])
                need(pe, qk_sb, L, 5)
                qk(6, [cols(proj, 0), cols(proj, PART)])
                need(pe, qk_sb, L, 6)
                akf = ak[:].rearrange("p t h d -> p t (h d)")
                qk(7, [cols(akf, 0), cols(akf, PART)])
                need(pe, cx_made, L, 1)
                need(pe, qk_sb, L, 7)
                for kv in range(2):
                    for q in range(16):
                        m = mm(pb[4][0:HD, kv * 32:kv * 32 + 32], w1[:, kv, q, :],
                               cx[:, kv, q].rearrange("p g n -> p (g n)"), (kv, q) == (0, 0), q == 15)
                c1_ps.by(m)
                need(pe, h_made, L, ROUNDS)
                need(pe, qk_sb, L, 8)
                for a in range(2):
                    for j in range(4 * a, 4 * a + 4):
                        for i in range(2):
                            m = mm(pb[7][:, a * SEQ:(a + 1) * SEQ], ctab[:, i, j, :], et[:, i, j, :],
                                   (a, j, i) == (0, 0, 0), j % 4 == 3 and i == 1)
                y_ps.by(m)

                def glu():
                    need(pe, y_g, L, 1)
                    for a in range(2):
                        for k in range(2):
                            m = mm(pb[7][:, a * SEQ:(a + 1) * SEQ], glw[:, k, a * PART:(a + 1) * PART],
                                   yg[:, k * SEQ:(k + 1) * SEQ], (a, k) == (0, 0), k == 1)
                    glu_ps.by(m)

                def c_second():
                    need(pe, gelu_c, L, 1)
                    mm(pb[4][:, 0:32], w2d[:], gk[:, 0].rearrange("p g n -> p (g n)"), True, True)
                    c2_ps.by(mm(pb[4][:, HD:2 * HD], gvr[:].rearrange("p h n -> p (h n)"), w2[:, 1, :], False, True))

                def c_scores():
                    need(pe, c2_sb, L, 1)
                    for t in range(TT):
                        for j in range(4):
                            m = mm(pb[4][:, t * PART + 32 * j:t * PART + 32 * j + 32], cqT[:, j, t * PART:(t + 1) * PART],
                                   kbd[:].rearrange("p g n -> p (g n)"), (t, j) == (0, 0), True)
                    cs_ps.by(m)

                def c_transpose():
                    need(pe, pc_made, L, 1)
                    for t in range(TT):
                        m = pe.transpose(pb[4][:, t * PART:(t + 1) * PART], pc[:, t].rearrange("p h n -> p (h n)"),
                                         ident[:])
                    pcT_ps.by(m)

                def c_values():
                    need(pe, pcT_sb, L, 1)
                    for b in range(4):
                        m = mm(pb[5 + b // 2][:, (b % 2) * SEQ:(b % 2 + 1) * SEQ],
                               vbd[:, 2 * b:2 * b + 2, :].rearrange("p h d -> p (h d)"), pcT[:], False, b < 2)
                    c_open.by(m)

                between = {3: glu, 4: c_second, 6: c_scores, 10: c_transpose, 12: c_values}
                for i in range(UNITS + 3):
                    if i < UNITS:
                        kind, h, br, _ = units[i]
                        if i >= 2:
                            need(pe, s_sb, L, i - 1)
                        q, k = (cqrT[:, h % 4, :], kT[:, br, h // 4, :]) if kind == "C" else (aqT[:, h // 2, :], akT[:, h, :])
                        mm(pb[i % 2][:, 0:PART], q[:, 0:PART], k[:, 0:PART], True, True)
                        s_ps.by(mm(pb[i % 2][:, PART:384], q[:, PART:SEQ], k[:, 0:SEQ], False, True))
                    if 2 <= i < UNITS + 2:
                        u = i - 2
                        need(pe, pn_sb, L, u + 1)
                        if u >= 2:
                            need(pe, pT_sb, L, u - 1)
                        for c in range(3):
                            m = pe.transpose(pb[2 + u % 2][:, c * PART:(c + 1) * PART],
                                             pn[:, u % 2, c * PART:(c + 1) * PART], ident[:])
                        pT_ps.by(m)
                    if i >= 3:
                        u = i - 3
                        kind, h, br, b = units[u]
                        need(pe, pT_sb, L, u + 1)
                        if kind == "C":
                            o = pb[5 + b // 2][:, (b % 2) * SEQ:(b % 2 + 1) * SEQ]
                            a = 64 if h % 2 == 0 else 0
                            vs = [vpad[:, t, br, h // 4, a:a + PART] for t in range(TT)]
                        else:
                            o = pb[4][:, b * SEQ:(b + 1) * SEQ]
                            vs = [av[:, t, h, :] for t in range(TT)]
                        mm(o, vs[0], pT[:, u % 2, 0:SEQ], u in (0, C_HEADS, 2 * C_HEADS), False)
                        pv_done.by(mm(o[:, PART:SEQ], vs[1], pT[:, u % 2, SEQ:384], False,
                                      (kind == "A" or b > 1) and h % 2 == 1 and br == (kind == "C")))
                    if i in between:
                        between[i]()

                def sums_of(groups):
                    for g in groups:
                        ks = ((0, 1), (2, 3), (4, 5, 6, 7))[g]
                        for t in range(TT):
                            for k in ks:
                                m = mm(pb[7][:, 4 + 2 * g + t:5 + 2 * g + t], o_sq[:, k, t * PART:(t + 1) * PART],
                                       inv[:, g // 2:g // 2 + 1], (g, t, k) in ((1, 0, 2), (0, 0, 0)), k == ks[-1])
                    st_ps.by(m)

                need(pe, osq, L, 1)
                sums_of((1, 2))
                n = P_IN
                for s, (half, g, qs, banks) in enumerate(OUT):
                    if s >= 3:
                        need(pe, x_new, L, 2 * (s - 2))
                    need(pe, h_lo_made, L, (10, 14, 14, 14, 16, 16)[s])
                    for q in qs:
                        ready(n)
                        for kk in range(2):
                            k = 2 * q + kk
                            for t in range(TT):
                                tok = slice(t * PART, (t + 1) * PART)
                                m = mm3(pb[banks[t]][:], h_hi[:, k, tok], h_lo[:, k, tok],
                                        w_hi[:, n % RING, kk * 512:(kk + 1) * 512],
                                        w_lo[:, n % RING, kk * 512:(kk + 1) * 512],
                                        q == qs[0] and kk == 0, q == qs[-1] and kk == 1)
                        used.by(m)
                        n += 1
                    pe.wait_ge(used.sem, used.at(L, n))
                    o_ps.by(pe.nop())
                    if s == 0:
                        need(pe, osq, L, 2)
                        need(pe, sq_sum, L, 3)
                        sums_of((0,))
                transpose_x(12, 2)

                def up(c, par, n0, more, first=False):
                    for q in range(4):
                        ready(n0 + q, more)
                        if first:
                            need(pe, h_lo_made, L, 16 + 2 * q + 2)
                        for kk in range(2):
                            k = 2 * q + kk
                            for f in range(4):
                                col = slice(kk * 512 + f * PART, kk * 512 + (f + 1) * PART)
                                m = mm3(pb[2 * par + f // 2][:, (f % 2) * SEQ:(f % 2 + 1) * SEQ],
                                        w_hi[:, q, col], w_lo[:, q, col], h_hi[:, k, :], h_lo[:, k, :],
                                        k == 0 and f % 2 == 0, k == KB - 1)
                        used.by(m)
                    pe.wait_ge(used.sem, used.at(L, n0 + 4) + more)
                    up_ps.by(pe.nop())

                def down(c, par, n0, more, first=False, last=False):
                    pe.wait_ge(zlo_sb.sem, zlo_sb.at(L, 1) + c)
                    for f in range(4):
                        ready(n0 + f, more)
                        for t in range(TT):
                            tok = slice(t * PART, (t + 1) * PART)
                            for half in range(2):
                                m = mm3(pb[4 + 2 * t + half][:], z_hi[:, par, f, tok], z_lo[:, par, f, tok],
                                        w_hi[:, f, half * 512:(half + 1) * 512],
                                        w_lo[:, f, half * 512:(half + 1) * 512],
                                        first and f == 0, last and f == 3)
                        used.by(m)

                def chunk(c, par, more, first=False):
                    pe.wait_ge(relu_sb.sem, relu_sb.at(L, 0) + c) if not first else None
                    up(c, par, P_UP0 + 4, more)
                    down(c - 1, 1 - par, P_UP0 + 8, more, first)

                up(0, 0, P_UP0, 0, True)
                chunk(1, 1, 0, True)
                with pe.Fori(0, (CHUNKS - 2) // 2) as cc:
                    chunk(cc * 2 + 2, 0, cc * 16 + 8)
                    chunk(cc * 2 + 3, 1, cc * 16 + 16)
                down(CHUNKS - 1, 1, PIECES - 4, 0, last=True)
                pe.wait_ge(used.sem, used.at(L, PIECES))
                down_ps.by(pe.nop())
                pe.wait_ge(params.sem, (L + 1) * (16 * N_OTHER))


_INS = ["x", "positions", "ln1_g", "w_in", "kv_norm_g", "w_uk", "w_uv", "s5_lambda_re", "s5_lambda_im",
        "s5_log_step", "s5_b_re", "s5_b_im", "s5_c_re", "s5_c_im", "s5_d", "s5_glu_w", "s5_glu_b",
        "cmp_pos_k", "cmp_pos_v", "cmp_k_w1", "cmp_k_w2", "cmp_v_w1", "cmp_v_w2", "gain_a", "gain_b",
        "gain_c", "w_out", "ln2_g", "w_up", "w_down", "final_g"]

VSTEPS = (23, 218)
ASTEPS = (2, 63, 2)
PSTEPS = (144, 152)


def kernel(**inputs):
    import concourse.bacc as bacc
    from concourse.bass_utils import run_bass_kernel_spmd

    nc = bacc.Bacc("TRN2", target_bir_lowering=False, num_devices=1)
    arrays, args = {}, []
    for name in _INS:
        a = np.ascontiguousarray(inputs[name])
        arrays[f"in_{name}"] = a
        args.append(nc.dram_tensor(f"in_{name}", a.shape, mybir.dt.from_np(a.dtype), kind="ExternalInput").ap())
    out = nc.dram_tensor("out", (1, SEQ, D_MODEL), F32, kind="ExternalOutput").ap()
    trunk(nc, *args, out, VSTEPS, ASTEPS, PSTEPS)
    r = run_bass_kernel_spmd(nc, [arrays], core_ids=[0])
    return r.results[0]["out"]
```

```python
from contextlib import ExitStack

import numpy as np

import concourse.bass as bass
from concourse import mybir

F32 = mybir.dt.float32
F32R = mybir.dt.float32r
I32 = mybir.dt.int32
ALU = mybir.AluOpType
ACT = mybir.ActivationFunctionType
AX = mybir.AxisListType

PART = 128
D_MODEL = 1024
SEQ = 256
DEPTH = 2
TT = SEQ // PART
KB = D_MODEL // PART
D_FF = 4 * D_MODEL
EPS = 1e-6
NEG = -1e30

HD = 64
ROT = HD // 4
HALF = ROT // 2
A_HEADS, A_RANK, A_NOPE = 4, 128, HD - ROT
I_HEADS, I_DIM = 4, 32
I_HALF = I_DIM // 8
TOPK = min(256, SEQ // 4)
THETA = 500000.0

S5_W, S5_G, S5_GRP, S5_P = 256, 16, 16, 64
PAIRS = S5_G // 2
ROUNDS = 4
C_HEADS, C_KV, C_GRP = 8, 2, 4
CMP, CSTR = 32, 16
N_CMP = (SEQ - CMP) // CSTR + 1

O_AQ = 0
O_CKV = O_AQ + A_HEADS * HD
O_KR = O_CKV + A_RANK
O_IQ = O_KR + ROT
O_IK = O_IQ + I_HEADS * I_DIM
O_IW = O_IK + I_DIM
O_U = O_IW + I_HEADS
O_CQ = O_U + S5_W
O_KC = O_CQ + C_HEADS * HD
O_VC = O_KC + C_KV * HD
O_KS = O_VC + C_KV * HD
O_VS = O_KS + C_KV * HD
O_KW = O_VS + C_KV * HD
O_VW = O_KW + C_KV * HD
O_GT = O_VW + C_KV * HD
N_IN = O_GT + 3 * C_HEADS

RING = 4
PIECE = 1024
TILES = [(O_CQ - 512, 512), (0, O_CQ - 512), (O_CQ, 512), (O_KC, 512), (O_KC + 512, N_IN - O_KC - 512)]
P_IN = 4 * len(TILES)
P_OUT = 8
CHUNK = 512
CHUNKS = D_FF // CHUNK
LOOPED = (CHUNKS - 4) // 2
PIECES = P_IN + P_OUT + 8 * CHUNKS
P_UP0 = P_IN + P_OUT
assert PIECES % RING == 0 and DEPTH == 2


def width(n):
    return 2 * TILES[n // 4][1] if n < P_IN else PIECE


N_FIRST, N_OTHER = 7, 20
PI2 = 2 * float(np.pi)
C1 = 6.28125
C2 = float(np.float32(0.0019350051879882812))
C3 = PI2 - C1 - C2
MAGIC = 1.5 * 2.0 ** 23
GELU_A = float(np.sqrt(2 / np.pi))


class Signal:

    def __init__(self, sem, per, seed=0):
        self.sem, self.per, self.seed, self.made = sem, per, seed, 0

    def by(self, ins, n=1):
        ins.then_inc(self.sem, n)
        self.made += n
        return ins

    def at(self, layer, k):
        return layer * self.per + (self.seed + k)


class Steps:

    def __init__(self, eng, signal, before=0):
        self.eng, self.s, self.n, self.base, self.before = eng, signal, 0, 0, before

    def start(self, layer, extra=0):
        self.base = layer * self.s.per + self.before + extra

    def __call__(self, ins, wait=True):
        ins.then_inc(self.s.sem, 1)
        self.n += 1
        if wait:
            self.eng.wait_ge(self.s.sem, self.base + self.n)


def trunk(nc, x_in, positions, ln1_g, w_in, kv_norm_g, w_uk, w_uv, s5_lambda_re, s5_lambda_im,
          s5_log_step, s5_b_re, s5_b_im, s5_c_re, s5_c_im, s5_d, s5_glu_w, s5_glu_b, cmp_pos_k,
          cmp_pos_v, cmp_k_w1, cmp_k_w2, cmp_v_w1, cmp_v_w2, gain_a, gain_b, gain_c, w_out, ln2_g,
          w_up, w_down, final_g, out, VS, AS, PS):
    ctx = ExitStack()
    with ctx:
        def sb(name, shape, dt=F32):
            return ctx.enter_context(nc.sbuf_tensor(name, shape, dt))

        def sig(name, per, seed=0):
            return Signal(ctx.enter_context(nc.semaphore(name)), per, seed)

        with ExitStack() as split:
            h_hi, h_lo, z_hi, z_lo = (split.enter_context(nc.sbuf_tensor(name, shape, F32R)) for name, shape in (
                ("h_hi", [PART, KB, SEQ]), ("h_lo", [PART, KB, SEQ]),
                ("z_hi", [PART, 2, 4, SEQ]), ("z_lo", [PART, 2, 4, SEQ])))
        ikT = sb("ikT", [PART, 4, SEQ])
        iqT = sb("iqT", [PART, SEQ])
        cT = sb("cT", [PART, SEQ])
        kvc = sb("kvc", [PART, 2, C_KV, PART])
        cqr = sb("cqr", [PART, TT, C_HEADS * HD])
        cqT = sb("cqT", [PART, 4, SEQ])
        a_zone = sb("a_zone", [PART, 6 * SEQ])
        rel = a_zone[:].rearrange("p (h n) -> p h n", h=4)
        akT = a_zone[:, 0:4 * SEQ].rearrange("p (a t) -> p a t", a=4)
        aqT = a_zone[:, 4 * SEQ:6 * SEQ].rearrange("p (a t) -> p a t", a=2)
        vbd = sb("vbd", [PART, C_HEADS, HD])
        cqrT = sb("cqrT", [PART, 4, SEQ])
        kT = sb("kT", [PART, 2, C_KV, SEQ])
        x = sb("x", [PART, TT, D_MODEL])
        raw = sb("raw", [PART, RING, PIECE])
        w_hi = sb("w_hi", [PART, RING, PIECE], F32R)
        w_lo = sb("w_lo", [PART, RING, PIECE], F32R)
        proj = sb("proj", [PART, TT, N_IN])
        projf = proj[:].rearrange("p t n -> p (t n)")
        z_relu = projf[:, 0:4 * SEQ]
        z_sq = projf[:, 4 * SEQ:8 * SEQ]
        o_sq = projf[:, 0:KB * SEQ].rearrange("p (k t) -> p k t", k=KB)
        ident = sb("ident", [PART, PART])
        inv = sb("inv", [PART, 2])
        cmask = sb("cmask", [PART, 384])
        mask8 = sb("mask8", [PART, 8])
        mhalf = sb("mhalf", [PART, 2])
        mquart = sb("mquart", [PART, 4])
        cmcol = sb("cmcol", [PART, 4, PART])
        cadd = sb("cadd", [PART, TT, 16])
        cone = sb("cone", [PART, TT, 16])
        half_neg = sb("half_neg", [PART, 8])
        pos_i = sb("pos_i", [PART, TT], I32)
        pos_f = sb("pos_f", [PART, TT])
        ang = sb("ang", [PART, TT, HALF + I_HALF])
        ang2 = sb("ang2", [PART, TT, HALF + I_HALF])
        ang3 = sb("ang3", [PART, TT, HALF + I_HALF])
        freq = sb("freq", [PART, HALF + I_HALF])
        rc = sb("rc", [PART, TT, ROT])
        rs = sb("rs", [PART, TT, ROT])
        ric = sb("ric", [PART, TT, 2 * I_HALF])
        ris = sb("ris", [PART, TT, 2 * I_HALF])
        g1 = sb("g1", [PART, KB])
        g2 = sb("g2", [PART, KB])
        gm = sb("gm", [PART, KB])
        kvg = sb("kvg", [PART, 1])
        ukv = sb("ukv", [PART, 448])
        glw = sb("glw", [PART, 2, S5_W])
        glb = sb("glb", [PART, 2])
        s5d = sb("s5d", [PART, 2])
        w1 = sb("w1", [PART, 2, 16, HD])
        w2 = sb("w2", [HD, 2, HD])
        lam = sb("lam", [PART, 3, PAIRS])
        braw = sb("braw", [PART, 2, PAIRS, 16])
        craw = sb("craw", [PART, 2, 2, 2, HD])
        sp = sb("sp", [PART, 24, PAIRS])
        e1 = sb("e1", [PART, 2, PAIRS, 17])
        e2 = sb("e2", [PART, 2, PAIRS, 16])
        bb = sb("bb", [PART, 2, PAIRS, 2, 16])
        bt = sb("bt", [PART, 3, 16 * PAIRS])
        et = sb("et", [PART, 2, PAIRS, SEQ])
        btab = sb("btab", [PART, 2, PAIRS, PART])
        ctab = sb("ctab", [PART, 2, PAIRS, PART])
        r1 = sb("r1", [PART, TT])
        r2 = sb("r2", [PART, TT])
        rkv = sb("rkv", [PART, TT])
        rg = sb("rg", [PART, 6])
        stat = sb("stat", [PART, 16])
        pst = sb("pst", [PART, 20])
        uT = sb("uT", [PART, 2, SEQ])
        ptmp = sb("ptmp", [PART, 2, 512])
        scan = sb("scan", [PART, 2, 2, 512])
        dtmp = sb("dtmp", [PART, 6, 512])
        iqr = sb("iqr", [PART, TT, PART])
        ikr = sb("ikr", [PART, TT, 4, I_DIM])
        cn = sb("cn", [PART, TT, A_RANK])
        ak = sb("ak", [PART, TT, A_HEADS, HD])
        av = sb("av", [PART, TT, A_HEADS, PART])
        vpad = sb("vpad", [PART, TT, 2, C_KV, 192])
        cx = dtmp[:, 0:2, :].rearrange("p v (q g n) -> p v q g n", q=16, g=C_KV)
        posT = sb("posT", [PART, 2, 16])
        gk = sb("gk", [HD, 2, C_KV, 16])
        gt = sb("gt", [HD, 3, 2 * C_KV * 16])
        gvr = sb("gvr", [HD, C_HEADS, 16])
        kbd = sb("kbd", [PART, C_KV, 16])
        w2d = sb("w2d", [HD, PART])
        pc, pc2 = (scan[:, 1, 0, i * SEQ:(i + 1) * SEQ].rearrange("p (t h n) -> p t h n", t=TT, h=C_HEADS)
                   for i in range(2))
        cs = sb("cs", [PART, 4, TT * C_HEADS])
        pcT = scan[:, 1, 1, 0:SEQ]
        gate = sb("gate", [PART, TT, 3 * C_HEADS])
        isc = dtmp[:, 3, 0:384]
        top8 = sb("top8", [PART, 16])
        abias = isc
        tab_zone = btab[:].rearrange("p i j s -> p (i j s)")
        ex = tab_zone[:, 0:3 * 384].rearrange("p (b n) -> p b n", b=3)
        sc = tab_zone[:, 3 * 384:5 * 384].rearrange("p (b n) -> p b n", b=2)
        pT = ptmp[:].rearrange("p b n -> p (b n)")[:, 0:2 * 384].rearrange("p (b n) -> p b n", b=2)
        pn = dtmp[:, 0:3].rearrange("p b n -> p (b n)")[:, 0:3 * 384].rearrange("p (b n) -> p b n", b=3)
        nmx = sb("nmx", [PART, 2, TT])
        sm = sb("sm", [PART, 3, TT])
        cf = sb("cf", [PART, 2, TT])
        yT = dtmp[:, 4, :]
        yg = dtmp[:, 5, :]
        yt = scan[:, 0, 0, :]
        y2 = scan[:, 0, 1, :]
        pb = [ctx.enter_context(nc.psum_tensor(f"pb{i}", [PART, 512], F32)) for i in range(8)]

        x_loaded = sig("x_loaded", 0)
        consts = sig("consts", 0)
        ident_made, freq_set, zeros = sig("ident_made", 0), sig("freq_set", 0), sig("zeros", 0)
        first0, params0 = sig("first0", 0), sig("params0", 0)
        first, params = sig("first", 0), sig("params", 0)
        raw_in = [sig(f"raw_in{i}", 16 * PIECES // RING) for i in range(RING)]
        hi_made = sig("hi_made", PIECES)
        lo_made = sig("lo_made", PIECES, RING)
        used = sig("used", PIECES, RING)
        x_new = sig("x_new", 16, 3)
        xT_ps = sig("xT_ps", 8)
        h_hi_made = sig("h_hi_made", 24)
        h_lo_made = sig("h_lo_made", 24)
        sq_sum = sig("sq_sum", 5)
        r_made = sig("r_made", 5)
        tile_ps = sig("tile_ps", len(TILES))
        tile_sb = sig("tile_sb", len(TILES))
        prep_b = sig("prep_b", 1)
        prep_e = sig("prep_e", ROUNDS)
        step_s5 = sig("step_s5", 1)
        lrs_s5 = sig("lrs_s5", 1)
        mag_s5 = sig("mag_s5", 1)
        ang_rope = sig("ang_rope", 0)
        trig_rope = sig("trig_rope", 0)
        fg_in = sig("fg_in", 0)
        trig_s5 = sig("trig_s5", 1)
        den_s5 = sig("den_s5", 1)
        rden_s5 = sig("rden_s5", 1)
        tab_ps = sig("tab_ps", 2)
        tab_sb = sig("tab_sb", 2)
        uT_ps = sig("uT_ps", 1)
        uT_sb = sig("uT_sb", 1)
        bu_ps = sig("bu_ps", ROUNDS)
        bu_read = sig("bu_read", ROUNDS)
        scanned = sig("scanned", ROUNDS)
        h_made = sig("h_made", ROUNDS)
        roped = sig("roped", 4)
        cn_made = sig("cn_made", 1)
        cT_ps = sig("cT_ps", 1)
        cT_sb = sig("cT_sb", 1)
        ix_ps = sig("ix_ps", 1)
        ix_sb = sig("ix_sb", 1)
        is_ps = sig("is_ps", 4)
        rel_sb = sig("rel_sb", 4)
        kv_ps = sig("kv_ps", 2)
        kv_sb = sig("kv_sb", 2)
        q_copied = sig("q_copied", 1)
        qk_ps = sig("qk_ps", 8)
        qk_sb = sig("qk_sb", 8)
        cx_made = sig("cx_made", 1)
        c1_ps = sig("c1_ps", 1)
        gelu_c = sig("gelu_c", 1)
        tanh_in = sig("tanh_in", 1)
        tanh_c = sig("tanh_c", 1)
        c2_ps = sig("c2_ps", 1)
        c2_sb = sig("c2_sb", 1)
        cs_ps = sig("cs_ps", 1)
        cs_max = sig("cs_max", 1)
        cs_exp = sig("cs_exp", 1)
        pc_made = sig("pc_made", 1)
        pcT_ps = sig("pcT_ps", 1)
        pcT_sb = sig("pcT_sb", 1)
        gate_in = sig("gate_in", 1)
        gate_sb = sig("gate_sb", 1)
        abias_sb = sig("abias_sb", 1)
        UNITS = 2 * C_HEADS + A_HEADS
        s_ps = sig("s_ps", UNITS)
        s_sb = sig("s_sb", UNITS)
        e_sb = sig("e_sb", UNITS)
        cf_sb = sig("cf_sb", UNITS)
        pn_sb = sig("pn_sb", UNITS)
        pT_ps = sig("pT_ps", UNITS)
        pT_sb = sig("pT_sb", UNITS)
        pv_done = sig("pv_done", UNITS)
        y_ps = sig("y_ps", 1)
        y_sum = sig("y_sum", 1)
        y_sq = sig("y_sq", 1)
        y_in = sig("y_in", 1)
        y_th = sig("y_th", 1)
        y_g = sig("y_g", 1)
        glu_ps = sig("glu_ps", 1)
        glu_th = sig("glu_th", 1)
        b_made = sig("b_made", 1)
        osq = sig("osq", 2)
        st_ps = sig("st_ps", 2)
        c_open = sig("c_open", 1)
        o_ps = sig("o_ps", 6)
        up_ps = sig("up_ps", CHUNKS)
        relu_sb = sig("relu_sb", CHUNKS)
        zsq_sb = sig("zsq_sb", CHUNKS)
        zhi_sb = sig("zhi_sb", CHUNKS)
        zlo_sb = sig("zlo_sb", CHUNKS)
        down_ps = sig("down_ps", 2)
        fin_x = sig("fin_x", 0)
        stored = sig("stored", 0)
        v_steps = sig("v_steps", VS[1])
        a_steps = sig("a_steps", AS[1])
        p_steps = sig("p_steps", PS[1])

        def need(eng, s, layer, k):
            eng.wait_ge(s.sem, s.at(layer, k))

        units = []
        for b in range(4):
            for h in (2 * b, 2 * b + 1):
                for br in range(2):
                    units.append(("C", h, br, b))
        for h in range(A_HEADS):
            units.append(("A", h, 0, h // 2))

        def load_params(eng, eng2, lyr, early, late):
            loads = []
            def ld(dst, src):
                queue, s = (eng, early) if len(loads) < N_FIRST else (eng2, late)
                loads.append(queue and queue.dma_start(dst, src).then_inc(s.sem, 16))
            ld(g1[:], ln1_g[lyr].rearrange("(k p) -> p k", p=PART))
            ld(lam[:, 0, :], s5_lambda_re[lyr].rearrange("(j g) p -> (g p) j", g=2))
            ld(lam[:, 1, :], s5_lambda_im[lyr].rearrange("(j g) p -> (g p) j", g=2))
            st = s5_log_step[lyr].rearrange("(o j g) -> o g j", g=2, o=1)
            for g in range(2):
                ld(lam[64 * g:64 * g + 64, 2, :], st[:, g, :].to_broadcast([64, PAIRS]))
            for i, bsrc in enumerate((s5_b_re, s5_b_im)):
                ld(braw[:, i], bsrc[lyr].rearrange("(j g) p h -> (g p) j h", g=2))
            for i, csrc in enumerate((s5_c_re, s5_c_im)):
                for d in range(2):
                    ld(craw[:, i, :, d, :], csrc[lyr].rearrange("(a g) h p -> (g h) a p", a=2))
            ld(g2[:], ln2_g[lyr].rearrange("(k p) -> p k", p=PART))
            ld(gm[:, 0:2], gain_a[lyr].rearrange("(k p) -> p k", p=PART))
            ld(gm[:, 2:4], gain_b[lyr].rearrange("(k p) -> p k", p=PART))
            ld(gm[:, 4:8], gain_c[lyr].rearrange("(k p) -> p k", p=PART))
            ld(kvg[:], kv_norm_g[lyr].rearrange("(k p) -> p k", p=PART))
            ld(ukv[:, 0:192], w_uk[lyr].rearrange("r h n -> r (h n)"))
            ld(ukv[:, 192:448], w_uv[lyr].rearrange("r h n -> r (h n)"))
            ld(glw[:], s5_glu_w[lyr].rearrange("(k p) n -> p k n", p=PART))
            ld(glb[:], s5_glu_b[lyr].rearrange("(k p) -> p k", p=PART))
            ld(s5d[:], s5_d[lyr].rearrange("(k g) h -> (g h) k", k=2))
            for i, (a, b, c) in enumerate(((cmp_k_w1, cmp_k_w2, cmp_pos_k), (cmp_v_w1, cmp_v_w2, cmp_pos_v))):
                ld(w1[:, i], a[lyr].rearrange("(q p) e -> p q e", p=PART))
                ld(w2[:, i], b[lyr])
                ld(posT[:, i, :], c[lyr].rearrange("(q r) d -> (r d) q", r=2))
            assert len(loads) == N_FIRST + N_OTHER

        OUT = [(0, 1, (1,), (0, 1)), (0, 2, (2, 3), (2, 3)), (1, 1, (1,), (5, 6)),
               (1, 2, (2, 3), (0, 1)), (0, 0, (0,), (2, 3)), (1, 0, (0,), (5, 6))]
        K_ORDER = (2, 3, 4, 5, 6, 7, 0, 1)

        def s5_loaded(occ):
            return (first0.sem, 16 * N_FIRST) if isinstance(occ, int) else (first.sem, occ * (16 * N_FIRST))

        def xT_rows(k, stage):
            bank = (0, 1, 2, 3)[k // 2] if stage == 0 else (4, 7, 5, 6)[k // 2]
            return pb[bank][:, (k % 2) * SEQ:(k % 2 + 1) * SEQ]

        def out_rows(k):
            src = {0: pb[4], 1: yg, 2: pb[5], 3: pb[6]}[k // 2]
            return src[:, (k % 2) * SEQ:(k % 2 + 1) * SEQ]

        ctx.enter_context(nc.allow_non_contiguous_dma(reason="vectors of parameters, one element a partition"))
        QK = (2, 5, 3, 4, 0, 1, 6, 7)
        QK_BANK = (0, 0, 6, 7, 4, 5, 4, 7)
        IX_BANK = (6, 7, 4, 5)
        block = ctx.enter_context(nc.Block())

        @block.sync
        def _(sp):
            sp.dma_start(pos_i[:], positions.rearrange("o (t p) -> p (o t)", p=PART)).then_inc(x_loaded.sem, 16)
            sp.dma_start(x[:], x_in.rearrange("o (t p) d -> p (o t) d", p=PART)).then_inc(x_loaded.sem, 16)

            def first_pieces(lyr, before):
                c0, w = TILES[0]
                for q in range(RING):
                    before(q)
                    raw_in[q].by(sp.dma_start(raw[:, q, 0:2 * w].rearrange("p (k n) -> p k n", k=2),
                                              w_in[lyr].rearrange("(k p) n -> p k n", p=PART)
                                              [:, 2 * q:2 * q + 2, c0:c0 + w]), 16)

            sp.wait_ge(first0.sem, 16 * N_FIRST)
            first_pieces(0, lambda q: None)
            load_params(None, sp, 0, first0, params0)
            with sp.Fori(0, DEPTH) as L:
                def piece(n, dst, src, more=0):
                    sp.wait_ge(lo_made.sem, lo_made.at(L, n + 1 - RING) + more)
                    sp.nop(nofuse=True)
                    raw_in[n % RING].by(sp.dma_start(dst, src), 16)

                w_l = w_in[L].rearrange("(k p) n -> p k n", p=PART)
                n = RING
                for c0, w in TILES[1:]:
                    for q in range(4):
                        piece(n, raw[:, n % RING, 0:2 * w].rearrange("p (k n) -> p k n", k=2),
                              w_l[:, 2 * q:2 * q + 2, c0:c0 + w])
                        n += 1
                wo_l = w_out[L].rearrange("(k p) n -> p k n", p=PART)
                for half, _, qs, _ in OUT:
                    for q in qs:
                        piece(n, raw[:, n % RING, :].rearrange("p (k n) -> p k n", k=2),
                              wo_l[:, 2 * q:2 * q + 2, half * 512:half * 512 + 512])
                        n += 1
                up_l = w_up[L].rearrange("(k p) n -> p k n", p=PART)
                down_l = w_down[L].rearrange("(f p) n -> p f n", p=PART)

                def up(c, n, more=0):
                    for q in range(4):
                        piece(n + q, raw[:, q, :].rearrange("p (k n) -> p k n", k=2),
                              up_l[:, 2 * q:2 * q + 2, bass.ds(c * CHUNK, CHUNK)], more)

                def down(c, n, more=0):
                    for q in range(4):
                        piece(n + q, raw[:, q, :],
                              down_l[:, bass.ds(c * 4 + q, 1), :].rearrange("p f n -> p (f n)"), more)

                up(0, n)
                with sp.Fori(1, CHUNKS) as c:
                    up(c, n + 4, (c - 1) * 8)
                    down(c - 1, n + 8, (c - 1) * 8)
                down(CHUNKS - 1, PIECES - 4)

                def split_before(q):
                    sp.wait_ge(lo_made.sem, lo_made.at(L, PIECES + q + 1 - RING))
                    sp.nop(nofuse=True)

                first_pieces(DEPTH - 1, split_before)
            for s in raw_in:
                sp.wait_ge(s.sem, s.at(DEPTH, 16))
            sp.wait_ge(x_new.sem, x_new.at(DEPTH, 0))
            sp.dma_start(proj[:, 1, 0:D_MODEL], final_g.rearrange("(o d) -> o d", o=1).to_broadcast([PART, D_MODEL])).then_inc(fg_in.sem, 16)
            for t in range(TT):
                sp.wait_ge(fin_x.sem, t + 1)
                sp.dma_start(out[0, t * PART:(t + 1) * PART, :], x[:, t, :]).then_inc(stored.sem, 16)
            sp.wait_ge(stored.sem, 16 * TT)

        @block.gpsimd
        def _(pool):
            step = Steps(pool, p_steps, PS[0])
            step(pool.memset(ident[:], 0.0))

            def select(t, pattern, op, fill, base, mul):
                step(pool.affine_select(out=t, in_=t, compare_op=op, fill=fill, base=base,
                                        pattern=pattern, channel_multiplier=mul))
            ident_made.by(pool.affine_select(out=ident[:], in_=ident[:], compare_op=ALU.not_equal, fill=1.0, base=0,
                                             pattern=[[-1, PART]], channel_multiplier=1))
            for i in range(HALF):
                m = pool.memset(freq[:, i:i + 1], float(np.float32(THETA ** (-(2.0 * i) / ROT))))
            for i in range(I_HALF):
                m = pool.memset(freq[:, HALF + i:HALF + i + 1], float(np.float32(THETA ** (-(2.0 * i) / (2 * I_HALF)))))
            freq_set.by(m)
            def tt(o, a, b, op, wait=True):
                step(pool.tensor_tensor(o, a, b, op), wait)

            def ts(o, a, s1, s2, op0, op1=ALU.bypass):
                pool.nop(nofuse=True)
                step(pool.tensor_scalar(o, a, s1, s2, op0, op1) if s2 is not None
                     else pool.tensor_scalar(o, a, s1, None, op0))

            def cmul(oc, os, ac, as_, bc, bs, t, t2):
                tt(oc, ac, bc, ALU.mult, False)
                tt(t, as_, bs, ALU.mult, False)
                tt(os, as_, bc, ALU.mult, False)
                tt(t2, ac, bs, ALU.mult)
                tt(oc, oc, t, ALU.subtract, False)
                return pool.tensor_tensor(os, os, t2, ALU.add)

            def prep(occ):
                pool.wait_ge(*s5_loaded(occ))
                lr, li = lam[:, 0, :], lam[:, 1, :]
                S = lambda i: sp[:, i, :]
                need(pool, step_s5, occ, 1)
                lrs_s5.by(pool.tensor_tensor(S(21), lr, S(0), ALU.mult))
                tt(S(2), li, S(0), ALU.mult)
                ts(S(3), S(2), 1.0 / PI2, MAGIC, ALU.mult, ALU.add)
                ts(S(3), S(3), -MAGIC, None, ALU.add)
                for c in (C1, C2, C3):
                    ts(S(4), S(3), c, None, ALU.mult)
                    tt(S(2), S(2), S(4), ALU.subtract)
                ts(S(2), S(2), 3.1415925, -3.1415925, ALU.min, ALU.max)
                ts(S(4), S(2), PI2 / 4, PI2, ALU.is_gt, ALU.mult)
                ts(S(3), S(2), PI2 / 4, None, ALU.add)
                tt(S(3), S(3), S(4), ALU.subtract)
                tt(S(5), lr, lr, ALU.mult)
                tt(S(6), li, li, ALU.mult)
                den_s5.by(pool.tensor_tensor(S(7), S(5), S(6), ALU.add))
                need(pool, trig_s5, occ, 1)
                need(pool, rden_s5, occ, 1)
                tt(S(11), S(1), S(9), ALU.mult)
                tt(S(12), S(1), S(8), ALU.mult)
                ts(S(11), S(11), -1.0, None, ALU.add)
                tt(S(13), S(11), lr, ALU.mult)
                tt(S(14), S(12), li, ALU.mult)
                tt(S(13), S(13), S(14), ALU.add)
                tt(S(13), S(13), S(10), ALU.mult)
                tt(S(15), S(12), lr, ALU.mult)
                tt(S(14), S(11), li, ALU.mult)
                tt(S(15), S(15), S(14), ALU.subtract)
                tt(S(15), S(15), S(10), ALU.mult)
                zr = S(13).unsqueeze(2).to_broadcast([PART, PAIRS, 16])
                zi = S(15).unsqueeze(2).to_broadcast([PART, PAIRS, 16])
                T = [bt[:, i, :].rearrange("p (j h) -> p j h", j=PAIRS) for i in range(3)]
                for i, op in ((0, ALU.subtract), (1, ALU.add)):
                    tt(T[0], zr, braw[:, i], ALU.mult)
                    tt(T[1], zi, braw[:, 1 - i], ALU.mult)
                    tt(bb[:, i, :, 0, :], T[0], T[1], op)
                    m = pool.tensor_tensor(bb[:, i, :, 1, :], T[0], T[1], op)
                    if i == 0:
                        step(m)
                prep_b.by(m)

            def prep_rest(occ):
                S = lambda i: sp[:, i, :]
                pool.nop(nofuse=True)
                for e in (e1, e2):
                    pool.memset(e[:, 0, :, 0:1], 1.0)
                    pool.memset(e[:, 1, :, 0:1], 0.0)
                pool.tensor_copy(e1[:, 0, :, 1], S(9))
                step(pool.tensor_copy(e1[:, 1, :, 1], S(8)))

                def double(e, n, m):
                    w = [e[:, i, :, n:n + 1].to_broadcast([PART, PAIRS, m]) for i in range(2)]
                    step(cmul(e[:, 0, :, n + 1:n + 1 + m], e[:, 1, :, n + 1:n + 1 + m], e[:, 0, :, 1:1 + m],
                              e[:, 1, :, 1:1 + m], w[0], w[1],
                              *(bt[:, i, 0:PAIRS * m].rearrange("p (j m) -> p j m", m=m) for i in range(2))))
                for n in (1, 2, 4, 8):
                    double(e1, n, n)
                pool.nop(nofuse=True)
                pool.tensor_copy(e2[:, 0, :, 1], e1[:, 0, :, 16])
                step(pool.tensor_copy(e2[:, 1, :, 1], e1[:, 1, :, 16]))
                for n, m in ((1, 1), (2, 2), (4, 4), (8, 7)):
                    double(e2, n, m)
                for r in range(ROUNDS):
                    for j in (2 * r, 2 * r + 1):
                        A = [e2[:, i, j, :].unsqueeze(2).to_broadcast([PART, 16, 16]) for i in range(2)]
                        B = [e1[:, i, j, 0:16].unsqueeze(1).to_broadcast([PART, 16, 16]) for i in range(2)]
                        O = [et[:, i, j, :].rearrange("p (a b) -> p a b", a=16) for i in range(2)]
                        m = cmul(O[0], O[1], A[0], A[1], B[0], B[1],
                                 *(ptmp[:, i, (j % 2) * SEQ:(j % 2 + 1) * SEQ].rearrange("p (a b) -> p a b", a=16)
                                   for i in range(2)))
                        if j == 2 * r:
                            step(m)
                    prep_e.by(m)

            def rstd(L, k, o, ss, n, scale=1.0):
                need(pool, sq_sum, L, k)
                w = o.shape[1]
                mean = pst[:, 4 * (k - 1):4 * (k - 1) + w]
                ts(mean, ss, scale / n, EPS, ALU.mult, ALU.add)
                r_made.by(pool.tensor_tensor(o, mean, half_neg[:, 0:w], ALU.pow))

            def masks():
                pool.wait_ge(zeros.sem, 1)
                for a in (0, 256):
                    select(cmask[:, a:a + PART], [[-1, PART]], ALU.is_ge, NEG, 0, 1)
                select(mask8[:], [[-16, 8]], ALU.is_ge, 0.0, 0, 1)
                select(mask8[:], [[16, 8]], ALU.is_ge, 0.0, 15, -1)
                select(mhalf[:], [[-64, 2]], ALU.is_ge, 0.0, 0, 1)
                select(mhalf[:], [[64, 2]], ALU.is_ge, 0.0, 63, -1)
                select(mquart[:], [[-32, 4]], ALU.is_ge, 0.0, 0, 1)
                select(mquart[:], [[32, 4]], ALU.is_ge, 0.0, 31, -1)
                for g in range(2):
                    v = cmcol[64 * g:64 * g + 64]
                    select(v, [[-32, 4], [1, PART]], ALU.is_ge, 0.0, -16 * g, 0)
                    select(v, [[32, 4], [-1, PART]], ALU.is_ge, 0.0, 16 * g + 15, 0)
                for t, fill in ((cadd, NEG), (cone, 0.0)):
                    select(t[:], [[PART, TT], [-CSTR, 16]], ALU.is_ge, fill, -(CMP - 1), 1)
                step(pool.memset(cadd[:, :, N_CMP:16], NEG))
                consts.by(pool.memset(cone[:, :, N_CMP:16], 0.0))

            masks()
            prep(0)
            rstd(0, 1, r1[:], stat[:, 0:2], D_MODEL)
            prep_rest(0)
            n0 = step.n
            with pool.Fori(0, DEPTH) as L:
                step.n = 0
                step.before = PS[0]
                step.start(L)
                rstd(L, 2, rkv[:], stat[:, 2:4], A_RANK)
                for r in range(ROUNDS):
                    need(pool, scanned, L, r + 1)
                    ec = et[:, 0, 2 * r:2 * r + 2, :].rearrange("p j t -> p (j t)")
                    es = et[:, 1, 2 * r:2 * r + 2, :].rearrange("p j t -> p (j t)")
                    gr, gi = scan[:, r % 2, 0, :], scan[:, r % 2, 1, :]
                    tt(ptmp[:, 0, :], es, gi, ALU.mult)
                    tt(ptmp[:, 1, :], ec, gi, ALU.mult)
                    tt(ec, ec, gr, ALU.mult)
                    tt(es, es, gr, ALU.mult)
                    tt(ec, ec, ptmp[:, 0, :], ALU.subtract)
                    h_made.by(pool.tensor_tensor(es, es, ptmp[:, 1, :], ALU.add))
                def lo_out(n):
                    need(pool, lo_made, L, n)
                    need(pool, hi_made, L, n + 1)
                    lo_made.by(pool.tensor_tensor(w_lo[:, n % RING, :], raw[:, n % RING, :],
                                                  w_hi[:, n % RING, :].bitcast(F32), ALU.subtract))

                need(pool, c1_ps, L, 1)
                for u in range(UNITS):
                    need(pool, cf_sb, L, u + 1)
                    if u >= 3:
                        need(pool, pT_ps, L, u - 2)
                    for t, (a, b) in enumerate(((0, PART), (PART, 384))):
                        m = pool.tensor_tensor(pn[:, u % 3, a:b], ex[:, u % 3, a:b],
                                               cf[:, u % 2, t:t + 1].to_broadcast([PART, b - a]), ALU.mult)
                        if t == 0:
                            step(m, False)
                    pn_sb.by(m)
                    if u in (3, 7, 11, 15):
                        lo_out(20 + u // 4)
                rstd(L, 3, rg[:, 2:6], stat[:, 6:10], 1.0)
                rstd(L, 4, rg[:, 0:2], stat[:, 4:6], 1.0)
                rstd(L, 5, r2[:], stat[:, 10:12], D_MODEL)
                need(pool, h_lo_made, L, 24)
                need(pool, h_hi_made, L, 24)
                pool.nop(nofuse=True)
                load_params(pool, pool, DEPTH - 1, first, params)
                prep(L + 1)
                prep_rest(L + 1)
                rstd(L + 1, 1, r1[:], stat[:, 0:2], D_MODEL)
            assert PS == (n0, step.n), f"PSTEPS = {(n0, step.n)}"

        @block.scalar
        def _(act):
            step = Steps(act, a_steps, AS[0])

            def s5_exp(occ, rope=False):
                act.wait_ge(*s5_loaded(occ))
                step_s5.by(act.activation(sp[:, 0, :], lam[:, 2, :], ACT.Exp))
                need(act, lrs_s5, occ, 1)
                mag_s5.by(act.activation(sp[:, 1, :], sp[:, 21, :], ACT.Exp))
                if rope:
                    act.wait_ge(ang_rope.sem, 1)
                    step(act.activation(ang2[:], ang[:], ACT.Sin))
                    act.activation(ang[:], ang3[:], ACT.Sin).then_inc(trig_rope.sem, 1)
                need(act, den_s5, occ, 1)
                step(act.activation(sp[:, 8, :], sp[:, 2, :], ACT.Sin))
                trig_s5.by(act.activation(sp[:, 9, :], sp[:, 3, :], ACT.Sin))

            def h_parts(L, stage, gains, ks=range(KB)):
                for k in ks:
                    need(act, xT_ps, L, (4 if stage == 2 else 0) + k // 2 + 1)
                    h_hi_made.by(act.activation(h_hi[:, k, :], xT_rows(k, stage),
                                                ACT.Copy, scale=gains[:, k:k + 1]))

            def hi(L, n, more=0):
                act.wait_ge(raw_in[n % RING].sem, raw_in[0].at(L, 16 * (n // RING + 1)) + more * 4)
                act.wait_ge(used.sem, used.at(L, n + 1 - RING) + more)
                hi_made.by(act.activation(w_hi[:, n % RING, 0:width(n)], raw[:, n % RING, 0:width(n)], ACT.Copy))

            def sums(L, c, s):
                for t in range(TT):
                    m = act.activation(projf[:, 0:D_MODEL], x[:, t, :], ACT.Square, accum_out=stat[:, c + t:c + t + 1])
                    if t < TT - 1:
                        step(m)
                s(m)

            load_params(act, None, 0, first0, params0)
            s5_exp(0, True)
            n0 = step.n
            with act.Fori(0, DEPTH) as L:
                step.n = 0
                step.before = AS[0]
                step.start(L)
                for n in range(4):
                    hi(L, n)
                    h_parts(L, 0, g1, (2 * n, 2 * n + 1))
                sums(L, 0, sq_sum.by)
                for n in range(4, 8):
                    hi(L, n)

                def tile_out(i):
                    c0, w = TILES[i]
                    need(act, tile_ps, L, i + 1)
                    for t in range(TT):
                        src = pb[4 + 2 * (i % 2) + t][:, 0:w]
                        dst = proj[:, t, c0:c0 + w]
                        if c0 == O_CQ:
                            src = src.rearrange("p (g j d) -> p g j d", g=2, d=HD)
                            dst = dst.rearrange("p (j g d) -> p g j d", g=2, d=HD)
                        m = act.activation(dst, src, ACT.Copy, scale=r1[:, t:t + 1])
                        if t < TT - 1:
                            step(m, False)
                    tile_sb.by(m)

                need(act, r_made, L, 1)
                tile_out(0)
                for n in range(8, 12):
                    hi(L, n)
                    if n == 9:
                        need(act, uT_ps, L, 1)
                        uT_sb.by(act.activation(uT[:].rearrange("p a b -> p (a b)"), pb[0][:], ACT.Copy))
                tile_out(1)
                need(act, tile_sb, L, 2)
                for t in range(TT):
                    m = act.activation(cn[:, t, :], proj[:, t, O_CKV:O_CKV + A_RANK], ACT.Square,
                                       accum_out=stat[:, 2 + t:3 + t])
                    if t < TT - 1:
                        step(m, False)
                sq_sum.by(m)
                for n in range(12, 16):
                    hi(L, n)
                tile_out(2)
                for n in range(16, 20):
                    hi(L, n)
                tile_out(3)
                tile_out(4)
                need(act, tile_sb, L, 5)
                q_copied.by(act.activation(cqr[:], proj[:, :, O_CQ:O_CQ + 512], ACT.Copy))
                need(act, ix_ps, L, 1)
                step(act.activation(iqT[:], pb[3][:, 0:SEQ], ACT.Copy), False)
                for h in range(I_HEADS):
                    m = act.activation(ikT[:, h, :], pb[3][:, SEQ:2 * SEQ], ACT.Copy, scale=mquart[:, h:h + 1])
                    if h < I_HEADS - 1:
                        step(m, False)
                ix_sb.by(m)

                def transposed(i):
                    need(act, qk_ps, L, i + 1)
                    src, what = pb[QK_BANK[i]], QK[i]
                    if what in (0, 1):
                        m = act.activation(cqT[:, 2 * what:2 * what + 2, :].rearrange("p a b -> p (a b)"), src[:],
                                           ACT.Copy)
                    elif what == 2:
                        for kv in range(2):
                            for g in range(2):
                                for par in range(2):
                                    m = act.activation(
                                        kvc[64 * par:64 * par + 64, kv, g, :],
                                        src[64 * g:64 * g + 64, kv * SEQ + par:(kv + 1) * SEQ:2], ACT.Copy)
                                    if (kv, g, par) != (1, 1, 1):
                                        step(m, False)
                    elif what in (3, 4):
                        m = act.activation(cqrT[:, 2 * (what - 3):2 * (what - 3) + 2, :].rearrange("p a b -> p (a b)"),
                                           src[:], ACT.Copy)
                    elif what == 6:
                        m = act.activation(aqT.rearrange("p a b -> p (a b)"), src[:], ACT.Copy)
                    else:
                        for g in range(2):
                            dst = kT[:, :, g, :] if what == 5 else akT[:, g::2, :]
                            m = act.activation(dst, src[:].rearrange("p (b n) -> p b n", b=2), ACT.Copy,
                                               scale=mhalf[:, g:g + 1])
                            if g == 0:
                                step(m, False)
                    qk_sb.by(m)

                transposed(0)
                gate_in.by(act.activation(gate[:], proj[:, :, O_GT:O_GT + 24], ACT.Tanh, scale=0.5))
                for h in range(I_HEADS):
                    need(act, is_ps, L, h + 1)
                    rel_sb.by(act.activation(rel[:, h, :], pb[IX_BANK[h]][:, 0:384], ACT.Relu, scale=I_DIM ** -0.5))
                need(act, cT_ps, L, 1)
                cT_sb.by(act.activation(cT[:], pb[3][:, 0:SEQ], ACT.Copy, scale=kvg[:]))
                for i in range(1, 4):
                    transposed(i)
                for t in range(TT):
                    need(act, kv_ps, L, t + 1)
                    step(act.activation(ak[:, t, :, ROT:HD], pb[1 + t][:, 0:192].rearrange("p (h n) -> p h n", h=4),
                                        ACT.Copy), False)
                    vsrc = pb[1 + t][:, 192:448].rearrange("p (a b d) -> p b a d", b=2, d=HD)
                    step(act.activation(av[:, t, 0::2, 0:HD], vsrc[:, 0], ACT.Copy), False)
                    kv_sb.by(act.activation(av[:, t, 1::2, HD:PART], vsrc[:, 1], ACT.Copy))
                for i in range(4, 6):
                    transposed(i)
                for br, o in ((0, O_VS), (1, O_VW)):
                    step(act.activation(vpad[:, :, br, :, 64:128],
                                        proj[:, :, o:o + 128].rearrange("p t (g d) -> p t g d", g=2), ACT.Copy), False)

                def split(first, count):
                    for k in K_ORDER[first:first + count]:
                        m = act.activation(o_sq[:, k, :], out_rows(k), ACT.Square)
                        if k not in (1, 7):
                            step(m, False)
                        else:
                            osq.by(m)
                    for k in K_ORDER[first:first + count]:
                        h_hi_made.by(act.activation(h_hi[:, k, :], out_rows(k), ACT.Copy, scale=gm[:, k:k + 1]))

                for i in range(UNITS + 3):
                    if i < UNITS:
                        need(act, s_sb, L, i + 1)
                        if i >= 3:
                            need(act, pn_sb, L, i - 2)
                        step(act.activation(ex[:, i % 3, 0:PART], sc[:, i % 2, 0:PART], ACT.Exp, scale=-1.0,
                                            bias=nmx[:, i % 2, 0:1], accum_out=sm[:, i % 3, 0:1]), False)
                        e_sb.by(act.activation(ex[:, i % 3, PART:384], sc[:, i % 2, PART:384], ACT.Exp, scale=-1.0,
                                               bias=nmx[:, i % 2, 1:2], accum_out=sm[:, i % 3, 1:2]))
                    if i >= 3:
                        u = i - 3
                        need(act, pT_ps, L, u + 1)
                        if u >= 2:
                            need(act, pv_done, L, u - 1)
                        pT_sb.by(act.activation(pT[:, u % 2, :], pb[2 + u % 2][:, 0:384], ACT.Copy))
                    if i in (4, 6):
                        transposed(6 + (i - 4) // 2)
                    if i in (2, 5, 8, 12):
                        hi(L, 20 + (2, 5, 8, 12).index(i))
                    if i == 5:
                        need(act, y_sum, L, 1)
                        y_sq.by(act.activation(yt, yT, ACT.Square, scale=0.044715 ** 0.5))
                    if i == 7:
                        need(act, y_in, L, 1)
                        y_th.by(act.activation(y2, y2, ACT.Tanh, scale=GELU_A))
                    if i == 3:
                        need(act, tanh_in, L, 1)
                        tanh_c.by(act.activation(gt[:, 2, :], gt[:, 1, :], ACT.Tanh, scale=GELU_A))
                    if i == 10:
                        need(act, glu_ps, L, 1)
                        for k in range(2):
                            m = act.activation(y2[:, k * SEQ:(k + 1) * SEQ], pb[7][:, k * SEQ:(k + 1) * SEQ],
                                               ACT.Tanh, scale=0.25, bias=glb[:, k:k + 1])
                            if k == 0:
                                step(m, False)
                        glu_th.by(m)
                    if i == 11:
                        need(act, cs_max, L, 1)
                        cs_exp.by(act.activation(pc2[:], pc2[:], ACT.Exp))
                    if i == 14:
                        need(act, pcT_ps, L, 1)
                        pcT_sb.by(act.activation(pcT[:], pb[4][:, 0:SEQ], ACT.Copy))
                    if i == 15:
                        need(act, b_made, L, 1)
                        split(0, 2)
                    if i == 17:
                        need(act, c_open, L, 1)
                        split(2, 2)
                    if i == 20:
                        need(act, pv_done, L, 2 * C_HEADS)
                        split(4, 2)
                need(act, pv_done, L, UNITS)
                split(6, 2)
                for i in range(2):
                    need(act, st_ps, L, i + 1)
                    a, b = ((6, 10), (4, 6))[i]
                    sq_sum.by(act.activation(stat[:, a:b], pb[7][:, a:b], ACT.Copy))
                for n in range(24, P_UP0 + 4):
                    hi(L, n)
                h_parts(L, 2, g2)
                sums(L, 10, sq_sum.by)

                def relu(c, par):
                    act.wait_ge(up_ps.sem, up_ps.at(L, 1) + c)
                    for i in range(2):
                        m = act.activation(z_relu[:, i * 512:(i + 1) * 512], pb[2 * par + i][:], ACT.Relu)
                        if i == 0:
                            step(m, False)
                    relu_sb.by(m)
                    act.wait_ge(zsq_sb.sem, zsq_sb.at(L, 1) + c)
                    zhi_sb.by(act.activation(z_hi[:, par].rearrange("p f t -> p (f t)"), z_sq, ACT.Copy))

                def chunk(c, par, more):
                    for n in range(P_UP0 + 4, P_UP0 + 12):
                        hi(L, n, more=more)
                    relu(c, par)

                for n in range(P_UP0 + 4, P_UP0 + 8):
                    hi(L, n)
                need(act, sq_sum, L, 5)
                relu(0, 0)
                for n in range(P_UP0 + 8, P_UP0 + 12):
                    hi(L, n)
                relu(1, 1)
                before = step.n
                with act.Fori(0, LOOPED) as cc:
                    step.start(L, cc * AS[2])
                    chunk(cc * 2 + 2, 0, cc * 16 + 8)
                    chunk(cc * 2 + 3, 1, cc * 16 + 16)
                    inner = step.n - before
                step.start(L)
                step.n = before + inner * LOOPED
                s5_exp(L + 1)
                chunk(CHUNKS - 2, 0, CHUNKS * 8 - 24)
                chunk(CHUNKS - 1, 1, CHUNKS * 8 - 16)
                for n in range(PIECES - 4, PIECES):
                    hi(L, n)
            assert AS == (n0, step.n, inner), f"ASTEPS = {(n0, step.n, inner)}"
            step.n = 0
            step.start(DEPTH)
            need(act, x_new, DEPTH, 0)
            sums(DEPTH, 0, sq_sum.by)

        @block.vector
        def _(dve):
            step = Steps(dve, v_steps, VS[0])

            def tt(o, a, b, op, wait=True):
                step(dve.tensor_tensor(o, a, b, op), wait)

            def ts(o, a, s1, s2, op0, op1=ALU.bypass, wait=True):
                step(dve.tensor_scalar(o, a, s1, s2, op0, op1) if s2 is not None
                     else dve.tensor_scalar(o, a, s1, None, op0), wait)

            def stt(o, a, s, b, op0, op1):
                return dve.scalar_tensor_tensor(out=o, in0=a, scalar=s, in1=b, op0=op0, op1=op1)

            dve.memset(nmx[:], 0.0).then_inc(lo_made.sem, RING)
            for t, v in ((half_neg, -0.5), (cmask, 0.0), (mask8, 1.0), (mhalf, 1.0), (mquart, 1.0),
                         (cmcol, 1.0), (cadd, 0.0), (cone, 1.0), (inv, 1.0 / 256)):
                m = dve.memset(t[:], v)
            zeros.by(m)
            dve.wait_ge(x_loaded.sem, 32)
            dve.memset(cf[:], 0.0).then_inc(x_new.sem, 3)
            dve.wait_ge(freq_set.sem, 1)
            step(dve.tensor_copy(pos_f[:], pos_i[:]))
            nf = HALF + I_HALF
            tt(ang[:], pos_f[:].unsqueeze(2).to_broadcast([PART, TT, nf]),
               freq[:].unsqueeze(1).to_broadcast([PART, TT, nf]), ALU.mult)
            ts(ang3[:], ang[:], 1.0 / PI2, MAGIC, ALU.mult, ALU.add)
            ts(ang3[:], ang3[:], -MAGIC, None, ALU.add)
            for c in (C1, C2, C3):
                ts(ang2[:], ang3[:], c, None, ALU.mult)
                tt(ang[:], ang[:], ang2[:], ALU.subtract)
            ts(ang[:], ang[:], 3.1415925, -3.1415925, ALU.min, ALU.max)
            ts(ang2[:], ang[:], PI2 / 4, PI2, ALU.is_gt, ALU.mult)
            ts(ang3[:], ang[:], PI2 / 4, None, ALU.add)
            dve.tensor_tensor(ang3[:], ang3[:], ang2[:], ALU.subtract).then_inc(ang_rope.sem, 1)
            for t in (av, vpad, gk, gvr):
                m = dve.memset(t[:], 0.0)
            step(m)
            dve.wait_ge(zeros.sem, 1)
            step(dve.memset(inv[:, 1:2], 1.0 / 512))
            dve.wait_ge(trig_rope.sem, 1)
            for cos_t, sin_t, a, n in ((rc, rs, 0, HALF), (ric, ris, HALF, I_HALF)):
                for d in range(2):
                    step(dve.tensor_copy(cos_t[:, :, d * n:(d + 1) * n], ang[:, :, a:a + n]))
                ts(sin_t[:, :, 0:n], ang2[:, :, a:a + n], -1.0, None, ALU.mult)
                step(dve.tensor_copy(sin_t[:, :, n:2 * n], ang2[:, :, a:a + n]))

            def den(occ):
                need(dve, den_s5, occ, 1)
                rden_s5.by(dve.reciprocal(sp[:, 10, :], sp[:, 7, :]))

            den(0)
            n0 = step.n

            def rope(o, src, heads, cos_t, sin_t, n):
                m = 2 * n
                c4 = cos_t[:].unsqueeze(2).to_broadcast([PART, TT, heads, m])
                s4 = sin_t[:].unsqueeze(2).to_broadcast([PART, TT, heads, m])
                A, B = [dtmp[:, i, 0:TT * heads * m].rearrange("p (t h m) -> p t h m", t=TT, h=heads)
                        for i in range(2)]
                tt(A, src, c4, ALU.mult, False)
                tt(B[:, :, :, 0:n], src[:, :, :, n:m], s4[:, :, :, 0:n], ALU.mult, False)
                tt(B[:, :, :, n:m], src[:, :, :, 0:n], s4[:, :, :, n:m], ALU.mult)
                return A, B

            def heads_of(t, off, n, w):
                return t[:, :, off:off + n * w].rearrange("p t (h w) -> p t h w", w=w)

            with dve.Fori(0, DEPTH) as L:
                step.n = 0
                step.start(L)

                def lo(n, more=0):
                    dve.wait_ge(hi_made.sem, hi_made.at(L, n + 1) + more)
                    lo_made.by(dve.tensor_tensor(w_lo[:, n % RING, 0:width(n)], raw[:, n % RING, 0:width(n)],
                                                 w_hi[:, n % RING, 0:width(n)].bitcast(F32), ALU.subtract))

                def h_rest(base, gains, src_of, order=range(KB), first=0, count=KB):
                    for i in range(first, first + count):
                        k = order[i]
                        need(dve, h_hi_made, L, base + (i | 1) + 1)
                        h_lo_made.by(stt(h_lo[:, k, :], src_of(k), gains[:, k:k + 1],
                                         h_hi[:, k, :].bitcast(F32), ALU.mult, ALU.subtract))

                for n in range(4):
                    lo(n)
                    h_rest(0, g1, lambda k: xT_rows(k, 0), first=2 * n, count=2)
                for n in range(4, 8):
                    lo(n)

                need(dve, tab_ps, L, 1)
                for i in range(2):
                    for a in range(2):
                        src = pb[0][:, (2 * i + a) * PART:(2 * i + a + 1) * PART].rearrange("p (g s) -> p g s", g=2)
                        m = dve.tensor_tensor(
                            btab[:, i, 4 * a:4 * a + 4, :].rearrange("p j (g s) -> p j g s", g=2),
                            src.unsqueeze(1).to_broadcast([PART, 4, 2, HD]),
                            mask8[:].rearrange("p (j g) -> p j g", g=2).unsqueeze(3).to_broadcast([PART, 4, 2, HD]),
                            ALU.mult)
                        if (i, a) != (1, 1):
                            step(m, False)
                tab_sb.by(m)
                need(dve, tab_ps, L, 2)
                for i in range(2):
                    for a in range(2):
                        src = pb[1][:, (2 * i + a) * PART:(2 * i + a + 1) * PART]
                        m = stt(ctab[:, i, 4 * a:4 * a + 4, :], src.unsqueeze(1).to_broadcast([PART, 4, PART]),
                                1.0 - 2 * i, cmcol[:], ALU.mult, ALU.mult)
                        if (i, a) != (1, 1):
                            step(m, False)
                tab_sb.by(m)
                ts(glb[:], glb[:], 0.5, None, ALU.mult)
                for d in range(2):
                    step(dve.tensor_copy(w2d[:, d * HD:(d + 1) * HD], w2[:, 0, :]))
                for n in range(8, 12):
                    lo(n)

                def s5_round(r):
                    need(dve, bu_ps, L, r + 1)
                    need(dve, prep_e, L, r + 1)
                    ec = et[:, 0, 2 * r:2 * r + 2, :].rearrange("p j t -> p (j t)")
                    es = et[:, 1, 2 * r:2 * r + 2, :].rearrange("p j t -> p (j t)")
                    tt(dtmp[:, 0, :], ec, pb[1][:], ALU.mult, False)
                    tt(dtmp[:, 1, :], es, pb[2][:], ALU.mult, False)
                    tt(dtmp[:, 2, :], ec, pb[2][:], ALU.mult, False)
                    bu_read.by(dve.tensor_tensor(dtmp[:, 3, :], es, pb[1][:], ALU.mult))
                    need(dve, bu_read, L, r + 1)
                    dve.wait_ge(v_steps.sem, step.base + step.n)
                    tt(dtmp[:, 4, :], dtmp[:, 0, :], dtmp[:, 1, :], ALU.add, False)
                    tt(dtmp[:, 5, :], dtmp[:, 2, :], dtmp[:, 3, :], ALU.subtract)
                    if r >= 2:
                        need(dve, h_made, L, r - 1)
                    for j in range(2):
                        mag = sp[:, 1, 2 * r + j:2 * r + j + 1].to_broadcast([PART, SEQ])
                        for i in range(2):
                            m = dve.tensor_tensor_scan(scan[:, r % 2, i, j * SEQ:(j + 1) * SEQ], mag,
                                                       dtmp[:, 4 + i, j * SEQ:(j + 1) * SEQ], 0.0, ALU.mult, ALU.add)
                            if (j, i) != (1, 1):
                                step(m, False)
                    scanned.by(m)
                    need(dve, scanned, L, r + 1)

                s5_round(0)
                need(dve, tile_sb, L, 2)
                step(dve.tensor_copy(iqr[:], proj[:, :, O_IQ:O_IQ + PART]))
                step(dve.tensor_copy(ikr[:], proj[:, :, O_IK:O_IK + I_DIM].unsqueeze(2).to_broadcast(
                    [PART, TT, 4, I_DIM])))
                A, B = rope(None, heads_of(proj, O_IQ, 4, I_DIM)[:, :, :, 0:2 * I_HALF], 4, ric, ris, I_HALF)
                tt(heads_of(iqr, 0, 4, I_DIM)[:, :, :, 0:2 * I_HALF], A, B, ALU.add)
                A, B = rope(None, heads_of(proj, O_IK, 1, I_DIM)[:, :, :, 0:2 * I_HALF], 1, ric, ris, I_HALF)
                roped.by(dve.tensor_tensor(ikr[:, :, :, 0:2 * I_HALF],
                                           A.to_broadcast([PART, TT, 4, 2 * I_HALF]),
                                           B.to_broadcast([PART, TT, 4, 2 * I_HALF]), ALU.add))
                need(dve, roped, L, 1)
                A, B = rope(None, heads_of(proj, O_AQ, 4, HD)[:, :, :, 0:ROT], 4, rc, rs, HALF)
                tt(heads_of(proj, O_AQ, 4, HD)[:, :, :, 0:ROT], A, B, ALU.add)
                A, B = rope(None, heads_of(proj, O_KR, 1, ROT), 1, rc, rs, HALF)
                roped.by(dve.tensor_tensor(ak[:, :, :, 0:ROT], A.to_broadcast([PART, TT, 4, ROT]),
                                           B.to_broadcast([PART, TT, 4, ROT]), ALU.add))
                need(dve, roped, L, 2)
                for n in range(12, 16):
                    lo(n)
                s5_round(1)
                for n in range(16, 20):
                    lo(n)
                s5_round(2)
                need(dve, r_made, L, 2)
                for t in range(TT):
                    m = dve.tensor_scalar(cn[:, t, :], proj[:, t, O_CKV:O_CKV + A_RANK], rkv[:, t:t + 1], None, ALU.mult)
                    if t == 0:
                        step(m, False)
                cn_made.by(m)
                need(dve, tile_sb, L, 5)
                for o in (O_KS, O_KW):
                    v = heads_of(proj, o, 2, HD)[:, :, :, 0:ROT]
                    A, B = rope(None, v, 2, rc, rs, HALF)
                    m = dve.tensor_tensor(v, A, B, ALU.add)
                    if o == O_KS:
                        step(m)
                    else:
                        roped.by(m)
                need(dve, roped, L, 3)
                need(dve, q_copied, L, 1)
                A, B = rope(None, heads_of(proj, O_CQ, 8, HD)[:, :, :, 0:ROT], 8, rc, rs, HALF)
                roped.by(dve.tensor_tensor(heads_of(cqr, 0, 8, HD)[:, :, :, 0:ROT], A, B, ALU.add))
                need(dve, roped, L, 4)
                s5_round(3)

                ts(cs[:, 3, 0:8].rearrange("p (t h) -> p t h", t=TT), proj[:, :, O_IW:O_IW + 4],
                   I_HEADS ** -0.5, None, ALU.mult)
                for h in range(I_HEADS):
                    need(dve, rel_sb, L, h + 1)
                    for t, (a, b) in enumerate(((0, PART), (PART, 384))):
                        if h == 0:
                            ts(isc[:, a:b], rel[:, 0, a:b], cs[:, 3, 4 * t:4 * t + 1], None, ALU.mult, wait=t == 1)
                        else:
                            step(stt(isc[:, a:b], rel[:, h, a:b], cs[:, 3, 4 * t + h:4 * t + h + 1], isc[:, a:b],
                                     ALU.mult, ALU.add), t == 1)
                tt(isc, isc, cmask[:], ALU.add)
                need(dve, qk_sb, L, 1)
                step(dve.memset(cx[:, :, :, :, N_CMP:16], 0.0), False)
                for kv in range(2):
                    for g in range(C_KV):
                        src = kvc[:, kv, g, :].rearrange("p (n q) -> p q n", q=8)
                        for qh in range(2):
                            m = dve.tensor_tensor(
                                cx[:, kv, 8 * qh:8 * qh + 8, g, 0:N_CMP], src[:, :, qh:qh + N_CMP],
                                posT[:, kv, 8 * qh:8 * qh + 8].unsqueeze(2).to_broadcast([PART, 8, N_CMP]), ALU.add)
                            if (kv, g, qh) != (1, 1, 1):
                                step(m, False)
                cx_made.by(m)
                def top8_of_rest():
                    dve.wait_ge(v_steps.sem, step.base + step.n)
                    dve.nop(nofuse=True)
                    for a, b, c in ((0, PART, 0), (PART, 384, 8)):
                        step(dve.max(top8[:, c:c + 8], isc[:, a:b]), False)
                    dve.wait_ge(v_steps.sem, step.base + step.n)
                    dve.nop(nofuse=True)
                    for a, b, c in ((0, PART, 0), (PART, 384, 8)):
                        step(dve.match_replace(isc[:, a:b], top8[:, c:c + 8], isc[:, a:b], -3e38), False)

                def a_mask():
                    dve.wait_ge(v_steps.sem, step.base + step.n)
                    ts(isc, isc, -2e38, NEG, ALU.is_gt, ALU.mult)
                    abias_sb.by(dve.tensor_tensor(abias[:], isc, cmask[:], ALU.add))
                    need(dve, abias_sb, L, 1)

                def y_open():
                    need(dve, y_ps, L, 1)
                    for k in range(2):
                        m = stt(yT[:, k * SEQ:(k + 1) * SEQ], uT[:, k, :], s5d[:, k:k + 1],
                                pb[7][:, k * SEQ:(k + 1) * SEQ], ALU.mult, ALU.add)
                        if k == 0:
                            step(m, False)
                    y_sum.by(m)

                def y_cube():
                    need(dve, y_sum, L, 1)
                    need(dve, y_sq, L, 1)
                    y_in.by(stt(y2, yt, 1.0, yT, ALU.add, ALU.mult))

                def y_gelu():
                    need(dve, y_th, L, 1)
                    y_g.by(stt(yg, y2, 1.0, yT, ALU.add, ALU.mult))
                    need(dve, y_g, L, 1)
                    ts(yt, yg, 0.25, None, ALU.mult, wait=False)

                def y_glu():
                    dve.wait_ge(v_steps.sem, step.base + step.n)
                    need(dve, glu_th, L, 1)
                    b_made.by(stt(yg, y2, 1.0, yt, ALU.add, ALU.mult))

                def c_open1():
                    need(dve, c1_ps, L, 1)
                    step(dve.tensor_copy(gt[:, 0, :], pb[4][0:HD, 0:64]))
                    tt(gt[:, 1, :], gt[:, 0, :], gt[:, 0, :], ALU.mult)
                    ts(gt[:, 1, :], gt[:, 1, :], 0.044715, 1.0, ALU.mult, ALU.add)
                    tanh_in.by(dve.tensor_tensor(gt[:, 1, :], gt[:, 1, :], gt[:, 0, :], ALU.mult))
                    ts(gt[:, 0, :], gt[:, 0, :], 0.5, None, ALU.mult, wait=False)

                def c_gelu():
                    dve.wait_ge(v_steps.sem, step.base + step.n)
                    need(dve, tanh_c, L, 1)
                    step(stt(gt[:, 1, :], gt[:, 2, :], 1.0, gt[:, 0, :], ALU.add, ALU.mult))
                    gv = gt[:, 1, 32:64].rearrange("p (g n) -> p g n", g=2)
                    step(dve.tensor_copy(gk[:, 0, :, :], gt[:, 1, 0:32].rearrange("p (g n) -> p g n", g=2)), False)
                    gelu_c.by(dve.tensor_copy(gvr[:].rearrange("p (g h) n -> p g h n", g=2),
                                              gv.unsqueeze(2).to_broadcast([HD, 2, 4, 16])))

                def c_keys():
                    need(dve, c2_ps, L, 1)
                    tt(kbd[:], pb[4][:, 0:32].rearrange("p (g n) -> p g n", g=2),
                       mhalf[:].unsqueeze(2).to_broadcast([PART, 2, 16]), ALU.mult, False)
                    c2_sb.by(dve.tensor_tensor(vbd[:], pb[4][:, HD:2 * HD].unsqueeze(1).to_broadcast([PART, 8, HD]),
                                               mask8[:].unsqueeze(2).to_broadcast([PART, 8, HD]), ALU.mult))

                p2 = pc2[:].rearrange("p t h n -> p (t h) n")

                def c_max():
                    need(dve, cs_ps, L, 1)
                    for t in range(TT):
                        step(stt(pc2[:, t], pb[4][:, t * PART:(t + 1) * PART].rearrange("p (h n) -> p h n", h=8), HD ** -0.5,
                                 cadd[:, t, :].unsqueeze(1).to_broadcast([PART, 8, 16]), ALU.mult, ALU.add), t == 1)
                    step(dve.tensor_reduce(cs[:, 0, :], p2, AX.X, ALU.max))
                    cs_max.by(dve.tensor_tensor(p2, p2, cs[:, 0, :].unsqueeze(2).to_broadcast([PART, 16, 16]), ALU.subtract))

                def c_probs():
                    need(dve, cs_exp, L, 1)
                    step(dve.tensor_reduce(cs[:, 1, :], p2, AX.X, ALU.add))
                    step(dve.reciprocal(cs[:, 2, :], cs[:, 1, :]))
                    for t in range(TT):
                        gv = gate[:, t, 0::3].rearrange("p (g j) -> p j g", g=2)
                        tt(cs[:, 1, 8 * t:8 * t + 8].rearrange("p (j g) -> p j g", g=2),
                           cs[:, 2, 8 * t:8 * t + 8].rearrange("p (j g) -> p j g", g=2), gv, ALU.mult, t == 1)
                    tt(p2, p2, cs[:, 1, :].unsqueeze(2).to_broadcast([PART, 16, 16]), ALU.mult)
                    for t in range(TT):
                        m = dve.tensor_tensor(pc[:, t].rearrange("p (g j) n -> p j g n", g=2),
                                              pc2[:, t].rearrange("p (j g) n -> p j g n", g=2),
                                              cone[:, t, :].unsqueeze(1).unsqueeze(1).to_broadcast([PART, 4, 2, 16]), ALU.mult)
                        if t == 0:
                            step(m, False)
                    pc_made.by(m)

                need(dve, gate_in, L, 1)
                gate_sb.by(dve.tensor_scalar(gate[:], gate[:], 0.5, 0.5, ALU.mult, ALU.add))
                need(dve, gate_sb, L, 1)
                need(dve, h_made, L, ROUNDS)
                between = {0: (top8_of_rest,), 1: (top8_of_rest,), 2: (c_open1,), 3: (top8_of_rest,),
                           4: (y_open, c_gelu), 5: (top8_of_rest,), 6: (y_cube, top8_of_rest), 7: (c_keys,),
                           8: (y_gelu,), 9: (c_max, top8_of_rest), 10: (top8_of_rest,), 11: (y_glu, top8_of_rest),
                           12: (c_probs,), 13: (a_mask,),
                           16: (lambda: h_rest(8, gm, out_rows, K_ORDER, 0, 2),),
                           18: (lambda: h_rest(8, gm, out_rows, K_ORDER, 2, 2),),
                           UNITS: (lambda: h_rest(8, gm, out_rows, K_ORDER, 4, 2),)}
                assert sum(w.count(top8_of_rest) for w in between.values()) * 8 == TOPK
                for i in range(UNITS + 1):
                    if i < UNITS:
                        kind = units[i][0]
                        mask = cmask if kind == "C" else abias
                        need(dve, s_ps, L, i + 1)
                        if i >= 2:
                            need(dve, e_sb, L, i - 1)
                        dve.nop(nofuse=True)
                        for t, (a, b) in enumerate(((0, PART), (PART, 384))):
                            m = dve.tensor_tensor_reduce(sc[:, i % 2, a:b], pb[i % 2][:, a:b], mask[:, a:b],
                                                         -(HD ** -0.5), 3e38, ALU.add, ALU.min,
                                                         nmx[:, i % 2, t:t + 1])
                            if t == 0:
                                step(m, False)
                        s_sb.by(m)
                    if i >= 1:
                        u = i - 1
                        kind, h, br, _ = units[u]
                        need(dve, e_sb, L, u + 1)
                        if u >= 2:
                            need(dve, pn_sb, L, u - 1)
                        m = dve.reciprocal(cf[:, u % 2, :], sm[:, u % 3, :])
                        if kind == "C":
                            step(m)
                            m = dve.tensor_tensor(cf[:, u % 2, :], cf[:, u % 2, :], gate[:, :, 3 * h + 1 + br], ALU.mult)
                        cf_sb.by(m)
                    for work in between.get(i, ()):
                        work()
                h_rest(8, gm, out_rows, K_ORDER, 6, 2)
                need(dve, r_made, L, 3)
                last = {}
                for s, (half, g, _, banks) in enumerate(OUT):
                    need(dve, o_ps, L, s + 1)
                    if g == 0:
                        need(dve, r_made, L, 4)
                    if half in last:
                        need(dve, x_new, L, 2 * last[half] + 2)
                    for t in range(TT):
                        dst = x[:, t, half * 512:(half + 1) * 512]
                        x_new.by(stt(dst, pb[banks[t]][:], rg[:, 2 * g + t:2 * g + t + 1], dst,
                                     ALU.mult, ALU.add))
                    last[half] = s
                    if s == 0:
                        need(dve, lo_made, L, 24)
                    for n in ((24,), (25, 26), (27,), (28, 29), (30,), (31,))[s]:
                        lo(n)
                h_rest(16, g2, lambda k: xT_rows(k, 2))

                def square(c, par, first=False):
                    if not first:
                        dve.wait_ge(zlo_sb.sem, zlo_sb.at(L, 0) + c)
                    dve.wait_ge(relu_sb.sem, relu_sb.at(L, 1) + c)
                    zsq_sb.by(dve.tensor_tensor(z_sq, z_relu, z_relu, ALU.mult))
                    dve.wait_ge(zhi_sb.sem, zhi_sb.at(L, 1) + c)
                    zlo_sb.by(dve.tensor_tensor(z_lo[:, par].rearrange("p f t -> p (f t)"), z_sq,
                                                z_hi[:, par].rearrange("p f t -> p (f t)").bitcast(F32), ALU.subtract))

                def chunk(c, par, more):
                    for n in range(P_UP0 + 4, P_UP0 + 12):
                        lo(n, more=more)
                    square(c, par)

                for n in range(P_UP0 + 4, P_UP0 + 8):
                    lo(n)
                square(0, 0, True)
                for n in range(P_UP0 + 8, P_UP0 + 12):
                    lo(n)
                square(1, 1)
                with dve.Fori(0, LOOPED) as cc:
                    chunk(cc * 2 + 2, 0, cc * 16 + 8)
                    chunk(cc * 2 + 3, 1, cc * 16 + 16)
                den(L + 1)
                chunk(CHUNKS - 2, 0, CHUNKS * 8 - 24)
                chunk(CHUNKS - 1, 1, CHUNKS * 8 - 16)
                for n in range(PIECES - 4, PIECES):
                    lo(n)
                need(dve, r_made, L, 5)
                tt(r2[:], r2[:], r2[:], ALU.mult)
                for half in range(2):
                    need(dve, down_ps, L, half + 1)
                    for t in range(TT):
                        dst = x[:, t, half * 512:(half + 1) * 512]
                        x_new.by(stt(dst, pb[4 + 2 * t + half][:], r2[:, t:t + 1], dst, ALU.mult, ALU.add))
            assert VS == (n0, step.n), f"VSTEPS = {(n0, step.n)}"
            dve.wait_ge(fg_in.sem, 16)
            need(dve, r_made, DEPTH, 1)
            for t in range(TT):
                stt(x[:, t, :], x[:, t, :], r1[:, t:t + 1], proj[:, 1, 0:D_MODEL], ALU.mult, ALU.mult)\
                    .then_inc(fin_x.sem, 1)

        @block.tensor
        def _(pe):
            pe.nop().then_inc(used.sem, RING)
            pe.wait_ge(ident_made.sem, 1)

            def mm(o, l, r, start, stop):
                return pe.matmul(o, l, r, start=start, stop=stop, skip_group_check=True)

            def mm3(o, lh, ll, rh, rl, start, stop):
                mm(o, lh, rh, start, False)
                mm(o, ll, rh, False, False)
                return mm(o, lh, rl, False, stop)

            with pe.Fori(0, DEPTH) as L:
                def ready(n, more=0):
                    pe.wait_ge(lo_made.sem, lo_made.at(L, n + 1) + more)

                def transpose_x(k_new, stage):
                    for b in range(4):
                        if b % 2 == 0:
                            need(pe, x_new, L, k_new - 2 + b)
                        for k in (2 * b, 2 * b + 1):
                            for t in range(TT):
                                m = pe.transpose(xT_rows(k, stage)[:, t * PART:(t + 1) * PART],
                                                 x[:, t, k * PART:(k + 1) * PART], ident[:])
                        xT_ps.by(m)

                transpose_x(0, 0)

                def tile(i, halfway=None):
                    c0, w = TILES[i]
                    if i >= 2:
                        need(pe, tile_sb, L, i - 1)
                    for q in range(4):
                        n = 4 * i + q
                        ready(n)
                        if i == 0:
                            need(pe, h_lo_made, L, 2 * q + 2)
                        for kk in range(2):
                            k = 2 * q + kk
                            for t in range(TT):
                                o = pb[4 + 2 * (i % 2) + t][:, 0:w]
                                tok = slice(t * PART, (t + 1) * PART)
                                m = mm3(o, h_hi[:, k, tok], h_lo[:, k, tok], w_hi[:, n % RING, kk * w:(kk + 1) * w],
                                        w_lo[:, n % RING, kk * w:(kk + 1) * w],
                                        k == 0, k == KB - 1)
                        if q < 3:
                            used.by(m)
                        if q == 1 and halfway:
                            halfway()
                    return m

                def finish(i, m):
                    used.by(m)
                    pe.wait_ge(used.sem, used.at(L, 4 * i + 4))
                    tile_ps.by(pe.nop())

                finish(0, tile(0))
                pe.wait_ge(consts.sem, 1)
                need(pe, prep_b, L, 1)
                for i in range(2):
                    for a in range(2):
                        m = pe.transpose(pb[0][:, (2 * i + a) * PART:(2 * i + a + 1) * PART],
                                         bb[:, i, 4 * a:4 * a + 4].rearrange("p j g h -> p (j g h)"), ident[:])
                tab_ps.by(m)
                pe.wait_ge(params0.sem, 16 * N_OTHER)
                for i in range(2):
                    for a in range(2):
                        m = pe.transpose(pb[1][:, (2 * i + a) * PART:(2 * i + a + 1) * PART],
                                         craw[:, i, a].rearrange("p d s -> p (d s)"), ident[:])
                tab_ps.by(m)

                def u_transposed():
                    need(pe, tile_sb, L, 1)
                    need(pe, tab_sb, L, 1)
                    for k in range(2):
                        for t in range(TT):
                            m = pe.transpose(pb[0][:, k * SEQ + t * PART:k * SEQ + (t + 1) * PART],
                                             proj[:, t, O_U + k * PART:O_U + (k + 1) * PART], ident[:])
                    uT_ps.by(m)

                finish(1, tile(1, u_transposed))

                def bu(r):
                    if r == 0:
                        need(pe, tab_sb, L, 2)
                        need(pe, uT_sb, L, 1)
                    else:
                        need(pe, bu_read, L, r)
                    for i in range(2):
                        for jj in range(2):
                            j = 2 * r + jj
                            m = mm(pb[1 + i][:, jj * SEQ:(jj + 1) * SEQ], btab[:, i, j, :], uT[:, j // 4, :],
                                   jj == 0, True)
                    bu_ps.by(m)

                bu(0)
                finish(2, tile(2))
                bu(1)
                finish(3, tile(3))
                bu(2)
                finish(4, tile(4))
                bu(3)
                def qk(i, blocks):
                    for b, src in enumerate(blocks):
                        for t in range(TT):
                            m = pe.transpose(pb[QK_BANK[i]][:, b * SEQ + t * PART:b * SEQ + (t + 1) * PART],
                                             src[:, t], ident[:])
                    qk_ps.by(m)

                def cols(t, off):
                    return t[:, :, off:off + PART]

                need(pe, roped, L, 1)
                for t in range(TT):
                    pe.transpose(pb[3][:, t * PART:(t + 1) * PART], iqr[:, t, :], ident[:])
                    m = pe.transpose(pb[3][:, SEQ + t * PART:SEQ + (t + 1) * PART],
                                     ikr[:, t].rearrange("p h d -> p (h d)"), ident[:])
                ix_ps.by(m)
                need(pe, tile_sb, L, 5)
                qk(0, [cols(proj, O_KC), cols(proj, O_VC)])
                need(pe, ix_sb, L, 1)
                for h in range(I_HEADS):
                    mm(pb[IX_BANK[h]][:, 0:PART], iqT[:, 0:PART], ikT[:, h, 0:PART], True, True)
                    is_ps.by(mm(pb[IX_BANK[h]][:, PART:384], iqT[:, PART:SEQ], ikT[:, h, :], False, True))
                need(pe, cn_made, L, 1)
                for t in range(TT):
                    m = pe.transpose(pb[3][:, t * PART:(t + 1) * PART], cn[:, t, :], ident[:])
                cT_ps.by(m)
                need(pe, qk_sb, L, 1)
                need(pe, roped, L, 3)
                qk(1, [cols(proj, O_KS), cols(proj, O_KW)])
                need(pe, roped, L, 4)
                need(pe, rel_sb, L, 2)
                qk(2, [cols(cqr, 0), cols(cqr, PART)])
                qk(3, [cols(cqr, 2 * PART), cols(cqr, 3 * PART)])
                need(pe, cT_sb, L, 1)
                need(pe, bu_read, L, ROUNDS)
                for t in range(TT):
                    kv_ps.by(mm(pb[1 + t][:, 0:448], cT[:, t * PART:(t + 1) * PART], ukv[:], True, True))
                need(pe, rel_sb, L, 4)
                qk(4, [cols(proj, O_CQ), cols(proj, O_CQ + PART)])
                qk(5, [cols(proj, O_CQ + 2 * PART), cols(proj, O_CQ + 3 * PART)])
                need(pe, qk_sb, L, 4)
                need(pe, kv_sb, L, 2)

                def a_queries():
                    need(pe, tanh_in, L, 1)
                    qk(6, [cols(proj, 0), cols(proj, PART)])

                def a_keys():
                    need(pe, y_sum, L, 1)
                    akf = ak[:].rearrange("p t h d -> p t (h d)")
                    qk(7, [cols(akf, 0), cols(akf, PART)])

                def c_first():
                    need(pe, cx_made, L, 1)
                    need(pe, qk_sb, L, 5)
                    for kv in range(2):
                        for q in range(16):
                            m = mm(pb[4][0:HD, kv * 32:kv * 32 + 32], w1[:, kv, q, :],
                                   cx[:, kv, q].rearrange("p g n -> p (g n)"), (kv, q) == (0, 0), q == 15)
                    c1_ps.by(m)

                def s5_out(a):
                    need(pe, h_made, L, ROUNDS)
                    for j in range(4 * a, 4 * a + 4):
                        for i in range(2):
                            m = mm(pb[7][:, a * SEQ:(a + 1) * SEQ], ctab[:, i, j, :], et[:, i, j, :],
                                   (a, j, i) == (0, 0, 0), j % 4 == 3 and i == 1)
                    if a == 1:
                        y_ps.by(m)

                def glu():
                    need(pe, y_g, L, 1)
                    need(pe, qk_sb, L, 8)
                    for a in range(2):
                        for k in range(2):
                            m = mm(pb[7][:, a * SEQ:(a + 1) * SEQ], glw[:, k, a * PART:(a + 1) * PART],
                                   yg[:, k * SEQ:(k + 1) * SEQ], (a, k) == (0, 0), k == 1)
                    glu_ps.by(m)

                def c_second():
                    need(pe, gelu_c, L, 1)
                    need(pe, qk_sb, L, 7)
                    mm(pb[4][:, 0:32], w2d[:], gk[:, 0].rearrange("p g n -> p (g n)"), True, True)
                    c2_ps.by(mm(pb[4][:, HD:2 * HD], gvr[:].rearrange("p h n -> p (h n)"), w2[:, 1, :], False, True))

                def c_scores():
                    need(pe, c2_sb, L, 1)
                    for t in range(TT):
                        for j in range(4):
                            m = mm(pb[4][:, t * PART + 32 * j:t * PART + 32 * j + 32], cqT[:, j, t * PART:(t + 1) * PART],
                                   kbd[:].rearrange("p g n -> p (g n)"), (t, j) == (0, 0), True)
                    cs_ps.by(m)

                def c_transpose():
                    need(pe, pc_made, L, 1)
                    for t in range(TT):
                        m = pe.transpose(pb[4][:, t * PART:(t + 1) * PART], pc[:, t].rearrange("p h n -> p (h n)"),
                                         ident[:])
                    pcT_ps.by(m)

                def c_values():
                    need(pe, pcT_sb, L, 1)
                    for b in range(4):
                        m = mm(pb[5 + b // 2][:, (b % 2) * SEQ:(b % 2 + 1) * SEQ],
                               vbd[:, 2 * b:2 * b + 2, :].rearrange("p h d -> p (h d)"), pcT[:], False, b < 3)
                    c_open.by(m)

                between = {1: (c_first,), 2: (lambda: s5_out(0),), 3: (lambda: s5_out(1),), 4: (a_queries,), 5: (c_second,), 6: (a_keys,), 8: (c_scores,), 9: (glu,), 13: (c_transpose,),
                           15: (c_values,)}
                for i in range(UNITS + 4):
                    if i < UNITS:
                        kind, h, br, _ = units[i]
                        if i >= 2:
                            need(pe, s_sb, L, i - 1)
                        q, k = (cqrT[:, h % 4, :], kT[:, br, h // 4, :]) if kind == "C" else (aqT[:, h // 2, :], akT[:, h, :])
                        mm(pb[i % 2][:, 0:PART], q[:, 0:PART], k[:, 0:PART], True, True)
                        s_ps.by(mm(pb[i % 2][:, PART:384], q[:, PART:SEQ], k[:, 0:SEQ], False, True))
                    if 3 <= i < UNITS + 3:
                        u = i - 3
                        need(pe, pn_sb, L, u + 1)
                        if u >= 2:
                            need(pe, pT_sb, L, u - 1)
                        for c in range(3):
                            m = pe.transpose(pb[2 + u % 2][:, c * PART:(c + 1) * PART],
                                             pn[:, u % 3, c * PART:(c + 1) * PART], ident[:])
                        pT_ps.by(m)
                    if i >= 4:
                        u = i - 4
                        kind, h, br, b = units[u]
                        need(pe, pT_sb, L, u + 1)
                        if kind == "C":
                            o = pb[5 + b // 2][:, (b % 2) * SEQ:(b % 2 + 1) * SEQ]
                            a = 64 if h % 2 == 0 else 0
                            vs = [vpad[:, t, br, h // 4, a:a + PART] for t in range(TT)]
                        else:
                            o = pb[4][:, b * SEQ:(b + 1) * SEQ]
                            vs = [av[:, t, h, :] for t in range(TT)]
                        mm(o, vs[0], pT[:, u % 2, 0:SEQ], u in (0, C_HEADS, 2 * C_HEADS), False)
                        pv_done.by(mm(o[:, PART:SEQ], vs[1], pT[:, u % 2, SEQ:384], False,
                                      (kind == "A" or b > 2) and h % 2 == 1 and br == (kind == "C")))
                    for work in between.get(i, ()):
                        work()

                def sums_of(groups):
                    for g in groups:
                        ks = ((0, 1), (2, 3), (4, 5, 6, 7))[g]
                        for t in range(TT):
                            for k in ks:
                                m = mm(pb[7][:, 4 + 2 * g + t:5 + 2 * g + t], o_sq[:, k, t * PART:(t + 1) * PART],
                                       inv[:, g // 2:g // 2 + 1], (g, t, k) in ((1, 0, 2), (0, 0, 0)), k == ks[-1])
                    st_ps.by(m)

                need(pe, osq, L, 1)
                sums_of((1, 2))
                n = P_IN
                for s, (half, g, qs, banks) in enumerate(OUT):
                    if s >= 3:
                        need(pe, x_new, L, 2 * (s - 2))
                    need(pe, h_lo_made, L, (10, 14, 14, 14, 16, 16)[s])
                    for q in qs:
                        ready(n)
                        for kk in range(2):
                            k = 2 * q + kk
                            for t in range(TT):
                                tok = slice(t * PART, (t + 1) * PART)
                                m = mm3(pb[banks[t]][:], h_hi[:, k, tok], h_lo[:, k, tok],
                                        w_hi[:, n % RING, kk * 512:(kk + 1) * 512],
                                        w_lo[:, n % RING, kk * 512:(kk + 1) * 512],
                                        q == qs[0] and kk == 0, q == qs[-1] and kk == 1)
                        used.by(m)
                        n += 1
                    pe.wait_ge(used.sem, used.at(L, n))
                    o_ps.by(pe.nop())
                    if s == 0:
                        need(pe, osq, L, 2)
                        need(pe, sq_sum, L, 3)
                        sums_of((0,))
                transpose_x(12, 2)

                def up(c, par, n0, more, first=False):
                    for q in range(4):
                        ready(n0 + q, more)
                        if first:
                            need(pe, h_lo_made, L, 16 + 2 * q + 2)
                        for kk in range(2):
                            k = 2 * q + kk
                            for f in range(4):
                                col = slice(kk * 512 + f * PART, kk * 512 + (f + 1) * PART)
                                m = mm3(pb[2 * par + f // 2][:, (f % 2) * SEQ:(f % 2 + 1) * SEQ],
                                        w_hi[:, q, col], w_lo[:, q, col], h_hi[:, k, :], h_lo[:, k, :],
                                        k == 0 and f % 2 == 0, k == KB - 1)
                        used.by(m)
                    pe.wait_ge(used.sem, used.at(L, n0 + 4) + more)
                    up_ps.by(pe.nop())

                def down(c, par, n0, more, first=False):
                    pe.wait_ge(zlo_sb.sem, zlo_sb.at(L, 1) + c)
                    for f in range(4):
                        ready(n0 + f, more)
                        for t in range(TT):
                            tok = slice(t * PART, (t + 1) * PART)
                            for half in range(2):
                                m = mm3(pb[4 + 2 * t + half][:], z_hi[:, par, f, tok], z_lo[:, par, f, tok],
                                        w_hi[:, f, half * 512:(half + 1) * 512],
                                        w_lo[:, f, half * 512:(half + 1) * 512],
                                        first and f == 0, False)
                        used.by(m)

                def chunk(c, par, more, first=False):
                    pe.wait_ge(relu_sb.sem, relu_sb.at(L, 0) + c) if not first else None
                    up(c, par, P_UP0 + 4, more)
                    down(c - 1, 1 - par, P_UP0 + 8, more, first)

                up(0, 0, P_UP0, 0, True)
                chunk(1, 1, 0, True)
                with pe.Fori(0, (CHUNKS - 2) // 2) as cc:
                    chunk(cc * 2 + 2, 0, cc * 16 + 8)
                    chunk(cc * 2 + 3, 1, cc * 16 + 16)
                need(pe, zlo_sb, L, CHUNKS)
                for half in range(2):
                    for f in range(4):
                        if half == 0:
                            ready(PIECES - 4 + f)
                        for t in range(TT):
                            tok = slice(t * PART, (t + 1) * PART)
                            m = mm3(pb[4 + 2 * t + half][:], z_hi[:, 1, f, tok], z_lo[:, 1, f, tok],
                                    w_hi[:, f, half * 512:(half + 1) * 512],
                                    w_lo[:, f, half * 512:(half + 1) * 512], False, f == 3)
                        if half == 1:
                            used.by(m)
                    if half == 0:
                        down_ps.by(m)
                pe.wait_ge(used.sem, used.at(L, PIECES))
                down_ps.by(pe.nop())
                pe.wait_ge(params.sem, (L + 1) * (16 * N_OTHER))


_INS = ["x", "positions", "ln1_g", "w_in", "kv_norm_g", "w_uk", "w_uv", "s5_lambda_re", "s5_lambda_im",
        "s5_log_step", "s5_b_re", "s5_b_im", "s5_c_re", "s5_c_im", "s5_d", "s5_glu_w", "s5_glu_b",
        "cmp_pos_k", "cmp_pos_v", "cmp_k_w1", "cmp_k_w2", "cmp_v_w1", "cmp_v_w2", "gain_a", "gain_b",
        "gain_c", "w_out", "ln2_g", "w_up", "w_down", "final_g"]

VSTEPS = (23, 174)
ASTEPS = (2, 63, 2)
PSTEPS = (144, 172)


def kernel(**inputs):
    import concourse.bacc as bacc
    from concourse.bass_utils import run_bass_kernel_spmd

    nc = bacc.Bacc("TRN2", target_bir_lowering=False, num_devices=1)
    arrays, args = {}, []
    for name in _INS:
        a = np.ascontiguousarray(inputs[name])
        arrays[f"in_{name}"] = a
        args.append(nc.dram_tensor(f"in_{name}", a.shape, mybir.dt.from_np(a.dtype), kind="ExternalInput").ap())
    out = nc.dram_tensor("out", (1, SEQ, D_MODEL), F32, kind="ExternalOutput").ap()
    trunk(nc, *args, out, VSTEPS, ASTEPS, PSTEPS)
    r = run_bass_kernel_spmd(nc, [arrays], core_ids=[0])
    return r.results[0]["out"]
```
